# Optimizing a Trainium2 kernel written in Bass

```python
import math
import jax, jax.numpy as jnp
from jax import lax
import numpy as np

D_MODEL = 1024
BATCH = 1
SEQ = 512
DEPTH = 1

CHUNK = 64
Q_BLOCK = 128
HEAD_DIM = 64
H_DIFF = 4
H_FOX = 6
H_CHUNK = 6
N_PREV_CHUNKS = 8
REL_CLIP = 128
D_FF = 2816
CONV_WIDTH = 3
PLE_DIM = 256
EPS = 1e-6
NEG_INF = -1e30

W_DIFF = H_DIFF * HEAD_DIM
W_FOX = H_FOX * HEAD_DIM
W_CHUNK = H_CHUNK * HEAD_DIM
MIX_WIDTH = W_DIFF + W_FOX + W_CHUNK
IN_SIZES = (W_DIFF,) * 5 + (W_FOX,) * 3 + (H_FOX,) + (W_CHUNK,) * 3
IN_COLS = sum(IN_SIZES)
IN_SPLITS = tuple(int(c) for c in np.cumsum(IN_SIZES)[:-1])
ALIBI_SLOPES = tuple(2.0 ** (-8.0 * (h + 1) / H_DIFF) for h in range(H_DIFF))


def rms_norm(x, g):
    xf = x.astype(jnp.float32)
    y = xf * lax.rsqrt(jnp.mean(xf * xf, axis=-1, keepdims=True) + EPS)
    return (y * g.astype(jnp.float32)).astype(x.dtype)

def split_heads(t, n_heads):
    return t.reshape(t.shape[0], t.shape[1], n_heads, HEAD_DIM)

def query_blocks(q):
    b, s = q.shape[0], q.shape[1]
    q = q.reshape((b, s // Q_BLOCK, Q_BLOCK) + q.shape[2:])
    return jnp.swapaxes(q, 0, 1)

def merge_blocks(o):
    nb, b, qb, h, d = o.shape
    return jnp.swapaxes(o, 0, 1).reshape(b, nb * qb, h * d)

def diff_attention(q1, q2, k1, k2, v, lam, subln_g, lam_init):
    S = k1.shape[1]
    slopes = jnp.asarray(ALIBI_SLOPES, jnp.float32)
    kpos = jnp.arange(S)
    scale = HEAD_DIM ** -0.5

    def block(args):
        q1b, q2b, blk = args
        qpos = blk * Q_BLOCK + jnp.arange(Q_BLOCK)
        dist = jnp.abs(qpos[:, None] - kpos[None, :]).astype(jnp.float32)
        bias = -slopes[:, None, None] * dist
        allowed = (kpos[None, :] // CHUNK) <= (qpos[:, None] // CHUNK)

        def probs(qb, k):
            s = jnp.einsum('bqhd,bkhd->bhqk', qb, k).astype(jnp.float32) * scale + bias
            s = jnp.where(allowed, s, NEG_INF)
            return jax.nn.softmax(s, axis=-1)

        a = probs(q1b, k1) - lam * probs(q2b, k2)
        return jnp.einsum('bhqk,bkhd->bqhd', a.astype(v.dtype), v)

    nb = S // Q_BLOCK
    o = lax.map(block, (query_blocks(q1), query_blocks(q2), jnp.arange(nb)))
    o = rms_norm(o, subln_g) * (1.0 - lam_init)
    return merge_blocks(o)

def forgetting_attention(q, k, v, log_f):
    B, S, H, _ = q.shape
    F = jnp.cumsum(log_f, axis=1)
    F_k = jnp.transpose(F, (0, 2, 1))
    F_q = jnp.transpose(query_blocks(F), (0, 1, 3, 2))
    kpos = jnp.arange(S)
    scale = HEAD_DIM ** -0.5

    def block(args):
        qb, fq, blk = args
        qpos = blk * Q_BLOCK + jnp.arange(Q_BLOCK)
        s = jnp.einsum('bqhd,bkhd->bhqk', qb, k).astype(jnp.float32) * scale
        s = s + fq[..., None] - F_k[:, :, None, :]
        allowed = kpos[None, :] <= qpos[:, None]
        s = jnp.where(allowed, s, NEG_INF)
        pr = jax.nn.softmax(s, axis=-1)
        return jnp.einsum('bhqk,bkhd->bqhd', pr.astype(v.dtype), v)

    nb = S // Q_BLOCK
    o = lax.map(block, (query_blocks(q), F_q, jnp.arange(nb)))
    return merge_blocks(o)

def chunk_band(t):
    b, s, h, d = t.shape
    nc = s // CHUNK
    tc = t.reshape(b, nc, CHUNK, h, d)
    tp = jnp.pad(tc, ((0, 0), (N_PREV_CHUNKS, 0), (0, 0), (0, 0), (0, 0)))
    return jnp.concatenate([tp[:, j:j + nc] for j in range(N_PREV_CHUNKS + 1)], axis=2)

def chunk_attention(q, k, v, rel_table):
    B, S, H, d = q.shape
    nc = S // CHUNK
    band_len = (N_PREV_CHUNKS + 1) * CHUNK
    qc = q.reshape(B, nc, CHUNK, H, d)
    kb = chunk_band(k)
    vb = chunk_band(v)
    qq = np.arange(CHUNK)[:, None]
    kk = np.arange(band_len)[None, :]
    rel = N_PREV_CHUNKS * CHUNK + qq - kk
    idx = np.clip(rel, -REL_CLIP, REL_CLIP) + REL_CLIP
    bias = rel_table[:, idx].astype(jnp.float32)
    key_chunk = (jnp.arange(nc)[:, None] - N_PREV_CHUNKS
                 + (jnp.arange(band_len) // CHUNK)[None, :])
    valid = (key_chunk >= 0)[:, None, None, :]
    s = jnp.einsum('bcqhd,bckhd->bchqk', qc, kb).astype(jnp.float32) * (HEAD_DIM ** -0.5) + bias
    s = jnp.where(valid, s, NEG_INF)
    pr = jax.nn.softmax(s, axis=-1)
    o = jnp.einsum('bchqk,bckhd->bcqhd', pr.astype(v.dtype), vb)
    return o.reshape(B, S, H * d)

def conv_gated_mlp(h, w_up, conv_w, conv_b, w_down):
    u = h @ w_up
    S = u.shape[1]
    up = jnp.pad(u, ((0, 0), (CONV_WIDTH - 1, 0), (0, 0)))
    c = conv_b
    for j in range(CONV_WIDTH):
        c = c + conv_w[j] * up[:, j:j + S]
    gate, val = jnp.split(c, 2, axis=-1)
    return (jax.nn.silu(gate) * val) @ w_down

def first_inputs(seed: int = 0) -> dict:
    key = jax.random.key(seed)
    ks = jax.random.split(key, 20)
    f32 = jnp.float32
    nrm = lambda k, shape, s: jax.random.normal(k, shape, f32) * s
    gain = lambda k, shape: 1.0 + 0.05 * jax.random.normal(k, shape, f32)
    return {
        "x": jax.random.normal(ks[0], (BATCH, SEQ, D_MODEL), f32),
        "p": jax.random.normal(ks[1], (DEPTH, BATCH, SEQ, PLE_DIM), f32),
        "ln_mix": gain(ks[2], (DEPTH, D_MODEL)),
        "w_in": nrm(ks[3], (DEPTH, D_MODEL, IN_COLS), D_MODEL ** -0.5),
        "qk_gain": gain(ks[4], (DEPTH, 6, HEAD_DIM)),
        "lam_params": nrm(ks[5], (DEPTH, 4, HEAD_DIM), 0.1),
        "subln_gain": gain(ks[6], (DEPTH, HEAD_DIM)),
        "fgate_bias": jax.random.uniform(ks[7], (DEPTH, H_FOX), f32, 1.0, 4.0),
        "rel_bias": nrm(ks[8], (DEPTH, H_CHUNK, 2 * REL_CLIP + 1), 0.1),
        "w_out": nrm(ks[9], (DEPTH, MIX_WIDTH, D_MODEL), MIX_WIDTH ** -0.5),
        "ln_ffn": gain(ks[10], (DEPTH, D_MODEL)),
        "w_up": nrm(ks[11], (DEPTH, D_MODEL, 2 * D_FF), D_MODEL ** -0.5),
        "conv_w": nrm(ks[12], (DEPTH, CONV_WIDTH, 2 * D_FF), CONV_WIDTH ** -0.5),
        "conv_b": nrm(ks[13], (DEPTH, 2 * D_FF), 0.02),
        "w_down": nrm(ks[14], (DEPTH, D_FF, D_MODEL), D_FF ** -0.5),
        "ln_ple": gain(ks[15], (DEPTH, D_MODEL)),
        "w_ple_gate": nrm(ks[16], (DEPTH, D_MODEL, D_MODEL), D_MODEL ** -0.5),
        "w_ple_proj": nrm(ks[17], (DEPTH, PLE_DIM, D_MODEL), PLE_DIM ** -0.5),
    }

def first_block(x, p, ln_mix, w_in, qk_gain, lam_params, subln_gain, fgate_bias, rel_bias,
              w_out, ln_ffn, w_up, conv_w, conv_b, w_down, ln_ple, w_ple_gate, w_ple_proj):
    h = x
    for i in range(DEPTH):
        hn = rms_norm(h, ln_mix[i])
        z = hn @ w_in[i]
        (q1, q2, k1, k2, va, qf, kf, vf, fg, qc, kc, vc) = jnp.split(z, IN_SPLITS, axis=-1)
        g = qk_gain[i]
        q1 = rms_norm(split_heads(q1, H_DIFF), g[0])
        q2 = rms_norm(split_heads(q2, H_DIFF), g[0])
        k1 = rms_norm(split_heads(k1, H_DIFF), g[1])
        k2 = rms_norm(split_heads(k2, H_DIFF), g[1])
        va = split_heads(va, H_DIFF)
        lp = lam_params[i].astype(jnp.float32)
        lam_init = 0.8 - 0.6 * math.exp(-0.3 * i)
        lam = jnp.exp(jnp.sum(lp[0] * lp[1])) - jnp.exp(jnp.sum(lp[2] * lp[3])) + lam_init
        o_a = diff_attention(q1, q2, k1, k2, va, lam, subln_gain[i], lam_init)
        qf = rms_norm(split_heads(qf, H_FOX), g[2])
        kf = rms_norm(split_heads(kf, H_FOX), g[3])
        vf = split_heads(vf, H_FOX)
        log_f = jax.nn.log_sigmoid(fg.astype(jnp.float32) + fgate_bias[i].astype(jnp.float32))
        o_b = forgetting_attention(qf, kf, vf, log_f)
        qc = rms_norm(split_heads(qc, H_CHUNK), g[4])
        kc = rms_norm(split_heads(kc, H_CHUNK), g[5])
        vc = split_heads(vc, H_CHUNK)
        o_c = chunk_attention(qc, kc, vc, rel_bias[i])
        h = h + jnp.concatenate([o_a, o_b, o_c], axis=-1) @ w_out[i]
        h = h + conv_gated_mlp(rms_norm(h, ln_ffn[i]), w_up[i], conv_w[i], conv_b[i], w_down[i])
        gate = jax.nn.sigmoid(rms_norm(h, ln_ple[i]) @ w_ple_gate[i])
        h = h + (p[i] @ w_ple_proj[i]) * gate
    return h


SSD_EXPAND = 2
D_SSD = SSD_EXPAND * D_MODEL
SSD_HEADDIM = 64
SSD_HEADS = D_SSD // SSD_HEADDIM
SSD_GROUPS = 8
SSD_STATE = 128
SSD_CONV = 4
SSD_CHUNK = 128
D_XBC = D_SSD + 2 * SSD_GROUPS * SSD_STATE
POOL_WINDOWS = (2, 4, 8, 16)
POOL_GROUPS = len(POOL_WINDOWS)
D_POOL = D_MODEL
POOL_GDIM = D_POOL // POOL_GROUPS
N_BRANCHES = 2
SPLIT_OFFSETS = (D_SSD, D_SSD + D_XBC, D_SSD + D_XBC + SSD_HEADS, D_SSD + D_XBC + SSD_HEADS + D_POOL)
D_IN_PROJ = D_SSD + D_XBC + SSD_HEADS + D_POOL + N_BRANCHES * D_MODEL
N_EXPERTS = 64
TOP_K = 8
N_EXPERT_GROUPS = 8
EXPERTS_PER_GROUP = N_EXPERTS // N_EXPERT_GROUPS
TOPK_GROUPS = 4
D_EXPERT = 256
D_SHARED = 256
ROUTED_SCALE = 2.5
MOE_BLOCK = 128
N_ADA = 6


def rmsnorm(x, g):
    xf = x.astype(jnp.float32)
    inv = lax.rsqrt(jnp.mean(xf * xf, axis=-1, keepdims=True) + EPS)
    return (xf * inv * g.astype(jnp.float32)).astype(x.dtype)

def modulate(x, shift, scale):
    return x * (1 + scale[:, None, :]) + shift[:, None, :]

def causal_dwconv(x, w, b):
    K, C = w.shape
    y = lax.conv_general_dilated(x, w[:, None, :].astype(x.dtype), window_strides=(1,),
                                 padding=[(K - 1, 0)], dimension_numbers=('NWC', 'WIO', 'NWC'),
                                 feature_group_count=C)
    return y + b

def segsum_exp(a):
    Q = a.shape[-1]
    cs = jnp.cumsum(a, axis=-1)
    diff = cs[..., :, None] - cs[..., None, :]
    mask = jnp.tril(jnp.ones((Q, Q), dtype=bool))
    return jnp.where(mask, jnp.exp(jnp.where(mask, diff, 0.0)), 0.0)

def ssd_chunked(xh, dt, A, Bm, Cm):
    Bsz, S, H, P = xh.shape
    G, N = Bm.shape[-2:]
    R = H // G
    Q = SSD_CHUNK
    nc = S // Q
    x = (xh * dt[..., None]).reshape(Bsz, nc, Q, G, R, P)
    a = (dt * A).reshape(Bsz, nc, Q, G, R).transpose(0, 1, 3, 4, 2)
    Bc = Bm.reshape(Bsz, nc, Q, G, N)
    Cc = Cm.reshape(Bsz, nc, Q, G, N)
    a_cs = jnp.cumsum(a, axis=-1)
    L = segsum_exp(a)
    CB = jnp.einsum('bclgn,bcsgn->bcgls', Cc, Bc)
    y_diag = jnp.einsum('bcgls,bcgrls,bcsgrp->bclgrp', CB, L, x)
    decay_states = jnp.exp(a_cs[..., -1:] - a_cs)
    states = jnp.einsum('bclgn,bcgrl,bclgrp->bcgrpn', Bc, decay_states, x)
    chunk_decay = jnp.exp(a_cs[..., -1])

    def step(carry, inp):
        st, dec = inp
        return carry * dec[..., None, None] + st, carry

    init = jnp.zeros(states.shape[:1] + states.shape[2:], states.dtype)
    _, prev = lax.scan(step, init, (jnp.moveaxis(states, 1, 0), jnp.moveaxis(chunk_decay, 1, 0)))
    prev = jnp.moveaxis(prev, 0, 1)
    y_off = jnp.einsum('bclgn,bcgrpn,bcgrl->bclgrp', Cc, prev, jnp.exp(a_cs))
    return (y_diag + y_off).reshape(Bsz, S, H, P)

def ssd_branch(z, xbc, dt_raw, conv_w, conv_b, dt_bias, A_log, D_skip, norm_g):
    xbc = jax.nn.silu(causal_dwconv(xbc, conv_w, conv_b))
    Bsz, S, _ = xbc.shape
    GN = SSD_GROUPS * SSD_STATE
    xs = xbc[..., :D_SSD].reshape(Bsz, S, SSD_HEADS, SSD_HEADDIM)
    Bm = xbc[..., D_SSD:D_SSD + GN].reshape(Bsz, S, SSD_GROUPS, SSD_STATE)
    Cm = xbc[..., D_SSD + GN:].reshape(Bsz, S, SSD_GROUPS, SSD_STATE)
    dt = jax.nn.softplus((dt_raw + dt_bias).astype(jnp.float32))
    A = -jnp.exp(A_log.astype(jnp.float32))
    y = ssd_chunked(xs, dt, A, Bm, Cm) + D_skip[:, None] * xs
    y = y.reshape(Bsz, S, D_SSD) * jax.nn.silu(z)
    y = rmsnorm(y.reshape(Bsz, S, SSD_GROUPS, D_SSD // SSD_GROUPS), norm_g.reshape(SSD_GROUPS, -1))
    return y.reshape(Bsz, S, D_SSD)

def pool_branch(xp, pool_w, pool_scale):
    Bsz, S, _ = xp.shape
    xg = xp.reshape(Bsz, S, POOL_GROUPS, POOL_GDIM).astype(jnp.float32)
    csp = jnp.pad(jnp.cumsum(xg, axis=1), ((0, 0), (1, 0), (0, 0), (0, 0)))
    pos = jnp.arange(1, S + 1, dtype=jnp.float32)
    outs = []
    for gi, w in enumerate(POOL_WINDOWS):
        c_g = csp[:, :, gi]
        lower = jnp.concatenate([jnp.zeros((Bsz, w - 1, POOL_GDIM), c_g.dtype), c_g[:, :S + 1 - w]], axis=1)
        mean = (c_g[:, 1:] - lower) / jnp.minimum(pos, w)[None, :, None]
        outs.append(mean - xg[:, :, gi])
    pooled = jnp.stack(outs, axis=2).astype(xp.dtype)
    mixed = jnp.einsum('bsgc,gcd->bsgd', pooled, pool_w)
    return mixed.reshape(Bsz, S, D_POOL) * pool_scale

def moe_ffn(u, w_router, router_bias, we_gate, we_up, we_down, ws_gate, ws_up, ws_down):
    Bsz, S, D = u.shape
    N = Bsz * S
    uf = u.reshape(N, D)
    scores = jax.nn.sigmoid((uf @ w_router).astype(jnp.float32))
    choice = scores + router_bias.astype(jnp.float32)
    grp = choice.reshape(N, N_EXPERT_GROUPS, EXPERTS_PER_GROUP)
    grp_score = lax.top_k(grp, 2)[0].sum(-1)
    _, top_grp = lax.top_k(grp_score, TOPK_GROUPS)
    grp_mask = jnp.any(top_grp[:, :, None] == jnp.arange(N_EXPERT_GROUPS)[None, None, :], axis=1)
    masked = jnp.where(jnp.repeat(grp_mask, EXPERTS_PER_GROUP, axis=1), choice, -jnp.inf)
    _, top_e = lax.top_k(masked, TOP_K)
    wts = jnp.take_along_axis(scores, top_e, axis=1)
    wts = wts / jnp.sum(wts, axis=-1, keepdims=True) * ROUTED_SCALE
    NK = N * TOP_K
    e_flat = top_e.reshape(NK).astype(jnp.int32)
    tok_flat = jnp.arange(NK, dtype=jnp.int32) // TOP_K
    order = jnp.argsort(e_flat)
    e_sorted = e_flat[order]
    counts = jax.ops.segment_sum(jnp.ones((NK,), jnp.int32), e_flat, num_segments=N_EXPERTS)
    padded = (counts + MOE_BLOCK - 1) // MOE_BLOCK * MOE_BLOCK
    starts = jnp.cumsum(counts) - counts
    pends = jnp.cumsum(padded)
    pstarts = pends - padded
    dest = pstarts[e_sorted] + jnp.arange(NK, dtype=jnp.int32) - starts[e_sorted]
    n_blocks = -(-NK // MOE_BLOCK) + N_EXPERTS
    n_slots = n_blocks * MOE_BLOCK
    slot_tok = jnp.full((n_slots,), N, jnp.int32).at[dest].set(tok_flat[order])
    slot_w = jnp.zeros((n_slots,), u.dtype).at[dest].set(wts.reshape(NK)[order].astype(u.dtype))
    block_e = jnp.minimum(jnp.searchsorted(pends, jnp.arange(n_blocks, dtype=jnp.int32) * MOE_BLOCK, side='right'),
                          N_EXPERTS - 1).astype(jnp.int32)
    u_pad = jnp.concatenate([uf, jnp.zeros((1, D), uf.dtype)], axis=0)

    def expert_block(args):
        toks, ws, e = args
        xb = u_pad[toks]
        hid = jax.nn.silu(xb @ we_gate[e]) * (xb @ we_up[e])
        return (hid @ we_down[e]) * ws[:, None]

    y_slots = lax.map(expert_block, (slot_tok.reshape(n_blocks, MOE_BLOCK),
                                     slot_w.reshape(n_blocks, MOE_BLOCK), block_e))
    routed = jax.ops.segment_sum(y_slots.reshape(n_slots, D), slot_tok, num_segments=N + 1)[:N]
    shared = (jax.nn.silu(uf @ ws_gate) * (uf @ ws_up)) @ ws_down
    return (routed + shared).reshape(Bsz, S, D)

def second_inputs(seed: int = 0) -> dict:
    key = jax.random.key(seed)
    ks = jax.random.split(key, 32)
    f32 = jnp.float32

    def nrm(k, shape, scale):
        return jax.random.normal(k, shape, f32) * scale

    dt0 = jnp.exp(jax.random.uniform(ks[8], (DEPTH, SSD_HEADS), f32, math.log(1e-3), math.log(1e-1)))
    return {
        'x': nrm(ks[0], (BATCH, SEQ, D_MODEL), 1.0),
        'c': nrm(ks[1], (BATCH, D_MODEL), 1.0),
        'w_ada': nrm(ks[2], (DEPTH, D_MODEL, N_ADA * D_MODEL), 0.5 * D_MODEL ** -0.5),
        'b_ada': nrm(ks[3], (DEPTH, N_ADA * D_MODEL), 0.02),
        'norm_mix_g': 1.0 + nrm(ks[4], (DEPTH, D_MODEL), 0.02),
        'w_in': nrm(ks[5], (DEPTH, D_MODEL, D_IN_PROJ), D_MODEL ** -0.5),
        'conv_w': nrm(ks[6], (DEPTH, SSD_CONV, D_XBC), SSD_CONV ** -0.5),
        'conv_b': nrm(ks[7], (DEPTH, D_XBC), 0.02),
        'dt_bias': dt0 + jnp.log(-jnp.expm1(-dt0)),
        'A_log': jnp.log(jax.random.uniform(ks[9], (DEPTH, SSD_HEADS), f32, 1.0, 16.0)),
        'D_skip': 1.0 + nrm(ks[10], (DEPTH, SSD_HEADS), 0.02),
        'ssd_norm_g': 1.0 + nrm(ks[11], (DEPTH, D_SSD), 0.02),
        'pool_w': nrm(ks[12], (DEPTH, POOL_GROUPS, POOL_GDIM, POOL_GDIM), POOL_GDIM ** -0.5),
        'pool_scale': 1.0 + nrm(ks[13], (DEPTH, D_POOL), 0.02),
        'w_br_ssd': nrm(ks[14], (DEPTH, D_SSD, D_MODEL), D_SSD ** -0.5),
        'w_br_pool': nrm(ks[15], (DEPTH, D_POOL, D_MODEL), D_POOL ** -0.5),
        'w_out': nrm(ks[16], (DEPTH, D_MODEL, D_MODEL), D_MODEL ** -0.5),
        'norm_ffn_g': 1.0 + nrm(ks[17], (DEPTH, D_MODEL), 0.02),
        'w_router': nrm(ks[18], (DEPTH, D_MODEL, N_EXPERTS), D_MODEL ** -0.5),
        'router_bias': nrm(ks[19], (DEPTH, N_EXPERTS), 0.01),
        'we_gate': nrm(ks[20], (DEPTH, N_EXPERTS, D_MODEL, D_EXPERT), D_MODEL ** -0.5),
        'we_up': nrm(ks[21], (DEPTH, N_EXPERTS, D_MODEL, D_EXPERT), D_MODEL ** -0.5),
        'we_down': nrm(ks[22], (DEPTH, N_EXPERTS, D_EXPERT, D_MODEL), D_EXPERT ** -0.5),
        'ws_gate': nrm(ks[23], (DEPTH, D_MODEL, D_SHARED), D_MODEL ** -0.5),
        'ws_up': nrm(ks[24], (DEPTH, D_MODEL, D_SHARED), D_MODEL ** -0.5),
        'ws_down': nrm(ks[25], (DEPTH, D_SHARED, D_MODEL), D_SHARED ** -0.5),
        'final_norm_g': 1.0 + nrm(ks[26], (D_MODEL,), 0.02),
    }

def second_block(x, c, w_ada, b_ada, norm_mix_g, w_in, conv_w, conv_b, dt_bias, A_log, D_skip, ssd_norm_g,
              pool_w, pool_scale, w_br_ssd, w_br_pool, w_out, norm_ffn_g, w_router, router_bias,
              we_gate, we_up, we_down, ws_gate, ws_up, ws_down, final_norm_g):
    h = x
    c_act = jax.nn.silu(c)
    for l in range(DEPTH):
        mod = c_act @ w_ada[l] + b_ada[l]
        sh1, sc1, g1, sh2, sc2, g2 = jnp.split(mod, N_ADA, axis=-1)
        u = modulate(rmsnorm(h, norm_mix_g[l]), sh1, sc1)
        proj = u @ w_in[l]
        z, xbc, dt_raw, xp, gts = jnp.split(proj, SPLIT_OFFSETS, axis=-1)
        y_ssd = ssd_branch(z, xbc, dt_raw, conv_w[l], conv_b[l], dt_bias[l], A_log[l], D_skip[l],
                           ssd_norm_g[l]) @ w_br_ssd[l]
        y_pool = pool_branch(xp, pool_w[l], pool_scale[l]) @ w_br_pool[l]
        g_ssd, g_pool = jnp.split(jax.nn.sigmoid(gts), N_BRANCHES, axis=-1)
        mixed = (g_ssd * y_ssd + g_pool * y_pool) @ w_out[l]
        h = h + g1[:, None, :] * mixed
        u2 = modulate(rmsnorm(h, norm_ffn_g[l]), sh2, sc2)
        h = h + g2[:, None, :] * moe_ffn(u2, w_router[l], router_bias[l], we_gate[l], we_up[l], we_down[l],
                                         ws_gate[l], ws_up[l], ws_down[l])
    return rmsnorm(h, final_norm_g)


def setup_inputs(seed=0):
    out = dict(first_inputs(seed))
    for name, value in second_inputs(seed + 1).items():
        if name != "x":
            out[name + "_2"] = value
    return out


def reference(
    x, p, ln_mix, w_in, qk_gain, lam_params, subln_gain, fgate_bias, rel_bias, w_out, ln_ffn,
    w_up, conv_w, conv_b, w_down, ln_ple, w_ple_gate, w_ple_proj, c_2, w_ada_2, b_ada_2,
    norm_mix_g_2, w_in_2, conv_w_2, conv_b_2, dt_bias_2, A_log_2, D_skip_2, ssd_norm_g_2,
    pool_w_2, pool_scale_2, w_br_ssd_2, w_br_pool_2, w_out_2, norm_ffn_g_2, w_router_2,
    router_bias_2, we_gate_2, we_up_2, we_down_2, ws_gate_2, ws_up_2, ws_down_2, final_norm_g_2,
):
    x = first_block(
        x, p, ln_mix, w_in, qk_gain, lam_params, subln_gain, fgate_bias, rel_bias, w_out,
        ln_ffn, w_up, conv_w, conv_b, w_down, ln_ple, w_ple_gate, w_ple_proj,
    )
    return second_block(
        x, c_2, w_ada_2, b_ada_2, norm_mix_g_2, w_in_2, conv_w_2, conv_b_2, dt_bias_2, A_log_2,
        D_skip_2, ssd_norm_g_2, pool_w_2, pool_scale_2, w_br_ssd_2, w_br_pool_2, w_out_2,
        norm_ffn_g_2, w_router_2, router_bias_2, we_gate_2, we_up_2, we_down_2, ws_gate_2,
        ws_up_2, ws_down_2, final_norm_g_2,
    )


_drawn_inputs = setup_inputs


def setup_inputs(seed=0):
    import zlib

    import numpy as np

    out = dict(_drawn_inputs(seed))
    spreads = {}
    factors = {'rel_bias': 3.892,
     'ln_ple': 3.96,
     'norm_mix_g_2': 6.093,
     'conv_b_2': 48.312,
     'D_skip_2': 64.0,
     'ssd_norm_g_2': 51.416,
     'pool_scale_2': 20.559,
     'final_norm_g_2': 7.783,
     'conv_b': 3.03,
     'norm_ffn_g_2': 8.0,
     'router_bias_2': 8.0}
    for name, (base, spread) in spreads.items():
        noise = np.random.default_rng([zlib.crc32(name.encode()), seed]).standard_normal(out[name].shape)
        drawn = base * np.exp(spread * noise) if base else spread * noise
        out[name] = __import__('jax').numpy.asarray(drawn.astype(out[name].dtype))
    for name, factor in factors.items():
        out[name] = (out[name] * factor).astype(out[name].dtype)
    return out
```

```python
import math
from contextlib import ExitStack

import concourse.bass as bass
from concourse import mybir

P = 128
T = 512
D = 1024
KD = D // P
TT = T // P
HD = 64
N_DIFF, N_FOX, N_CHUNK = 4, 6, 6
HEADS = N_DIFF + N_FOX + N_CHUNK
FF = 2816
FT = FF // P
EPS = 1e-6
MASKED = -1e33
LAM_INIT = 0.8 - 0.6 * math.exp(-0.3 * 0)

N_ADA = 6
SG = 8
SH = 32
HPG = SH // SG
E = 64
EG = 8
FE = 256
ROUTED_SCALE = 2.5
WINDOWS = (2, 4, 8, 16)
PAD = 16

COLUMN_SIZES = [
    ("ln_mix", KD), ("ln_ffn", KD), ("ln_ple", KD), ("conv_w", 3 * 2 * FT), ("conv_b", 2 * FT),
    ("qk_gain", 6), ("subln", 1), ("fgate", 1), ("lam", 4 * HD),
    ("c", KD), ("b_ada", N_ADA * KD), ("norm_mix", KD), ("conv_w2", 4 * 32), ("conv_b2", 32),
    ("dt_bias", 1), ("A_log", 1), ("D_skip", 16), ("ssd_norm", 16), ("pool_scale", KD),
    ("norm_ffn", KD), ("router_bias", E), ("final_norm", KD),
]
SHAPE_SIZES = [("ident", P), ("ones_d", P), ("ones_g", P), ("ones_h", P), ("tri", P), ("ones", P),
               ("dist", T), ("causal", T), ("chunked", T), ("inv_count", len(WINDOWS) * PAD),
               ("eps", 1)]


def places(sizes):
    at, found = 0, {}
    for name, n in sizes:
        found[name] = (at, n)
        at += n
    return found, at


COLS, N_COLS = places(COLUMN_SIZES)
SHAPES, N_SHAPES = places(SHAPE_SIZES)

NSLOT = 3
PANEL = KD * 512
RING = NSLOT * PANEL
ARENA = 26200
NSET = 4


def two_blocks(nc, A, out_T, wT_dram):
    f32 = mybir.dt.float32
    ALU = mybir.AluOpType
    ACT = mybir.ActivationFunctionType
    AX = mybir.AxisListType

    ctx = ExitStack()
    with ctx:
        def sb(name, shape):
            return ctx.enter_context(nc.sbuf_tensor(name, shape, f32))

        sems = {}

        def S(name):
            if name not in sems:
                sems[name] = ctx.enter_context(nc.semaphore(name))
            return sems[name]

        cols = sb("cols", [P, N_COLS])
        shp = sb("shp", [P, N_SHAPES])
        h = sb("h", [P, KD, T])
        hn = sb("hn", [P, KD, T])
        sq = sb("sq", [P, 4, T])
        inv = sb("inv", [P, 2, T])
        mod = sb("mod", [P, N_ADA * KD])
        small = sb("small", [P, 192])
        arena = sb("arena", [P, RING + ARENA])
        banks = [ctx.enter_context(nc.psum_tensor(f"bank{i}", [P, 512], f32)) for i in range(8)]
        NORM = 7

        def lay(first, **shapes):
            made = {}
            for name, shape in shapes.items():
                n = 1
                for s in shape:
                    n *= s
                assert first + n <= RING + ARENA, (name, first + n - RING - ARENA)
                v = arena[:, first:first + n]
                if len(shape) == 2:
                    v = v.rearrange("p (a b) -> p a b", b=shape[1])
                if len(shape) == 3:
                    v = v.rearrange("p (a b c) -> p a b c", b=shape[1], c=shape[2])
                made[name] = v
                first += n
            made["end"] = first
            return made

        def col(name, i=0, n=1):
            return cols[:, COLS[name][0] + i:COLS[name][0] + i + n]

        def const(name):
            a, n = SHAPES[name]
            return shp[:, a:a + n]

        ident, ones, tri = const("ident"), const("ones"), const("tri")
        EPS_COLUMN = const("eps")
        LAM_DOT, LAM_EXP = small[:, 0:2], small[:, 2:4]
        NEG_LAM, SUBLN = small[:, 4:5], small[:, 5:6]
        NEG_MAX = small[:, 8:88]
        ROW_SUM = small[:, 88:168]
        RECIP = small[:, 168:172]
        C_ACT = small[:, 172:180]
        GAIN1 = small[:, 180:188]
        EXP_A = small[0:SH, 188:189]

        att = lay(RING, qk=(20, T), V=(TT, D), tab_diff=(N_DIFF, T), tab_chunk=(N_CHUNK, T),
                  F8=(T,), t=(4, T), pt2=(TT, T))
        fgt = lay(RING + 10240 + 4096 + 2048 + 3072 + T, x=(T,), a=(T,), e=(T,), l=(T,), lf=(T,), F=(T,))
        PT = [sq, att["pt2"]]
        NORMED = inv
        ffn = lay(RING, hid=(FT, T), cv=(6, T), sg=(2, T), ada=(12, T))
        ple = lay(RING, pT=(2, T), gt=(2, T), tmp=(2, T))
        mix = lay(RING, yn=(16, T), pooled=(KD, T))
        dtk = lay(mix["end"], dtp=(T,), tok=(TT, 96))
        pool = lay(dtk["end"], x=(2, PAD + T), s=(4, PAD + T), head=(2, PAD), raw=(T,), ab=(T,), l=(T,),
                   a=(T,), acs=(T,))
        ssd = lay(dtk["end"], zs=(4, T), xs=(4, T), B=(2, T), C=(2, T), xtok=(2, 3 * P),
                  xdt=(2, 2 * P), xdec=(2, 2 * P), CB=(2, P), Ex=(2, HPG * P), L=(2, HPG * P),
                  CE=(2, HPG * P), state=(HPG * HD,), carry=(HPG * HD,), th=(2, T))
        late = lay(dtk["end"], gs=(16, T), tmp=(2, T))
        moe = lay(0, w=(NSET, 6144 + T), acc=(KD, T), hid=(4, T), sg=(2, T), wT=(T,), sc=(TT, E), ch=(TT, E),
                  mk=(TT, E), best=(TT, EG * 8), gsum=(TT, EG), gtop=(TT, 8), gm=(TT, EG), gneg=(TT, EG),
                  top=(TT, 8), wsum=(TT,), tmp=(2, T))

        NORMS = {"n1": 0, "n2": 1, "n3": 2, "n4": 3, "n5": 4, "n6": 5}

        PANELS = []

        def slot(i, w):
            v = arena[:, (i % NSLOT) * PANEL:(i % NSLOT) * PANEL + KD * w]
            return v.rearrange("p (k n) -> p k n", n=w)

        def rows(W, k0, k1, c0, c1):
            return W[k0 * P:k1 * P, c0:c1].rearrange("(k p) n -> p k n", p=P)

        def add_panel(copies, semaphore, value):
            i = len(PANELS)
            PANELS.append(([(slot(i, w)[:, 0:b - a, d0:d0 + c1 - c0], rows(W, a, b, c0, c1))
                            for W, a, b, c0, c1, w, d0 in copies], semaphore, value))
            return i

        def one(W, k0, k1, c0, c1):
            return [(W, k0, k1, c0, c1, c1 - c0, 0)]

        Z_PANELS = [(0, 512), (512, 1024), (1024, 1280), (1280, 1664), (1664, 2048), (2048, 2438),
                    (2438, 2822), (2822, 3206), (3206, 3590)]
        V_PANELS = {2: (0, 256), 5: (256, 384), 8: (640, 384)}
        Z_GROUPS = []
        for pn, (c0, c1) in enumerate(Z_PANELS):
            if pn in V_PANELS:
                Z_GROUPS += [("v", pn, tt, V_PANELS[pn][1]) for tt in range(TT)]
                if pn == 5:
                    Z_GROUPS.append(("fg", pn, 384, N_FOX))
            else:
                Z_GROUPS += [("qk", pn, c, P) for c in range(0, c1 - c0, P)]
            add_panel(one(A["w_in"], 0, KD, c0, c1), S("z_ready"), len(Z_GROUPS))
        QK_GAIN = [0, 0, 0, 0, 1, 1, 1, 1, 2, 2, 2, 3, 3, 3, 4, 4, 4, 5, 5, 5]
        Z_FREED = []
        n_qk = n_v = 0
        for kind, *_ in Z_GROUPS:
            if kind == "qk":
                n_qk += 1
                Z_FREED.append((S("qk_done"), n_qk))
            else:
                n_v += 1
                Z_FREED.append((S("v_done"), n_v))

        wo_panel = len(PANELS)
        for half in range(2):
            add_panel(one(A["w_out"], 0, KD, 512 * half, 512 * half + 512), S("wo_ready"), 4 * half + 4)
        up_panel = len(PANELS)
        for q in range(FT // 2):
            add_panel([(A["w_up"], 0, KD, 256 * q, 256 * q + 256, 512, 0),
                       (A["w_up"], 0, KD, FF + 256 * q, FF + 256 * q + 256, 512, 256)],
                      S("up_ready"), 4 * q + 4)
        DOWN_K = [(0, 8), (8, 16), (16, 22)]
        down_panels, ada_panels = [], []
        for half in range(2):
            for k0, k1 in DOWN_K:
                down_panels.append(add_panel(one(A["w_down"], k0, k1, 512 * half, 512 * half + 512),
                                             S("down_part"), len(down_panels) + 1))
                for _ in range(2):
                    m = len(ada_panels)
                    ada_panels.append(add_panel(one(A["w_ada"], 0, KD, 512 * m, 512 * m + 512),
                                                S("ada_sum"), KD * (m + 1)))
        proj_panel = add_panel(one(A["w_ple_proj"], 0, 2, 0, D), S("ple_ready"), 2 * KD)
        gate_panel = len(PANELS)
        for half in range(2):
            add_panel(one(A["w_ple_gate"], 0, KD, 512 * half, 512 * half + 512), S("ple_ready"), 8 * half + 8)

        w_in2 = A["w_in_2"]
        x_panel = len(PANELS)
        for c0, c1, v in ((6144, 6560, 4), (6560, 6944, 7), (6944, 7200, 9)):
            add_panel(one(w_in2, 0, KD, c0, c1), S("x_ready"), v)
        X_TILES = [(x_panel, SH + P * i, 416) for i in range(3)] + \
                  [(x_panel + 1, P * i, 384) for i in range(3)] + [(x_panel + 2, P * i, 256) for i in range(2)]
        pool_panel = add_panel(one(A["pool_w"], 0, KD, 0, 256), S("pool_ready"), KD)
        ssd_panel = len(PANELS)
        for g in range(SG):
            add_panel([(w_in2, 0, KD, 256 * g, 256 * g + 256, 512, 0),
                       (w_in2, 0, KD, 2048 + 256 * g, 2048 + 256 * g + 256, 512, 256)],
                      S("s_ready"), 6 * g + 4)
            add_panel([(w_in2, 0, KD, 4096 + P * g, 4096 + P * g + P, 256, 0),
                       (w_in2, 0, KD, 5120 + P * g, 5120 + P * g + P, 256, P)],
                      S("s_ready"), 6 * g + 6)
        gts_panel = len(PANELS)
        for q in range(4):
            add_panel(one(w_in2, 0, KD, 7200 + 512 * q, 7712 + 512 * q), S("gts_ready"), 4 * q + 4)
        br_panel = len(PANELS)
        for half in range(2):
            for kg in range(2):
                add_panel(one(A["w_br_ssd"], KD * kg, KD * kg + KD, 512 * half, 512 * half + 512),
                          S("br_part"), 2 * half + kg + 1)
        bp_panel = len(PANELS)
        for half in range(2):
            add_panel(one(A["w_br_pool"], 0, KD, 512 * half, 512 * half + 512), S("bp_ready"), 4 * half + 4)
        wo2_panel = len(PANELS)
        for half in range(2):
            add_panel(one(A["w_out_2"], 0, KD, 512 * half, 512 * half + 512), S("wo2_ready"), 4 * half + 4)
        router_panel = add_panel(one(A["w_router"], 0, KD, 0, E), S("router_ready"), TT)

        ARRIVED, counted = [], [0] * NSLOT
        for i, (copies, _, _) in enumerate(PANELS):
            counted[i % NSLOT] += 16 * len(copies)
            ARRIVED.append(counted[i % NSLOT])

        def panel_here(eng, i):
            eng.wait_ge(S(f"panel_in_slot{i % NSLOT}"), ARRIVED[i])

        def s_freed(i):
            g, j = divmod(i, 6)
            return (S("z_read"), 2 * g + j + 1) if j < 2 else (S("s_taps"), 3 * (4 * g + j - 1))

        FILL = ((0, 1), (2,), (3, 4), (5,))

        UNITS, MAPS = [], []
        for hh in range(HEADS):
            for qt in range(TT):
                first = len(MAPS)
                if hh < N_DIFF:
                    MAPS += [(hh // 2, 4 + hh // 2), (2 + hh // 2, 6 + hh // 2)]
                elif hh < N_DIFF + N_FOX:
                    MAPS.append((8 + (hh - N_DIFF) // 2, 11 + (hh - N_DIFF) // 2))
                else:
                    MAPS.append((14 + (hh - N_DIFF - N_FOX) // 2, 17 + (hh - N_DIFF - N_FOX) // 2))
                UNITS.append((hh, qt, first, len(MAPS) - first))

        UNIT_OF = [u for u, (_, _, _, n) in enumerate(UNITS) for _ in range(n)]

        def table(hh, qt):
            if hh < N_DIFF:
                whole = att["tab_diff"][:, hh, :]
            elif hh < N_DIFF + N_FOX:
                whole = const("causal")
            else:
                whole = att["tab_chunk"][:, hh - N_DIFF - N_FOX, :]
            return whole[:, T - P * (qt + 1):T]

        def expert_set(s):
            w = moe["w"][:, s, :]
            return (w[:, 0:4096].rearrange("p (k n) -> p k n", n=512),
                    w[:, 4096:6144].rearrange("p (k n) -> p k n", n=D), w[:, 6144:6144 + T])

        block = ctx.enter_context(nc.Block())

        @block.sync
        def _(sp):
            for i, (copies, _, _) in enumerate(PANELS):
                if i >= NSLOT:
                    sp.wait_ge(PANELS[i - NSLOT][1], PANELS[i - NSLOT][2])
                for dst, src in copies:
                    sp.dma_start(dst, src).then_inc(S(f"panel_in_slot{i % NSLOT}"), 16)

            def load_expert(s, gate, up, down):
                gu, dn, _ = expert_set(s)
                sp.dma_start(gu[:, :, 0:FE], gate.rearrange("(k p) n -> p k n", p=P)).then_inc(S(f"expert_in{s}"), 16)
                sp.dma_start(gu[:, :, FE:2 * FE], up.rearrange("(k p) n -> p k n", p=P)).then_inc(S(f"expert_in{s}"), 16)
                sp.dma_start(dn, down.rearrange("(k p) n -> p k n", p=P)).then_inc(S(f"expert_in{s}"), 16)

            sp.wait_ge(S("router_ready"), TT)
            load_expert(NSET - 1, A["ws_gate"], A["ws_up"], A["ws_down"])

            def load_routed(e, s):
                load_expert(s, A["we_gate"][e], A["we_up"][e], A["we_down"][e])
                sp.dma_start(expert_set(s)[2], wT_dram[e].partition_broadcast(P)).then_inc(S(f"expert_in{s}"), 16)

            sp.wait_ge(S("wT_stored"), 16)
            for s in range(NSET - 1):
                load_routed(s, s)
            sp.wait_ge(S("moe_down"), KD)
            load_routed(NSET - 1, NSET - 1)
            with sp.Fori(1, E // NSET) as i:
                for s in range(NSET):
                    sp.wait_ge(S("moe_down"), (i * NSET + (s + 2 - NSET)) * KD)
                    sp.dma_start(expert_set(s)[0][:, :, 0:FE], A["we_gate"][bass.ds(i * NSET + s, 1)].rearrange("a (k p) n -> p (a k) n", p=P)).then_inc(S(f"expert_in{s}"), 16)
                    sp.dma_start(expert_set(s)[0][:, :, FE:2 * FE], A["we_up"][bass.ds(i * NSET + s, 1)].rearrange("a (k p) n -> p (a k) n", p=P)).then_inc(S(f"expert_in{s}"), 16)
                    sp.dma_start(expert_set(s)[1], A["we_down"][bass.ds(i * NSET + s, 1)].rearrange("a (k p) n -> p (a k) n", p=P)).then_inc(S(f"expert_in{s}"), 16)
                    sp.dma_start(expert_set(s)[2], wT_dram[bass.ds(i * NSET + s, 1)].rearrange("a n -> (a n)").partition_broadcast(P)).then_inc(S(f"expert_in{s}"), 16)

            for k in range(KD):
                sp.wait_ge(S("norm_out"), KD * NORMS["n6"] + k + 1)
                sp.dma_start(out_T[k * P:(k + 1) * P, :], hn[:, k, :]).then_inc(S("stored"), 16)
            sp.wait_ge(S("stored"), 16 * KD)

        @block.gpsimd
        def _(pool_eng):
            pool_eng.dma_start(cols[:, :], A["cols"]).then_inc(S("cols_in"), 16)
            for k in range(4):
                pool_eng.dma_start(h[:, 2 * k:2 * k + 2, :],
                                   A["x_T"][2 * k * P:(2 * k + 2) * P, :].rearrange("(k p) n -> p k n", p=P))\
                        .then_inc(S(f"x_in{k}"), 16)
                if k == 0:
                    pool_eng.dma_start(shp[:, :], A["shape_consts"]).then_inc(S("shp_in"), 16)
            for f in range(N_CHUNK):
                pool_eng.dma_start(att["tab_chunk"][:, f, :], A["rel_rows"][f]).then_inc(S("rel_in"), 16)
            pool_eng.wait_ge(S("down_part"), 6)
            pool_eng.dma_start(ple["pT"], A["p_T"].rearrange("(k p) n -> p k n", p=P)).then_inc(S("p_in"), 16)
            pool_eng.wait_ge(S("ple_ready"), 2 * KD)
            pool_eng.memset(pool["x"][:, :, 0:PAD], 0.0).then_inc(S("pads"), 1)
            pool_eng.memset(pool["s"][:, :, 0:PAD], 0.0).then_inc(S("pads"), 1)
            pool_eng.wait_ge(S("wT_done"), 1)
            pool_eng.dma_start(wT_dram, moe["wT"][0:E, :]).then_inc(S("wT_stored"), 16)
            pool_eng.wait_ge(S("wT_stored"), 16)

        @block.tensor
        def _(pe):
            def product(out, w, rhs, nk, first=True, last=True):
                for k in range(nk):
                    ins = nc.tensor.matmul(out, w(k), rhs(k), start=first and k == 0, stop=last and k == nk - 1)
                return ins

            def norm_sum(name):
                for k in range(KD):
                    pe.wait_ge(S("norm_sq"), KD * NORMS[name] + k + 1)
                    nc.tensor.matmul(banks[NORM][:, :], const("ones_d"), sq[:, k % 4, :], start=k == 0,
                                     stop=k == KD - 1).then_inc(S("norm_sum"), 1)

            def normed(name, k):
                pe.wait_ge(S("norm_out"), KD * NORMS[name] + k + 1)

            pe.wait_ge(S("shp_in"), 16)
            norm_sum("n1")
            j = 0
            pending = None

            def head_sum(j):
                pe.wait_ge(S("qk_sq"), j + 1)
                if j >= 2:
                    pe.wait_ge(S("qk_root"), j - 1)
                nc.tensor.matmul(banks[6 + j % 2][:, :], const("ones_h"), sq[:, j % 4, :], start=True,
                                 stop=True).then_inc(S("qk_sum"), 1)

            for t, (kind, pn, c, width) in enumerate(Z_GROUPS):
                panel_here(pe, pn)
                if t == 0:
                    for k in range(KD):
                        normed("n1", k)
                if t >= 6:
                    pe.wait_ge(*Z_FREED[t - 6])
                w = slot(pn, Z_PANELS[pn][1] - Z_PANELS[pn][0])
                bank = banks[t % 6]
                if kind == "v":
                    ins = product(bank[:, 0:width], lambda k: hn[:, k, c * P:(c + 1) * P],
                                  lambda k: w[:, k, 0:width], KD)
                else:
                    ins = product(bank[0:width, :], lambda k: w[:, k, c:c + width], lambda k: hn[:, k, :], KD)
                ins.then_inc(S("z_ready"), 1)
                if pending is not None:
                    head_sum(pending)
                    pending = None
                if kind == "qk":
                    pending, j = j, j + 1
            if pending is not None:
                head_sum(pending)

            pe.wait_ge(S("qk_done"), 20)
            pe.wait_ge(S("v_done"), 13)
            pe.wait_ge(S("F_done"), 1)

            def scores(u):
                hh, qt, first, n = UNITS[u]
                r = HD * (hh % 2)
                W = P * (qt + 1)
                fox = N_DIFF <= hh < N_DIFF + N_FOX
                for m in range(first, first + n):
                    if m >= 4:
                        pe.wait_ge(S("t_done"), m - 3)
                    out = banks[m % 4][:, 0:W]
                    qi, ki = MAPS[m]
                    ins = nc.tensor.matmul(out, att["qk"][r:r + HD, qi, P * qt:P * qt + P],
                                           att["qk"][r:r + HD, ki, 0:W], start=True, stop=not fox)
                    if fox:
                        f = hh - N_DIFF
                        ins = nc.tensor.matmul(out, ident[0:N_FOX, f:f + 1].to_broadcast([N_FOX, P]),
                                               att["F8"][0:N_FOX, 0:W], start=False, stop=True)
                    ins.then_inc(S("s_scores"), 1)

            def transposes(u):
                hh, qt, first, n = UNITS[u]
                pe.wait_ge(S("probs_done"), u + 1)
                if u >= 2:
                    pe.wait_ge(S("pt_done"), u - 1)
                for kt in range(qt + 1):
                    ins = nc.tensor.transpose(banks[4 + u % 2][:, kt * P:(kt + 1) * P],
                                              NORMED[:, u % 2, kt * P:(kt + 1) * P], ident)
                ins.then_inc(S("tr_ready"), 1)

            def values(hh):
                pe.wait_ge(S("pt_done"), 4 * hh + 4)
                if hh >= 2:
                    pe.wait_ge(S("o_done"), hh - 1)
                for kt in range(TT):
                    ins = nc.tensor.matmul(banks[6 + hh % 2][0:HD, kt * P:T], att["V"][:, kt, HD * hh:HD * hh + HD],
                                           PT[hh % 2][:, kt, kt * P:T], start=kt == 0, stop=kt == TT - 1)
                ins.then_inc(S("o_ready"), 1)

            for u in range(len(UNITS) + 3):
                if u < len(UNITS):
                    scores(u)
                if u >= 3 and (u - 3) % 4 == 3:
                    values((u - 3) // 4)
                if 2 <= u < len(UNITS) + 2:
                    transposes(u - 2)
            for i in range(2):
                pe.wait_ge(S("sub_sq"), i + 1)
                nc.tensor.matmul(banks[i][:, :], const("ones_h"), sq[:, i, :], start=True,
                                 stop=True).then_inc(S("sub_sum"), 1)

            pe.wait_ge(S("o_done"), HEADS)
            pe.wait_ge(S("sub_done"), 2)
            for t in range(KD):
                panel_here(pe, wo_panel + t // 4)
                if t >= 7:
                    pe.wait_ge(S("h1_done"), t - 6)
                w = slot(wo_panel + t // 4, 512)
                product(banks[t % 7][:, :], lambda k: w[:, k, P * (t % 4):P * (t % 4) + P],
                        lambda k: hn[:, k, :], KD).then_inc(S("wo_ready"), 1)
            norm_sum("n2")

            for i in range(2 * FT):
                pn = up_panel + i // 4
                panel_here(pe, pn)
                if i == 0:
                    for k in range(KD):
                        normed("n2", k)
                if i >= 6:
                    pe.wait_ge(S("taps"), 2 * (i - 5))
                c = 256 * (i % 2) + P * ((i // 2) % 2)
                w = slot(pn, 512)
                product(banks[i % 6][:, :], lambda k: w[:, k, c:c + P], lambda k: hn[:, k, :],
                        KD).then_inc(S("up_ready"), 1)
            pe.wait_ge(S("hid_done"), FT)
            for half in range(2):
                for n, (k0, k1) in enumerate(DOWN_K):
                    pn = down_panels[3 * half + n]
                    panel_here(pe, pn)
                    w = slot(pn, 512)
                    for i in range(4):
                        t = 4 * half + i
                        if t == 7 and n == 0:
                            pe.wait_ge(S("h2_done"), 1)
                        ins = product(banks[t % 7][:, :], lambda k: w[:, k, P * i:P * i + P],
                                      lambda k: ffn["hid"][:, k0 + k, :], k1 - k0, n == 0, n == 2)
                        if n == 2 and i < 3:
                            ins.then_inc(S("down_ready"), 1)
                    ins.then_inc(S("down_part"), 1)
            norm_sum("n3")
            for m in range(12):
                pe.wait_ge(S("ada_sum"), KD * (m + 1))
                for i in range(4):
                    ins = nc.tensor.matmul(banks[6][:, 4 * m + i:4 * m + i + 1],
                                           ffn["ada"][:, m, P * i:P * i + P], ones[:, 0:1], start=True, stop=True)
            ins.then_inc(S("ada_ready"), 1)

            pe.wait_ge(S("p_in"), 16)
            for t in range(KD):
                panel_here(pe, proj_panel)
                panel_here(pe, gate_panel + t // 4)
                if t == 0:
                    for k in range(KD):
                        normed("n3", k)
                if t >= 3:
                    pe.wait_ge(S("h3_done"), t - 2)
                w = slot(gate_panel + t // 4, 512)
                product(banks[2 * (t % 3)][:, :], lambda k: w[:, k, P * (t % 4):P * (t % 4) + P],
                        lambda k: hn[:, k, :], KD).then_inc(S("ple_ready"), 1)
                v = slot(proj_panel, D)
                product(banks[2 * (t % 3) + 1][:, :], lambda k: v[:, k, P * t:P * t + P],
                        lambda k: ple["pT"][:, k, :], 2).then_inc(S("ple_ready"), 1)
            norm_sum("n4")

            for i in range(9):
                if i == 0:
                    for k in range(KD):
                        normed("n4", k)
                    panel_here(pe, x_panel)
                    w = slot(x_panel, 416)
                    product(banks[0][0:SH, :], lambda k: w[:, k, 0:SH], lambda k: hn[:, k, :],
                            KD).then_inc(S("x_ready"), 1)
                    continue
                pn, c, width = X_TILES[i - 1]
                panel_here(pe, pn)
                if i >= 6:
                    pe.wait_ge(S("x_copied"), i - 5)
                w = slot(pn, width)
                product(banks[i % 6][:, :], lambda k: w[:, k, c:c + P], lambda k: hn[:, k, :],
                        KD).then_inc(S("x_ready"), 1)
            pe.wait_ge(S("dtp_done"), 1)
            pe.wait_ge(S("dtp_sums"), 1)
            for c in range(TT):
                ins = nc.tensor.transpose(banks[6][:, 96 * c:96 * c + 96], dtk["dtp"][0:96, c * P:(c + 1) * P],
                                          ident[0:96, 0:96])
            ins.then_inc(S("tok_ready"), 1)
            panel_here(pe, pool_panel)
            w = slot(pool_panel, 256)
            pe.wait_ge(S("x_copied"), 9)
            for t in range(KD):
                gi = t // 2
                pe.wait_ge(S("pooled"), 2 * gi + 2)
                if t >= 6:
                    pe.wait_ge(S("pool_out"), t - 5)
                product(banks[t % 6][:, :], lambda k: w[:, 2 * gi + k, P * (t % 2):P * (t % 2) + P],
                        lambda k: mix["pooled"][:, 2 * gi + k, :], 2).then_inc(S("pool_ready"), 1)

            def project(i):
                g, j = divmod(i, 6)
                if j < 4:
                    pn, width, c = ssd_panel + 2 * g, 512, P * j
                else:
                    pn, width, c = ssd_panel + 2 * g + 1, 256, P * (j - 4)
                panel_here(pe, pn)
                if i >= 2:
                    pe.wait_ge(*s_freed(i - 2))
                w = slot(pn, width)
                product(banks[i % 2][:, :], lambda k: w[:, k, c:c + P], lambda k: hn[:, k, :],
                        KD).then_inc(S("s_ready"), 1)

            pe.wait_ge(S("pool_out"), KD)
            pe.wait_ge(S("tok_done"), 1)
            for i in range(6):
                project(i)
            def y_sum(g):
                if g >= 1:
                    pe.wait_ge(S("y_root"), g)
                for i in range(2):
                    pe.wait_ge(S("y_sq"), 2 * g + i + 1)
                    ins = nc.tensor.matmul(banks[7][:, :], const("ones_g"), sq[:, 2 * (g % 2) + i, :],
                                           start=i == 0, stop=i == 1)
                ins.then_inc(S("y_sum"), 1)

            for g in range(SG):
                s = g % 2
                pe.wait_ge(S("xbc_done"), 4 * g + 4)
                for c in range(TT):
                    n = TT * g + c
                    now = slice(c * P, (c + 1) * P)
                    if n >= 1:
                        pe.wait_ge(S("xtok_done"), n)
                    for i in range(2):
                        nc.tensor.transpose(banks[2][:, i * P:(i + 1) * P], ssd["xs"][:, 2 * s + i, now], ident)
                    nc.tensor.transpose(banks[2][:, 2 * P:3 * P], ssd["B"][:, s, now], ident)\
                      .then_inc(S("tr2_ready"), 1)
                    if n >= 1:
                        pe.wait_ge(S("CB_done"), n)
                    nc.tensor.matmul(banks[3][:, 0:P], ssd["B"][:, s, now], ssd["C"][:, s, now], start=True,
                                     stop=True).then_inc(S("CB_ready"), 1)
                    if n >= 1:
                        pe.wait_ge(S("L0_done"), HPG * n)
                    for j in range(HPG):
                        hd = HPG * g + j
                        ins = nc.tensor.matmul(banks[4][:, j * P:(j + 1) * P],
                                               ident[SH:2 * SH, SH + hd:SH + hd + 1].to_broadcast([SH, P]),
                                               dtk["dtp"][SH:2 * SH, now], start=True, stop=True)
                    ins.then_inc(S("cum_ready"), 1)
                    if g + 1 < SG:
                        for i in FILL[c]:
                            project(6 * (g + 1) + i)
                    pe.wait_ge(S("M_done"), n + 1)
                    if c == 0 and g >= 1:
                        pe.wait_ge(S("y_read"), 2 * g)
                    if c >= 1:
                        pe.wait_ge(S("state_done"), 3 * g + c)
                    for j in range(HPG):
                        out = banks[5 + j // 2][HD * (j % 2):HD * (j % 2) + HD, now]
                        ins = nc.tensor.matmul(out, ssd["xdt"][:, n % 2, j * HD:(j + 1) * HD],
                                               ssd["L"][:, n % 2, j * P:(j + 1) * P], start=True, stop=c == 0)
                        if c > 0:
                            ins = nc.tensor.matmul(out, ssd["state"][:, j * HD:(j + 1) * HD],
                                                   ssd["CE"][:, n % 2, j * P:(j + 1) * P], start=False, stop=True)
                    ins.then_inc(S("y_ready"), 1)
                    if c < TT - 1:
                        if 3 * g + c >= 1:
                            pe.wait_ge(S("state_done"), 3 * g + c)
                        nc.tensor.matmul(banks[7][:, 0:HPG * HD], ssd["xtok"][:, n % 2, 2 * P:3 * P],
                                         ssd["xdec"][:, n % 2, :], start=True, stop=True)\
                          .then_inc(S("st_ready"), 1)
            for i in (6 * SG - 2, 6 * SG - 1):
                pe.wait_ge(*s_freed(i))
            pe.wait_ge(S("state_done"), 3 * SG)
            pe.wait_ge(S("y_read"), 2 * SG)
            for t in range(16):
                pn = gts_panel + t // 4
                panel_here(pe, pn)
                if t >= 7:
                    pe.wait_ge(S("gs_copied"), t - 6)
                w = slot(pn, 512)
                product(banks[t % 7][:, :], lambda k: w[:, k, P * (t % 4):P * (t % 4) + P],
                        lambda k: hn[:, k, :], KD).then_inc(S("gts_ready"), 1)
                if t % 2 == 1:
                    y_sum(t // 2)
            pe.wait_ge(S("gs_copied"), 16)
            pe.wait_ge(S("y_root"), SG)
            pe.wait_ge(S("yn_done"), 2 * SG)
            for half in range(2):
                for kg in range(2):
                    pn = br_panel + 2 * half + kg
                    panel_here(pe, pn)
                    w = slot(pn, 512)
                    for i in range(4):
                        ins = product(banks[4 * half + i][:, :], lambda k: w[:, k, P * i:P * i + P],
                                      lambda k: mix["yn"][:, KD * kg + k, :], KD, kg == 0, kg == 1)
                    ins.then_inc(S("br_part"), 1)
            for t in range(KD):
                panel_here(pe, bp_panel + t // 4)
                pe.wait_ge(S("mixed"), t + 1)
                w = slot(bp_panel + t // 4, 512)
                product(banks[t][:, :], lambda k: w[:, k, P * (t % 4):P * (t % 4) + P],
                        lambda k: mix["pooled"][:, k, :], KD).then_inc(S("bp_ready"), 1)
            pe.wait_ge(S("mixed"), 3 * KD)
            for t in range(KD):
                panel_here(pe, wo2_panel + t // 4)
                if t >= 7:
                    pe.wait_ge(S("h4_done"), t - 6)
                w = slot(wo2_panel + t // 4, 512)
                product(banks[t % 7][:, :], lambda k: w[:, k, P * (t % 4):P * (t % 4) + P],
                        lambda k: hn[:, k, :], KD).then_inc(S("wo2_ready"), 1)
            norm_sum("n5")

            panel_here(pe, router_panel)
            w = slot(router_panel, E)
            for k in range(KD):
                normed("n5", k)
            for tt in range(TT):
                product(banks[tt][:, 0:E], lambda k: hn[:, k, tt * P:(tt + 1) * P], lambda k: w[:, k, :],
                        KD).then_inc(S("router_ready"), 1)

            def up(s, n):
                gu, _, _ = expert_set(s)
                for f in range(2):
                    for part in range(2):
                        c = FE * part + P * f
                        ins = product(banks[2 * f + part][:, :], lambda k: gu[:, k, c:c + P],
                                      lambda k: hn[:, k, :], KD)
                    ins.then_inc(S("moe_up"), 1)

            def down(s, parity, n, wait):
                _, dn, _ = expert_set(s)
                pe.wait_ge(S("moe_hid"), n * 2 + 2)
                for d in range(KD):
                    if wait or d >= 4:
                        pe.wait_ge(S("moe_sum"), n * KD + (d - 3))
                    product(banks[4 + d % 4][:, :], lambda k: dn[:, k, P * d:P * d + P],
                            lambda k: moe["hid"][:, 2 * parity + k, :], 2).then_inc(S("moe_down"), 1)

            pe.wait_ge(S("sc_done"), TT)
            pe.wait_ge(S("expert_in3"), 48)
            up(NSET - 1, 0)
            pe.wait_ge(S("wt_done"), TT)
            for tt in range(TT):
                ins = nc.tensor.transpose(banks[4][0:E, tt * P:(tt + 1) * P], moe["sc"][:, tt, :], ident)
            ins.then_inc(S("wT_ready"), 1)
            pe.wait_ge(S("wT_done"), 1)
            down(NSET - 1, 0, 0, False)
            with pe.Fori(0, E // NSET) as i:
                for s in range(NSET):
                    pe.wait_ge(S(f"expert_in{s}"), (i + 1) * 64 + (48 if s == NSET - 1 else 0))
                    pe.wait_ge(S("moe_hid"), i * 2 * NSET + 2 * s + 2)
                    up(s, None)
                    down(s, (s + 1) % 2, i * NSET + (s + 1), True)
            norm_sum("n6")

        @block.scalar
        def _(act):
            def root(out, bank):
                return nc.scalar.activation(out, bank[:, :], ACT.Sqrt, bias=EPS_COLUMN)

            def squares(name, ready):
                for k in range(KD):
                    act.wait_ge(*ready(k))
                    if k >= 4:
                        act.wait_ge(S("norm_sum"), KD * NORMS[name] + k - 3)
                    nc.scalar.activation(sq[:, k % 4, :], h[:, k, :], ACT.Square).then_inc(S("norm_sq"), 1)
                act.wait_ge(S("norm_sum"), KD * NORMS[name] + KD)
                root(inv[:, 0, :], banks[NORM]).then_inc(S("norm_root"), 1)

            def shifted(name, first):
                for k in range(KD):
                    act.wait_ge(S("norm_mul"), KD * (NORMS[name] - NORMS["n4"]) + k + 1)
                    nc.scalar.activation(hn[:, k, :], hn[:, k, :], ACT.Identity,
                                         bias=mod[:, first + k:first + k + 1]).then_inc(S("norm_out"), 1)

            act.wait_ge(S("cols_in"), 16)
            act.wait_ge(S("shp_in"), 16)
            squares("n1", lambda k: (S(f"x_in{k // 2}"), 16))
            act.wait_ge(S("lam_dot"), 2)
            nc.scalar.activation(LAM_EXP, LAM_DOT, ACT.Exp).then_inc(S("lam_exp"), 1)
            j = rooted = 0

            def head_root():
                nonlocal rooted
                if rooted < j:
                    act.wait_ge(S("qk_sum"), rooted + 1)
                    if rooted >= 2:
                        act.wait_ge(S("qk_done"), rooted - 1)
                    root(inv[:, rooted % 2, :], banks[6 + rooted % 2]).then_inc(S("qk_root"), 1)
                    rooted += 1

            for t, (kind, pn, c, width) in enumerate(Z_GROUPS):
                act.wait_ge(S("z_ready"), t + 1)
                bank = banks[t % 6]
                if kind == "qk":
                    if j >= 4:
                        act.wait_ge(S("qk_sum"), j - 3)
                    nc.scalar.activation(sq[:, j % 4, :], bank[:, :], ACT.Square).then_inc(S("qk_sq"), 1)
                    head_root()
                    j += 1
                    continue
                head_root()
                if kind == "v":
                    v0 = V_PANELS[pn][0]
                    nc.scalar.activation(att["V"][:, c, v0:v0 + width], bank[:, 0:width], ACT.Copy)\
                      .then_inc(S("v_done"), 1)
                else:
                    nc.scalar.activation(fgt["x"][0:N_FOX, :], bank[0:N_FOX, :], ACT.Identity,
                                         bias=col("fgate")[0:N_FOX, :]).then_inc(S("v_done"), 1)
                    act.wait_ge(S("v_done"), 9)
                    nc.scalar.activation(fgt["a"][0:N_FOX, :], fgt["x"][0:N_FOX, :], ACT.Abs)\
                      .then_inc(S("fg_step"), 1)
                    act.wait_ge(S("fg_step"), 1)
                    nc.scalar.activation(fgt["e"][0:N_FOX, :], fgt["a"][0:N_FOX, :], ACT.Exp, scale=-1.0)\
                      .then_inc(S("fg_step"), 1)
                    act.wait_ge(S("fg_step"), 2)
                    nc.scalar.activation(fgt["l"][0:N_FOX, :], fgt["e"][0:N_FOX, :], ACT.Ln, bias=1.0)\
                      .then_inc(S("fg_ln"), 1)

            def exponentials(u):
                hh, qt, first, n = UNITS[u]
                for m in range(first, first + n):
                    act.wait_ge(S("t_done"), m + 1)
                    buf = att["t"][:, m % 4, 0:P * (qt + 1)]
                    nc.scalar.activation(buf, buf, ACT.Exp, bias=NEG_MAX[:, m:m + 1], scale=-1.0,
                                         accum_out=ROW_SUM[:, m:m + 1]).then_inc(S("e_done"), 1)

            def transposed(u):
                hh, qt, _, _ = UNITS[u]
                act.wait_ge(S("tr_ready"), u + 1)
                if hh >= 2:
                    act.wait_ge(S("o_ready"), hh - 1)
                nc.scalar.activation(PT[hh % 2][:, 0:qt + 1, qt * P:(qt + 1) * P],
                                     banks[4 + u % 2][:, 0:(qt + 1) * P].rearrange("p (k q) -> p k q", q=P),
                                     ACT.Copy).then_inc(S("pt_done"), 1)

            def head_out(hh):
                act.wait_ge(S("o_ready"), hh + 1)
                r = HD * (hh % 2)
                nc.scalar.activation(hn[r:r + HD, hh // 2, :], banks[6 + hh % 2][0:HD, :], ACT.Copy)\
                  .then_inc(S("o_done"), 1)

            for u in range(len(UNITS) + 3):
                if u < len(UNITS):
                    exponentials(u)
                if 2 <= u < len(UNITS) + 2:
                    transposed(u - 2)
                if u >= 3 and (u - 3) % 4 == 3:
                    head_out((u - 3) // 4)
            for i in range(2):
                act.wait_ge(S("o_done"), HEADS)
                nc.scalar.activation(sq[:, i, :], hn[:, i, :], ACT.Square).then_inc(S("sub_sq"), 1)
            for i in range(2):
                act.wait_ge(S("sub_sum"), i + 1)
                root(inv[:, i, :], banks[i]).then_inc(S("sub_root"), 1)

            squares("n2", lambda k: (S("h1_done"), k + 1))
            nc.scalar.activation(C_ACT, col("c", 0, KD), ACT.Silu).then_inc(S("c_act"), 1)

            def gate(p):
                act.wait_ge(S("taps"), 2 * (2 * p) + 2)
                if p >= 2:
                    act.wait_ge(S("hid_done"), p - 1)
                nc.scalar.activation(ffn["sg"][:, p % 2, :], ffn["cv"][:, 2 * (p % 3), :], ACT.Silu)\
                  .then_inc(S("sg_done"), 1)

            for p in range(FT):
                for part in range(2):
                    i = 2 * p + part
                    act.wait_ge(S("up_ready"), i + 1)
                    if p >= 3:
                        act.wait_ge(S("hid_done"), p - 2)
                    ch = FT * part + p
                    nc.scalar.activation(ffn["cv"][:, i % 6, :], banks[i % 6][:, :], ACT.Identity,
                                         scale=col("conv_w", 2 * 2 * FT + ch), bias=col("conv_b", ch))\
                      .then_inc(S("tap2"), 1)
                if p >= 1:
                    gate(p - 1)
            gate(FT - 1)

            squares("n3", lambda k: (S("h2_done"), k + 1))
            for t in range(KD):
                act.wait_ge(S("ple_ready"), 2 * t + 1)
                if t >= 2:
                    act.wait_ge(S("ple_mul"), t - 1)
                nc.scalar.activation(ple["gt"][:, t % 2, :], banks[2 * (t % 3)][:, :], ACT.Sigmoid)\
                  .then_inc(S("gt_done"), 1)
            squares("n4", lambda k: (S("h3_done"), k + 1))
            shifted("n4", 0)

            nc.scalar.activation(EXP_A, col("A_log")[0:SH, :], ACT.Exp).then_inc(S("expA"), 1)
            act.wait_ge(S("x_ready"), 1)
            nc.scalar.activation(pool["raw"][0:SH, :], banks[0][0:SH, :], ACT.Identity,
                                 bias=col("dt_bias")[0:SH, :]).then_inc(S("x_copied"), 1)
            act.wait_ge(S("x_copied"), 1)
            nc.scalar.activation(pool["ab"][0:SH, :], pool["raw"][0:SH, :], ACT.Abs).then_inc(S("dt_step"), 1)
            act.wait_ge(S("dt_step"), 1)
            nc.scalar.activation(pool["l"][0:SH, :], pool["ab"][0:SH, :], ACT.Exp, scale=-1.0)\
              .then_inc(S("dt_step"), 1)
            act.wait_ge(S("dt_step"), 2)
            nc.scalar.activation(pool["ab"][0:SH, :], pool["l"][0:SH, :], ACT.Ln, bias=1.0)\
              .then_inc(S("dt_ln"), 1)
            act.wait_ge(S("pads"), 2)
            for i in range(1, 9):
                act.wait_ge(S("x_ready"), i + 1)
                if i >= 3:
                    act.wait_ge(S("pooled"), i - 2)
                nc.scalar.activation(pool["x"][:, (i - 1) % 2, PAD:PAD + T], banks[i % 6][:, :], ACT.Copy)\
                  .then_inc(S("x_copied"), 1)
            act.wait_ge(S("dec_arg"), TT)
            nc.scalar.activation(dtk["dtp"][2 * SH:3 * SH, :], pool["a"][0:SH, :], ACT.Exp, scale=-1.0)\
              .then_inc(S("dtp_done"), 1)
            act.wait_ge(S("tok_ready"), 1)
            nc.scalar.activation(dtk["tok"], banks[6][:, 0:TT * 96].rearrange("p (c n) -> p c n", n=96),
                                 ACT.Copy).then_inc(S("tok_done"), 1)
            for t in range(KD):
                act.wait_ge(S("pool_ready"), t + 1)
                act.wait_ge(S("pool_ready"), 2 * (t // 2) + 2)
                nc.scalar.activation(mix["pooled"][:, t, :], banks[t % 6][:, :], ACT.Copy,
                                     scale=col("pool_scale", t)).then_inc(S("pool_out"), 1)

            waiting = []

            def xbc_silu():
                i, buf = waiting.pop(0)
                q = 4 * (i // 6) + i % 6 - 2
                act.wait_ge(*s_freed(i))
                if q >= 2:
                    act.wait_ge(S("xbc_done"), q - 1)
                nc.scalar.activation(ssd["th"][:, q % 2, :], buf, ACT.Tanh).then_inc(S("th_done"), 1)

            def read_tile(i):
                g, j = divmod(i, 6)
                s = g % 2
                act.wait_ge(S("s_ready"), i + 1)
                if g >= 2:
                    act.wait_ge(S("y_gated"), 2 * (g - 1))
                if j < 2:
                    nc.scalar.activation(ssd["zs"][:, 2 * s + j, :], banks[i % 2][:, :], ACT.Tanh,
                                         scale=0.5).then_inc(S("z_tanh"), 1)
                    return
                ch = {2: 2 * g, 3: 2 * g + 1, 4: 16 + g, 5: 24 + g}[j]
                buf = {2: ssd["xs"][:, 2 * s, :], 3: ssd["xs"][:, 2 * s + 1, :], 4: ssd["B"][:, s, :],
                       5: ssd["C"][:, s, :]}[j]
                nc.scalar.activation(buf, banks[i % 2][:, :], ACT.Identity, scale=col("conv_w2", 3 * 32 + ch),
                                     bias=col("conv_b2", ch)).then_inc(S("s_tap3"), 1)
                if waiting:
                    xbc_silu()
                waiting.append((i, buf))

            act.wait_ge(S("halved"), 1)
            for i in range(6):
                read_tile(i)
            xbc_silu()
            for g in range(SG):
                for c in range(TT):
                    n = TT * g + c
                    act.wait_ge(S("tr2_ready"), n + 1)
                    if n >= 2:
                        act.wait_ge(S("st_ready"), 3 * ((n - 2) // TT) + min((n - 2) % TT + 1, TT - 1))
                        act.wait_ge(S("xdec_done"), n - 1)
                    nc.scalar.activation(ssd["xtok"][:, n % 2, :], banks[2][:, 0:3 * P], ACT.Copy)\
                      .then_inc(S("xtok_done"), 1)
                    act.wait_ge(S("cum_ready"), n + 1)
                    if n >= 2:
                        act.wait_ge(S("CE_done"), n - 1)
                        act.wait_ge(S("state_done"), 3 * ((n - 2) // TT) + min((n - 2) % TT + 1, TT - 1))
                    nc.scalar.activation(ssd["Ex"][:, n % 2, :], banks[4][:, :], ACT.Exp).then_inc(S("Ex_done"), 1)
                    act.wait_ge(S("L0_done"), HPG * (n + 1))
                    nc.scalar.activation(ssd["L"][:, n % 2, :], ssd["L"][:, n % 2, :], ACT.Exp)\
                      .then_inc(S("L_done"), 1)
                    if g + 1 < SG:
                        for i in FILL[c]:
                            read_tile(6 * (g + 1) + i)
                        if c == TT - 1:
                            xbc_silu()

            for g in range(SG):
                for i in range(2):
                    act.wait_ge(S("y_gated"), 2 * g + i + 1)
                    if g >= 2:
                        act.wait_ge(S("y_sum"), g - 1)
                    nc.scalar.activation(sq[:, 2 * (g % 2) + i, :], mix["yn"][:, 2 * g + i, :], ACT.Square)\
                      .then_inc(S("y_sq"), 1)
                for t in (2 * g, 2 * g + 1):
                    act.wait_ge(S("gts_ready"), t + 1)
                    act.wait_ge(S("y_gated"), 2 * SG)
                    nc.scalar.activation(late["gs"][:, t, :], banks[t % 7][:, :], ACT.Copy)\
                      .then_inc(S("gs_copied"), 1)
                act.wait_ge(S("y_sum"), g + 1)
                if g >= 2:
                    act.wait_ge(S("yn_done"), 2 * (g - 1))
                root(inv[:, g % 2, :], banks[7]).then_inc(S("y_root"), 1)
            for t in range(16):
                act.wait_ge(S("gs_copied"), t + 1)
                nc.scalar.activation(late["gs"][:, t, :], late["gs"][:, t, :], ACT.Sigmoid).then_inc(S("gs_done"), 1)
            squares("n5", lambda k: (S("h4_done"), k + 1))
            shifted("n5", 3 * KD)

            for tt in range(TT):
                act.wait_ge(S("router_ready"), TT)
                nc.scalar.activation(moe["sc"][:, tt, :], banks[tt][:, 0:E], ACT.Sigmoid).then_inc(S("sc_done"), 1)

            def gate_silu(f):
                nc.scalar.activation(moe["sg"][:, f, :], banks[2 * f][:, :], ACT.Silu).then_inc(S("moe_sg"), 1)

            for f in range(2):
                act.wait_ge(S("moe_up"), f + 1)
                gate_silu(f)
            act.wait_ge(S("wT_ready"), 1)
            nc.scalar.activation(moe["wT"][0:E, :], banks[4][0:E, :], ACT.Copy).then_inc(S("wT_done"), 1)
            with act.Fori(0, E // NSET) as i:
                for s in range(NSET):
                    for f in range(2):
                        act.wait_ge(S("moe_up"), i * 2 * NSET + (2 * (s + 1) + f + 1))
                        act.wait_ge(S("moe_hid"), i * 2 * NSET + (2 * s + f + 1))
                        gate_silu(f)
            squares("n6", lambda k: (S("h5_done"), k + 1))

        @block.vector
        def _(dve):
            def apply_norm(name, gain, done):
                dve.wait_ge(S("norm_root"), NORMS[name] + 1)
                nc.vector.reciprocal(inv[:, 0, :], inv[:, 0, :]).then_inc(S("norm_inv"), 1)
                dve.wait_ge(S("norm_inv"), NORMS[name] + 1)
                for k in range(KD):
                    nc.vector.scalar_tensor_tensor(hn[:, k, :], h[:, k, :], gain(k), inv[:, 0, :], ALU.mult,
                                                   ALU.mult).then_inc(S("norm_" + done), 1)

            dve.wait_ge(S("cols_in"), 16)
            nc.vector.tensor_scalar(col("conv_w2", 0, 5 * 32), col("conv_w2", 0, 5 * 32), 0.5, None, ALU.mult)\
              .then_inc(S("halved"), 1)
            for i in range(2):
                nc.vector.tensor_tensor_reduce(out=inv[:, 1, 64 * i:64 * i + 64], in0=col("lam", 128 * i, 64),
                                               in1=col("lam", 128 * i + 64, 64), scale=1.0, scalar=0.0,
                                               op0=ALU.mult, op1=ALU.add, accum_out=LAM_DOT[:, i:i + 1])\
                  .then_inc(S("lam_dot"), 1)
            nc.vector.tensor_scalar(SUBLN, col("subln"), 1.0 - LAM_INIT, None, ALU.mult).then_inc(S("subln"), 1)
            apply_norm("n1", lambda k: col("ln_mix", k), "out")
            dve.wait_ge(S("lam_exp"), 1)
            nc.vector.tensor_scalar(NEG_LAM, LAM_EXP[:, 1:2], LAM_EXP[:, 0:1], LAM_INIT, ALU.subtract,
                                    ALU.subtract).then_inc(S("neg_lam"), 1)
            dve.wait_ge(S("shp_in"), 16)
            for i in range(N_DIFF):
                nc.vector.tensor_scalar(att["tab_diff"][:, i, :], const("dist"), 8.0 * 2.0 ** (-2.0 * (i + 1)), None,
                                        ALU.mult).then_inc(S("tables"), 1)
            dve.wait_ge(S("rel_in"), 16 * N_CHUNK)
            for f in range(N_CHUNK):
                tab = att["tab_chunk"][:, f, :]
                nc.vector.scalar_tensor_tensor(tab, tab, 8.0, const("chunked"), ALU.mult, ALU.add)\
                  .then_inc(S("tables"), 1)
            j = 0
            for t, (kind, *_) in enumerate(Z_GROUPS):
                if kind == "qk":
                    dve.wait_ge(S("qk_root"), j + 1)
                    nc.vector.reciprocal(inv[:, j % 2, :], inv[:, j % 2, :]).then_inc(S("qk_inv"), 1)
                    dve.wait_ge(S("qk_inv"), j + 1)
                    nc.vector.scalar_tensor_tensor(att["qk"][:, j, :], banks[t % 6][:, :],
                                                   col("qk_gain", QK_GAIN[j]), inv[:, j % 2, :], ALU.mult,
                                                   ALU.mult).then_inc(S("qk_done"), 1)
                    j += 1
                if kind == "fg":
                    dve.wait_ge(S("fg_ln"), 1)
                    nc.vector.scalar_tensor_tensor(fgt["lf"][0:N_FOX, :], fgt["x"][0:N_FOX, :], 0.0,
                                                   fgt["l"][0:N_FOX, :], ALU.min, ALU.subtract)\
                      .then_inc(S("F_step"), 1)
                    dve.wait_ge(S("F_step"), 1)
                    nc.vector.tensor_tensor_scan(fgt["F"][0:N_FOX, :], ones[0:N_FOX, 0:1].to_broadcast([N_FOX, T]),
                                                 fgt["lf"][0:N_FOX, :], 0.0, ALU.mult, ALU.add)\
                      .then_inc(S("F_step"), 1)
                    dve.wait_ge(S("F_step"), 2)
                    nc.vector.tensor_scalar(att["F8"][0:N_FOX, :], fgt["F"][0:N_FOX, :], -8.0, None, ALU.mult)\
                      .then_inc(S("F_done"), 1)

            dve.wait_ge(S("tables"), N_DIFF + N_CHUNK)

            def logits(u):
                hh, qt, first, n = UNITS[u]
                W = P * (qt + 1)
                for m in range(first, first + n):
                    dve.wait_ge(S("s_scores"), m + 1)
                    if m >= 4:
                        dve.wait_ge(S("probs_done"), UNIT_OF[m - 4] + 1)
                    nc.vector.tensor_tensor_reduce(out=att["t"][:, m % 4, 0:W], in0=banks[m % 4][:, 0:W],
                                                   in1=table(hh, qt), scale=-0.125, scalar=3.0e38, op0=ALU.add,
                                                   op1=ALU.min, accum_out=NEG_MAX[:, m:m + 1])\
                      .then_inc(S("t_done"), 1)

            probs_steps = 0

            def probabilities(u):
                nonlocal probs_steps

                def step(ins):
                    nonlocal probs_steps
                    probs_steps += 1
                    ins.then_inc(S("probs_step"), 1)
                    dve.wait_ge(S("probs_step"), probs_steps)

                hh, qt, m, n = UNITS[u]
                W = P * (qt + 1)
                r = RECIP[:, 2 * (u % 2):2 * (u % 2) + n]
                out = NORMED[:, u % 2, 0:W]
                dve.wait_ge(S("e_done"), m + n)
                step(nc.vector.reciprocal(r, ROW_SUM[:, m:m + n]))
                if u >= 2:
                    dve.wait_ge(S("tr_ready"), u - 1)
                if n == 1:
                    nc.vector.tensor_scalar(out, att["t"][:, m % 4, 0:W], r, None, ALU.mult)\
                      .then_inc(S("probs_done"), 1)
                    return
                step(nc.vector.tensor_scalar(r[:, 1:2], r[:, 1:2], NEG_LAM, None, ALU.mult))
                step(nc.vector.tensor_scalar(out, att["t"][:, m % 4, 0:W], r[:, 0:1], None, ALU.mult))
                nc.vector.scalar_tensor_tensor(out, att["t"][:, (m + 1) % 4, 0:W], r[:, 1:2], out, ALU.mult,
                                               ALU.add).then_inc(S("probs_done"), 1)

            dve.wait_ge(S("neg_lam"), 1)
            for u in range(len(UNITS) + 1):
                if u < len(UNITS):
                    logits(u)
                if u >= 1:
                    probabilities(u - 1)
            dve.wait_ge(S("subln"), 1)
            for i in range(2):
                dve.wait_ge(S("sub_root"), i + 1)
                nc.vector.reciprocal(inv[:, i, :], inv[:, i, :]).then_inc(S("sub_inv"), 1)
                dve.wait_ge(S("sub_inv"), i + 1)
                nc.vector.scalar_tensor_tensor(hn[:, i, :], hn[:, i, :], SUBLN, inv[:, i, :], ALU.mult, ALU.mult)\
                  .then_inc(S("sub_done"), 1)
            for t in range(KD):
                dve.wait_ge(S("wo_ready"), t + 1)
                nc.vector.tensor_tensor(h[:, t, :], h[:, t, :], banks[t % 7][:, :], ALU.add).then_inc(S("h1_done"), 1)
            apply_norm("n2", lambda k: col("ln_ffn", k), "out")

            for i in range(2 * FT):
                p, part = divmod(i, 2)
                ch = FT * part + p
                cv, u = ffn["cv"][:, i % 6, :], banks[i % 6]
                dve.wait_ge(S("tap2"), i + 1)
                for back in (1, 2):
                    nc.vector.scalar_tensor_tensor(cv[:, back:T], u[:, 0:T - back],
                                                   col("conv_w", (2 - back) * 2 * FT + ch), cv[:, back:T],
                                                   ALU.mult, ALU.add).then_inc(S("taps"), 1)
                    dve.wait_ge(S("taps"), 2 * i + back)
                if part == 1:
                    dve.wait_ge(S("sg_done"), p + 1)
                    nc.vector.tensor_tensor(ffn["hid"][:, p, :], ffn["sg"][:, p % 2, :], cv, ALU.mult)\
                      .then_inc(S("hid_done"), 1)

            dve.wait_ge(S("c_act"), 1)
            for n in range(6):
                for m in (2 * n, 2 * n + 1):
                    panel_here(dve, ada_panels[m])
                    w = slot(ada_panels[m], 512)
                    out = ffn["ada"][:, m, :]
                    for k in range(KD):
                        if k == 0:
                            ins = nc.vector.tensor_scalar(out, w[:, k, :], C_ACT[:, 0:1], None, ALU.mult)
                        else:
                            ins = nc.vector.scalar_tensor_tensor(out, w[:, k, :], C_ACT[:, k:k + 1], out,
                                                                 ALU.mult, ALU.add)
                        ins.then_inc(S("ada_sum"), 1)
                        dve.wait_ge(S("ada_sum"), KD * m + k + 1)
                if n in (2, 5):
                    half = n // 3
                    dve.wait_ge(S("down_part"), 3 * half + 3)
                    for t in range(4 * half, 4 * half + 4):
                        nc.vector.tensor_tensor(h[:, t, :], h[:, t, :], banks[t % 7][:, :], ALU.add)\
                          .then_inc(S("h2_done"), 1)
            apply_norm("n3", lambda k: col("ln_ple", k), "out")
            dve.wait_ge(S("ada_ready"), 1)
            nc.vector.tensor_tensor(mod[:, :], banks[6][:, 0:N_ADA * KD], col("b_ada", 0, N_ADA * KD), ALU.add)\
              .then_inc(S("mod_done"), 1)

            for t in range(KD):
                dve.wait_ge(S("gt_done"), t + 1)
                dve.wait_ge(S("ple_ready"), 2 * t + 2)
                nc.vector.tensor_tensor(ple["tmp"][:, t % 2, :], ple["gt"][:, t % 2, :], banks[2 * (t % 3) + 1][:, :],
                                        ALU.mult).then_inc(S("ple_mul"), 1)
                dve.wait_ge(S("ple_mul"), t + 1)
                nc.vector.tensor_tensor(h[:, t, :], h[:, t, :], ple["tmp"][:, t % 2, :], ALU.add)\
                  .then_inc(S("h3_done"), 1)

            def modulated(name, gain, first):
                dve.wait_ge(S("mod_done"), 1)
                nc.vector.scalar_tensor_tensor(GAIN1, mod[:, first:first + KD], 1.0, gain, ALU.add, ALU.mult)\
                  .then_inc(S("norm_gain"), 1)
                dve.wait_ge(S("norm_gain"), NORMS[name] - NORMS["n4"] + 1)
                apply_norm(name, lambda k: GAIN1[:, k:k + 1], "mul")

            modulated("n4", col("norm_mix", 0, KD), KD)

            dve.wait_ge(S("dt_ln"), 1)
            dve.wait_ge(S("expA"), 1)
            dt, sums = dtk["dtp"][0:SH, :], pool["acs"][0:SH, :]
            nc.vector.scalar_tensor_tensor(dt, pool["raw"][0:SH, :], 0.0, pool["ab"][0:SH, :], ALU.max, ALU.add)\
              .then_inc(S("dtp_step"), 1)
            dve.wait_ge(S("dtp_step"), 1)
            nc.vector.tensor_scalar(pool["a"][0:SH, :], dt, EXP_A, -1.0, ALU.mult, ALU.mult).then_inc(S("dtp_step"), 1)
            dve.wait_ge(S("dtp_step"), 2)
            for c in range(TT):
                now = slice(c * P, (c + 1) * P)
                nc.vector.tensor_tensor_scan(sums[:, now], ones[0:SH, :], pool["a"][0:SH, now], 0.0, ALU.mult,
                                             ALU.add).then_inc(S("dtp_step"), 1)
            dve.wait_ge(S("dtp_step"), 2 + TT)
            for c in range(TT):
                now = slice(c * P, (c + 1) * P)
                nc.vector.tensor_scalar(pool["a"][0:SH, now], sums[:, now], sums[:, (c + 1) * P - 1:(c + 1) * P],
                                        None, ALU.subtract).then_inc(S("dec_arg"), 1)
            nc.vector.tensor_copy(dtk["dtp"][SH:2 * SH, :], sums).then_inc(S("dtp_sums"), 1)

            dve.wait_ge(S("pads"), 2)
            steps = 0
            for i in range(KD):
                gi = i // 2
                w = WINDOWS[gi]
                x = pool["x"][:, i % 2, :]
                dve.wait_ge(S("x_copied"), i + 2)
                cur, back, a = x, 1, 0
                while back < w:
                    nxt = pool["s"][:, 2 * (i % 2) + a, :]
                    nc.vector.tensor_tensor(nxt[:, PAD:PAD + T], cur[:, PAD:PAD + T], cur[:, PAD - back:PAD + T - back],
                                            ALU.add).then_inc(S("pool_step"), 1)
                    steps += 1
                    dve.wait_ge(S("pool_step"), steps)
                    cur, back, a = nxt, 2 * back, 1 - a
                nc.vector.tensor_tensor(pool["head"][:, i % 2, :], cur[:, PAD:2 * PAD],
                                        shp[:, SHAPES["inv_count"][0] + PAD * gi:SHAPES["inv_count"][0] + PAD * gi + PAD],
                                        ALU.mult).then_inc(S("pool_step"), 1)
                nc.vector.scalar_tensor_tensor(mix["pooled"][:, i, PAD:T], cur[:, 2 * PAD:PAD + T], 1.0 / w,
                                               x[:, 2 * PAD:PAD + T], ALU.mult, ALU.subtract)\
                  .then_inc(S("pool_step"), 1)
                steps += 2
                dve.wait_ge(S("pool_step"), steps)
                nc.vector.tensor_tensor(mix["pooled"][:, i, 0:PAD], pool["head"][:, i % 2, :], x[:, PAD:2 * PAD],
                                        ALU.subtract).then_inc(S("pooled"), 1)

            taps = 0
            waiting = []

            def xbc_silu():
                q, buf = waiting.pop(0)
                dve.wait_ge(S("th_done"), q + 1)
                nc.vector.scalar_tensor_tensor(buf, ssd["th"][:, q % 2, :], 1.0, buf, ALU.add, ALU.mult)\
                  .then_inc(S("xbc_done"), 1)

            def read_tile(i):
                nonlocal taps
                g, j = divmod(i, 6)
                s = g % 2
                if j < 2:
                    zs = ssd["zs"][:, 2 * s + j, :]
                    dve.wait_ge(S("z_tanh"), 2 * g + j + 1)
                    nc.vector.scalar_tensor_tensor(zs, zs, 1.0, banks[i % 2][:, :], ALU.add, ALU.mult)\
                      .then_inc(S("z_read"), 1)
                    return
                ch = {2: 2 * g, 3: 2 * g + 1, 4: 16 + g, 5: 24 + g}[j]
                buf = {2: ssd["xs"][:, 2 * s, :], 3: ssd["xs"][:, 2 * s + 1, :], 4: ssd["B"][:, s, :],
                       5: ssd["C"][:, s, :]}[j]
                dve.wait_ge(S("s_tap3"), 4 * g + j - 1)
                for back in (1, 2, 3):
                    nc.vector.scalar_tensor_tensor(buf[:, back:T], banks[i % 2][:, 0:T - back],
                                                   col("conv_w2", (3 - back) * 32 + ch), buf[:, back:T], ALU.mult,
                                                   ALU.add).then_inc(S("s_taps"), 1)
                    taps += 1
                    dve.wait_ge(S("s_taps"), taps)
                if waiting:
                    xbc_silu()
                waiting.append((4 * g + j - 2, buf))

            def heads(ap, width):
                return ap.rearrange("p (h n) -> p h n", n=width)

            dve.wait_ge(S("tok_done"), 1)
            for i in range(6):
                read_tile(i)
            xbc_silu()
            for g in range(SG):
                s = g % 2
                for c in range(TT):
                    n = TT * g + c
                    b = n % 2
                    now = slice(c * P, (c + 1) * P)
                    per_head = lambda first: dtk["tok"][:, c, first + HPG * g:first + HPG * g + HPG]\
                        .unsqueeze(2).to_broadcast([P, HPG, HD])
                    dve.wait_ge(S("xtok_done"), n + 1)
                    if n >= 2:
                        dve.wait_ge(S("y_ready"), n - 1)
                    nc.vector.tensor_tensor(heads(ssd["xdt"][:, b, :], HD), heads(ssd["xtok"][:, b, 0:2 * P], HD),
                                            per_head(0), ALU.mult).then_inc(S("xdt_done"), 1)
                    dve.wait_ge(S("xdt_done"), n + 1)
                    if n >= 2:
                        dve.wait_ge(S("st_ready"), 3 * ((n - 2) // TT) + min((n - 2) % TT + 1, TT - 1))
                    nc.vector.tensor_tensor(heads(ssd["xdec"][:, b, :], HD), heads(ssd["xdt"][:, b, :], HD),
                                            per_head(2 * SH), ALU.mult).then_inc(S("xdec_done"), 1)
                    dve.wait_ge(S("CB_ready"), n + 1)
                    nc.vector.tensor_tensor(ssd["CB"][:, b, :], banks[3][:, 0:P], tri, ALU.mult)\
                      .then_inc(S("CB_done"), 1)
                    dve.wait_ge(S("Ex_done"), n + 1)
                    for j in range(HPG):
                        a = SH + HPG * g + j
                        nc.vector.tensor_scalar(ssd["L"][:, b, j * P:(j + 1) * P], banks[4][:, j * P:(j + 1) * P],
                                                dtk["tok"][:, c, a:a + 1], 0.0, ALU.subtract, ALU.min)\
                          .then_inc(S("L0_done"), 1)
                    nc.vector.tensor_tensor(heads(ssd["CE"][:, b, :], P), heads(ssd["Ex"][:, b, :], P),
                                            ssd["C"][:, s, now].unsqueeze(1).to_broadcast([P, HPG, P]), ALU.mult)\
                      .then_inc(S("CE_done"), 1)
                    dve.wait_ge(S("L_done"), n + 1)
                    dve.wait_ge(S("CB_done"), n + 1)
                    nc.vector.tensor_tensor(heads(ssd["L"][:, b, :], P), heads(ssd["L"][:, b, :], P),
                                            ssd["CB"][:, b, :].unsqueeze(1).to_broadcast([P, HPG, P]), ALU.mult)\
                      .then_inc(S("M_done"), 1)
                    if g + 1 < SG:
                        for i in FILL[c]:
                            read_tile(6 * (g + 1) + i)
                        if c == TT - 1:
                            xbc_silu()
                    if c < TT - 1:
                        k = 3 * g + c
                        if c > 0:
                            dve.wait_ge(S("state_done"), k)
                            nc.vector.tensor_tensor(heads(ssd["carry"], HD), heads(ssd["state"], HD),
                                                    heads(ssd["Ex"][:, b, :], P)[:, :, P - 1:P]
                                                    .to_broadcast([P, HPG, HD]), ALU.mult)\
                              .then_inc(S("carried"), 1)
                            dve.wait_ge(S("carried"), 2 * g + c)
                        dve.wait_ge(S("st_ready"), k + 1)
                        if c > 0:
                            ins = nc.vector.tensor_tensor(ssd["state"], ssd["carry"], banks[7][:, 0:HPG * HD], ALU.add)
                        else:
                            ins = nc.vector.tensor_copy(ssd["state"], banks[7][:, 0:HPG * HD])
                        ins.then_inc(S("state_done"), 1)
                dve.wait_ge(S("y_ready"), TT * (g + 1))
                for i in range(2):
                    y = mix["yn"][:, 2 * g + i, :]
                    nc.vector.scalar_tensor_tensor(y, ssd["xs"][:, 2 * s + i, :], col("D_skip", 2 * g + i),
                                                   banks[5 + i][:, :], ALU.mult, ALU.add).then_inc(S("y_read"), 1)
                dve.wait_ge(S("y_read"), 2 * g + 2)
                for i in range(2):
                    y = mix["yn"][:, 2 * g + i, :]
                    nc.vector.scalar_tensor_tensor(y, y, 0.5, ssd["zs"][:, 2 * s + i, :], ALU.mult, ALU.mult)\
                      .then_inc(S("y_gated"), 1)
            for g in range(SG):
                dve.wait_ge(S("y_root"), g + 1)
                nc.vector.reciprocal(inv[:, g % 2, :], inv[:, g % 2, :]).then_inc(S("y_inv"), 1)
                dve.wait_ge(S("y_inv"), g + 1)
                for i in range(2):
                    y = mix["yn"][:, 2 * g + i, :]
                    nc.vector.scalar_tensor_tensor(y, y, col("ssd_norm", 2 * g + i), inv[:, g % 2, :], ALU.mult,
                                                   ALU.mult).then_inc(S("yn_done"), 1)

            for t in range(KD):
                dve.wait_ge(S("br_part"), 2 * (t // 4) + 2)
                dve.wait_ge(S("gs_done"), t + 1)
                nc.vector.tensor_tensor(hn[:, t, :], banks[t][:, :], late["gs"][:, t, :], ALU.mult)\
                  .then_inc(S("mixed"), 1)
            for t in range(KD):
                dve.wait_ge(S("bp_ready"), t + 1)
                dve.wait_ge(S("gs_done"), KD + t + 1)
                nc.vector.tensor_tensor(late["tmp"][:, t % 2, :], banks[t][:, :], late["gs"][:, KD + t, :], ALU.mult)\
                  .then_inc(S("mixed"), 1)
                dve.wait_ge(S("mixed"), KD + 2 * t + 1)
                nc.vector.tensor_tensor(hn[:, t, :], hn[:, t, :], late["tmp"][:, t % 2, :], ALU.add)\
                  .then_inc(S("mixed"), 1)
            for t in range(KD):
                dve.wait_ge(S("wo2_ready"), t + 1)
                nc.vector.scalar_tensor_tensor(h[:, t, :], banks[t % 7][:, :], mod[:, 2 * KD + t:2 * KD + t + 1],
                                               h[:, t, :], ALU.mult, ALU.add).then_inc(S("h4_done"), 1)
            modulated("n5", col("norm_ffn", 0, KD), 4 * KD)

            routed = 0

            def step(ins):
                nonlocal routed
                routed += 1
                ins.then_inc(S("route_step"), 1)
                dve.wait_ge(S("route_step"), routed)

            dve.wait_ge(S("sc_done"), TT)
            for tt in range(TT):
                sc, ch, mk = moe["sc"][:, tt, :], moe["ch"][:, tt, :], moe["mk"][:, tt, :]
                best, gsum, gtop = moe["best"][:, tt, :], moe["gsum"][:, tt, :], moe["gtop"][:, tt, :]
                gm, gneg, top, ws = moe["gm"][:, tt, :], moe["gneg"][:, tt, :], moe["top"][:, tt, :], moe["wsum"][:, tt:tt + 1]
                groups = lambda ap: ap.rearrange("p (g e) -> p g e", e=E // EG)
                over = lambda ap: ap.unsqueeze(2).to_broadcast([P, EG, E // EG])
                step(nc.vector.tensor_tensor(ch, sc, col("router_bias", 0, E), ALU.add))
                for g in range(EG):
                    ins = nc.vector.max(best[:, 8 * g:8 * g + 8], ch[:, 8 * g:8 * g + 8])
                    if g < EG - 1:
                        ins.then_inc(S("route_max"), 1)
                step(ins)
                dve.wait_ge(S("route_max"), (EG - 1) * (tt + 1))
                step(nc.vector.tensor_tensor(gsum, groups(best)[:, :, 0], groups(best)[:, :, 1], ALU.add))
                step(nc.vector.max(gtop, gsum))
                step(nc.vector.tensor_scalar(gm, gsum, gtop[:, 3:4], None, ALU.is_ge))
                step(nc.vector.tensor_scalar(gneg, gm, -1.0, 1e30, ALU.add, ALU.mult))
                step(nc.vector.tensor_tensor(groups(mk), groups(ch), over(gm), ALU.mult))
                step(nc.vector.tensor_tensor(groups(mk), groups(mk), over(gneg), ALU.add))
                step(nc.vector.max(top, mk))
                step(nc.vector.tensor_scalar(mk, mk, top[:, 7:8], None, ALU.is_ge))
                step(nc.vector.tensor_tensor(sc, sc, mk, ALU.mult))
                step(nc.vector.tensor_reduce(ws, sc, AX.X, ALU.add))
                step(nc.vector.reciprocal(ws, ws))
                nc.vector.tensor_scalar(sc, sc, ws, ROUTED_SCALE, ALU.mult, ALU.mult).then_inc(S("wt_done"), 1)

            def add_down(n, d, first):
                dve.wait_ge(S("moe_down"), n * KD + (d + 1))
                acc = moe["acc"][:, d, :]
                if first:
                    ins = nc.vector.tensor_copy(acc, banks[4 + d % 4][:, :])
                else:
                    ins = nc.vector.tensor_tensor(acc, acc, banks[4 + d % 4][:, :], ALU.add)
                ins.then_inc(S("moe_sum"), 1)

            for f in range(2):
                dve.wait_ge(S("moe_sg"), f + 1)
                nc.vector.tensor_tensor(moe["hid"][:, f, :], moe["sg"][:, f, :], banks[2 * f + 1][:, :], ALU.mult)\
                  .then_inc(S("moe_hid"), 1)
            for d in range(KD):
                add_down(0, d, True)
            with dve.Fori(0, E // NSET) as i:
                for s in range(NSET):
                    parity = (s + 1) % 2
                    for f in range(2):
                        hid = moe["hid"][:, 2 * parity + f, :]
                        dve.wait_ge(S("moe_sg"), i * 2 * NSET + (2 * (s + 1) + f + 1))
                        nc.vector.tensor_tensor(hid, moe["sg"][:, f, :], banks[2 * f + 1][:, :], ALU.mult)\
                          .then_inc(S("moe_mul"), 1)
                        dve.wait_ge(S("moe_mul"), i * 2 * NSET + (2 * s + f + 1))
                        dve.wait_ge(S(f"expert_in{s}"), (i + 1) * 64 + (48 if s == NSET - 1 else 0))
                        nc.vector.tensor_tensor(hid, hid, expert_set(s)[2], ALU.mult).then_inc(S("moe_hid"), 1)
                    for d in range(KD):
                        add_down(i * NSET + (s + 1), d, False)
            dve.wait_ge(S("moe_sum"), KD * (E + 1))
            for k in range(KD):
                nc.vector.scalar_tensor_tensor(h[:, k, :], moe["acc"][:, k, :], mod[:, 5 * KD + k:5 * KD + k + 1],
                                               h[:, k, :], ALU.mult, ALU.add).then_inc(S("h5_done"), 1)
            apply_norm("n6", lambda k: col("final_norm", k), "out")


def shape_constants(np):
    p = np.arange(P)[:, None]
    j = np.arange(P)[None, :]
    key = np.arange(T)[None, :] - (T - P)
    parts = {
        "ident": (p == j) * 1.0,
        "ones_d": np.full((P, P), 1.0 / D),
        "ones_g": np.full((P, P), 1.0 / 256),
        "ones_h": (p // HD == j // HD) / float(HD),
        "tri": (p <= j) * 1.0,
        "ones": np.ones((P, P)),
        "dist": np.where(key // HD <= p // HD, -np.abs(p - key) * 1.0, MASKED),
        "causal": np.where(key <= p, 0.0, MASKED),
        "chunked": np.where(key // HD <= p // HD, 0.0, MASKED),
        "inv_count": np.concatenate([np.tile(1.0 / np.minimum(np.arange(1, PAD + 1), w), (P, 1))
                                     for w in WINDOWS], axis=1),
        "eps": np.full((P, 1), EPS),
    }
    return np.concatenate([parts[name] for name, _ in SHAPE_SIZES], axis=1).astype(np.float32)


def kernel(**inputs):
    import numpy as np
    import concourse.bacc as bacc
    from concourse.bass_utils import run_bass_kernel_spmd

    x = {name: np.asarray(a) for name, a in inputs.items()}

    def tiles(v):
        v = v.reshape(-1, P)
        return np.ascontiguousarray(v.T)

    def padded(v):
        out = np.zeros((P, v.shape[1]), v.dtype)
        out[:v.shape[0]] = v
        return out

    def everywhere(v):
        return np.repeat(v.reshape(1, -1), P, axis=0)

    gain = x["qk_gain"][0]
    columns = {
        "ln_mix": tiles(x["ln_mix"]), "ln_ffn": tiles(x["ln_ffn"]), "ln_ple": tiles(x["ln_ple"]),
        "conv_w": tiles(x["conv_w"]), "conv_b": tiles(x["conv_b"]),
        "qk_gain": np.concatenate([gain, gain], axis=1).T,
        "subln": np.concatenate([x["subln_gain"][0]] * 2).reshape(P, 1),
        "fgate": padded(x["fgate_bias"].T), "lam": everywhere(x["lam_params"]),
        "c": tiles(x["c_2"]), "b_ada": tiles(x["b_ada_2"]), "norm_mix": tiles(x["norm_mix_g_2"]),
        "conv_w2": tiles(x["conv_w_2"]), "conv_b2": tiles(x["conv_b_2"]),
        "dt_bias": padded(x["dt_bias_2"].T), "A_log": padded(x["A_log_2"].T),
        "D_skip": tiles(np.repeat(x["D_skip_2"][0], HD)), "ssd_norm": tiles(x["ssd_norm_g_2"]),
        "pool_scale": tiles(x["pool_scale_2"]), "norm_ffn": tiles(x["norm_ffn_g_2"]),
        "router_bias": everywhere(x["router_bias_2"]), "final_norm": tiles(x["final_norm_g_2"]),
    }
    distance = np.clip(np.arange(P)[:, None] - (np.arange(T)[None, :] - (T - P)), -P, P) + P
    arrays = {
        "cols": np.concatenate([columns[name] for name, _ in COLUMN_SIZES], axis=1),
        "shape_consts": shape_constants(np),
        "x_T": np.ascontiguousarray(x["x"][0].T),
        "p_T": np.ascontiguousarray(x["p"][0, 0].T),
        "rel_rows": np.ascontiguousarray(x["rel_bias"][0][:, distance]),
        "w_in": x["w_in"][0], "w_out": x["w_out"][0], "w_up": x["w_up"][0], "w_down": x["w_down"][0],
        "w_ple_gate": x["w_ple_gate"][0], "w_ple_proj": x["w_ple_proj"][0], "w_ada": x["w_ada_2"][0],
        "w_in_2": x["w_in_2"][0], "pool_w": x["pool_w_2"][0].reshape(D, 256), "w_br_ssd": x["w_br_ssd_2"][0],
        "w_br_pool": x["w_br_pool_2"][0], "w_out_2": x["w_out_2"][0], "w_router": x["w_router_2"][0],
        "we_gate": x["we_gate_2"][0], "we_up": x["we_up_2"][0], "we_down": x["we_down_2"][0],
        "ws_gate": x["ws_gate_2"][0], "ws_up": x["ws_up_2"][0], "ws_down": x["ws_down_2"][0],
    }
    nc = bacc.Bacc("TRN2", target_bir_lowering=False, num_devices=1)
    feed, A = {}, {}
    for name, a in arrays.items():
        feed[f"in_{name}"] = np.ascontiguousarray(a)
        A[name] = nc.dram_tensor(f"in_{name}", a.shape, mybir.dt.from_np(a.dtype), kind="ExternalInput").ap()
    out_T = nc.dram_tensor("out_T", (D, T), mybir.dt.float32, kind="ExternalOutput").ap()
    wT_dram = nc.dram_tensor("routing_weights", (E, T), mybir.dt.float32, kind="Internal").ap()
    two_blocks(nc, A, out_T, wT_dram)
    result = run_bass_kernel_spmd(nc, [feed], core_ids=[0])
    return np.ascontiguousarray(result.results[0]["out_T"].T).reshape(1, T, D)
```

```python
import math
from contextlib import ExitStack

import concourse.bass as bass
from concourse import mybir

P = 128
T = 512
D = 1024
KD = D // P
TT = T // P
HD = 64
N_DIFF, N_FOX, N_CHUNK = 4, 6, 6
HEADS = N_DIFF + N_FOX + N_CHUNK
FF = 2816
FT = FF // P
EPS = 1e-6
MASKED = -1e33
LAM_INIT = 0.8 - 0.6 * math.exp(-0.3 * 0)

N_ADA = 6
SG = 8
SH = 32
HPG = SH // SG
E = 64
EG = 8
FE = 256
ROUTED_SCALE = 2.5
WINDOWS = (2, 4, 8, 16)
PAD = 16

COLUMN_SIZES = [
    ("ln_mix", KD), ("ln_ffn", KD), ("ln_ple", KD), ("conv_w", 3 * 2 * FT), ("conv_b", 2 * FT),
    ("qk_gain", 6), ("subln", 1), ("fgate", 1), ("lam", 4 * HD),
    ("c", KD), ("b_ada", N_ADA * KD), ("norm_mix", KD), ("conv_w2", 4 * 32), ("conv_b2", 32),
    ("dt_bias", 1), ("A_log", 1), ("D_skip", 16), ("ssd_norm", 16), ("pool_scale", KD),
    ("norm_ffn", KD), ("router_bias", E), ("final_norm", KD),
]
SHAPE_SIZES = [("ident", P), ("ones_d", P), ("ones_g", P), ("ones_h", P), ("tri", P), ("ones", P),
               ("dist", T), ("causal", T), ("chunked", T), ("inv_count", len(WINDOWS) * PAD),
               ("eps", 1), ("before", P), ("iota", P), ("row", 1),
               ("pad_row", 1), ("tokens", TT)]


def places(sizes):
    at, found = 0, {}
    for name, n in sizes:
        found[name] = (at, n)
        at += n
    return found, at


COLS, N_COLS = places(COLUMN_SIZES)
SHAPES, N_SHAPES = places(SHAPE_SIZES)

NSLOT = 3
PANEL = KD * 512
RING = NSLOT * PANEL
ARENA = 25640
TOP = 8
MAX_BLOCKS = T * TOP // P + E
PAD_ROW = T


def two_blocks(nc, A, out_T, u_rows, y_rows):
    f32 = mybir.dt.float32
    ALU = mybir.AluOpType
    ACT = mybir.ActivationFunctionType
    AX = mybir.AxisListType

    ctx = ExitStack()
    with ctx:
        def sb(name, shape):
            return ctx.enter_context(nc.sbuf_tensor(name, shape, f32))

        sems = {}

        def S(name):
            if name not in sems:
                sems[name] = ctx.enter_context(nc.semaphore(name))
            return sems[name]

        cols = sb("cols", [P, N_COLS])
        shp = sb("shp", [P, N_SHAPES])
        h = sb("h", [P, KD, T])
        hn = sb("hn", [P, KD, T])
        sq = sb("sq", [P, 4, T])
        inv = sb("inv", [P, 2, T])
        mod = sb("mod", [P, N_ADA * KD])
        small = sb("small", [P, 192])
        arena = sb("arena", [P, RING + ARENA])
        banks = [ctx.enter_context(nc.psum_tensor(f"bank{i}", [P, 512], f32)) for i in range(8)]
        NORM = 7

        def lay(first, **shapes):
            made = {}
            for name, shape in shapes.items():
                n = 1
                for s in shape:
                    n *= s
                assert first + n <= RING + ARENA, (name, first + n - RING - ARENA)
                v = arena[:, first:first + n]
                if len(shape) == 2:
                    v = v.rearrange("p (a b) -> p a b", b=shape[1])
                if len(shape) == 3:
                    v = v.rearrange("p (a b c) -> p a b c", b=shape[1], c=shape[2])
                made[name] = v
                first += n
            made["end"] = first
            return made

        def col(name, i=0, n=1):
            return cols[:, COLS[name][0] + i:COLS[name][0] + i + n]

        def const(name):
            a, n = SHAPES[name]
            return shp[:, a:a + n]

        ident, ones, tri = const("ident"), const("ones"), const("tri")
        EPS_COLUMN = const("eps")
        LAM_DOT, LAM_EXP = small[:, 0:2], small[:, 2:4]
        NEG_LAM, SUBLN = small[:, 4:5], small[:, 5:6]
        NEG_MAX = small[:, 8:88]
        ROW_SUM = small[:, 88:168]
        RECIP = small[:, 168:172]
        C_ACT = small[:, 172:180]
        GAIN1 = small[:, 180:188]
        EXP_A = small[0:SH, 188:189]

        att = lay(RING, qk=(20, T), V=(TT, D), tab_diff=(N_DIFF, T), tab_chunk=(N_CHUNK, T),
                  F8=(T,), t=(4, T), pt2=(TT, T))
        fgt = lay(RING + 10240 + 4096 + 2048 + 3072 + T, x=(T,), a=(T,), e=(T,), l=(T,), lf=(T,), F=(T,))
        PT = [sq, att["pt2"]]
        NORMED = inv
        ffn = lay(RING, hid=(FT, T), cv=(6, T), sg=(2, T), ada=(12, T))
        ple = lay(RING, pT=(2, T), gt=(2, T), tmp=(2, T))
        mix = lay(RING, yn=(16, T), pooled=(KD, T))
        dtk = lay(mix["end"], dtp=(T,), tok=(TT, 96))
        pool = lay(dtk["end"], x=(2, PAD + T), s=(4, PAD + T), head=(2, PAD), raw=(T,), ab=(T,), l=(T,),
                   a=(T,), acs=(T,))
        ssd = lay(dtk["end"], zs=(4, T), xs=(4, T), B=(2, T), C=(2, T), xtok=(2, 3 * P),
                  xdt=(2, 2 * P), xdec=(2, 2 * P), CB=(2, P), Ex=(2, HPG * P), L=(2, HPG * P),
                  CE=(2, HPG * P), state=(HPG * HD,), carry=(HPG * HD,))
        ssd["th"] = sq[:, 2:4, :]
        late = lay(dtk["end"], gs=(16, T), tmp=(2, T))
        moe = lay(0, gu=(2, KD * 512), dn=(2, 2 * D), X=(2, D), xT=(2, KD * P), sg=(2, FE), hid=(2, FE),
                  hidT=(2, 2 * P), y=(2, D), wcol=(2,), go=(2,), idx=(MAX_BLOCKS,), ws=(MAX_BLOCKS,),
                  sgu=(KD, 512), sdn=(2, D), ssg=(2, FE), sup=(2, FE), shid=(2, FE), shT=(2, 2 * P),
                  sy=(2, D),
                  sc=(TT, E), ch=(TT, E), mk=(TT, E), best=(TT, EG * 8), gsum=(TT, EG), gtop=(TT, EG), gf=(TT, EG),
                  gm=(TT, EG), gneg=(TT, EG), top=(TT, TOP), ef=(TT, TOP), sel=(TT, E), wk=(TT, TOP), wsum=(TT,),
                  junk=(E,), nb=(E,), bend=(E,), bstart=(E,), start=(TT, E), place=(TT * TOP,), blk=(TT * TOP,),
                  spot=(TT * TOP,), ebcol=(2,), ebrow=(MAX_BLOCKS + 1,), OHs=(4, P), OHb=(4, 3 * MAX_BLOCKS),
                  free=(MAX_BLOCKS,))
        moe["zero"] = moe["y"][:, 1, :]
        moe["ut"] = moe["dn"].rearrange("p a (b n) -> p (a b) n", n=D)
        acc = lay(0, acc=(TT, D))["acc"]
        u32, i32 = mybir.dt.uint32, mybir.dt.int32

        def ints(name, n, dt):
            return ctx.enter_context(nc.sbuf_tensor(name, [P, n], dt))

        gix = ints("gix", TT * 8, u32)
        eix = ints("eix", TT * TOP, u32)
        place_i, slot_i = ints("place_i", TT * TOP, i32), ints("slot_i", TT * TOP, i32)
        block_i = ints("block_i", TT * TOP, i32)
        expert_of = ints("expert_of", MAX_BLOCKS + 1, i32)
        rows_in = [ints(f"rows_in{i}", 1, u32) for i in range(2)]
        rows_out = [ints(f"rows_out{i}", 1, u32) for i in range(2)]

        NORMS = {"n1": 0, "n2": 1, "n3": 2, "n4": 3, "n5": 4, "n6": 5}

        N_QK = 20
        PRODUCTS, _ = places([("z", N_QK + 3 * TT + 1), ("wo", KD), ("up", 2 * FT), ("down", 6), ("ple", 2 * KD),
                              ("x", 9), ("pool", KD), ("ssd", 6 * SG), ("gates", 16), ("ssd_out", 4),
                              ("pool_out", KD), ("wo2", KD), ("router", TT)])
        PRODUCTS = {name: first for name, (first, _) in PRODUCTS.items()}
        PREPARED = {"halved": 0, "lam_dot": 1, "subln": 3, "neg_lam": 4, "tables": 5}

        PANELS = []

        def slot(i, w):
            v = arena[:, (i % NSLOT) * PANEL:(i % NSLOT) * PANEL + KD * w]
            return v.rearrange("p (k n) -> p k n", n=w)

        def rows(W, k0, k1, c0, c1):
            return W[k0 * P:k1 * P, c0:c1].rearrange("(k p) n -> p k n", p=P)

        def add_panel(copies, semaphore, value):
            i = len(PANELS)
            PANELS.append(([(slot(i, w)[:, 0:b - a, d0:d0 + c1 - c0], rows(W, a, b, c0, c1))
                            for W, a, b, c0, c1, w, d0 in copies], semaphore, value))
            return i

        def one(W, k0, k1, c0, c1):
            return [(W, k0, k1, c0, c1, c1 - c0, 0)]

        Z_PANELS = [(0, 512), (512, 1024), (1024, 1280), (1280, 1664), (1664, 2048), (2048, 2438),
                    (2438, 2822), (2822, 3206), (3206, 3590)]
        V_PANELS = {2: (0, 256), 5: (256, 384), 8: (640, 384)}
        Z_GROUPS = []
        for pn, (c0, c1) in enumerate(Z_PANELS):
            if pn in V_PANELS:
                Z_GROUPS += [("v", pn, tt, V_PANELS[pn][1]) for tt in range(TT)]
                if pn == 5:
                    Z_GROUPS.append(("fg", pn, 384, N_FOX))
            else:
                Z_GROUPS += [("qk", pn, c, P) for c in range(0, c1 - c0, P)]
            add_panel(one(A["w_in"], 0, KD, c0, c1), S("product"), PRODUCTS["z"] + len(Z_GROUPS))
        QK_GAIN = [0, 0, 0, 0, 1, 1, 1, 1, 2, 2, 2, 3, 3, 3, 4, 4, 4, 5, 5, 5]
        Z_FREED = []
        n_qk = n_v = 0
        for kind, *_ in Z_GROUPS:
            if kind == "qk":
                n_qk += 1
                Z_FREED.append((S("qk_done"), n_qk))
            else:
                n_v += 1
                Z_FREED.append((S("v_done"), n_v))

        wo_panel = len(PANELS)
        for half in range(2):
            add_panel(one(A["w_out"], 0, KD, 512 * half, 512 * half + 512), S("product"), PRODUCTS["wo"] + 4 * half + 4)
        up_panel = len(PANELS)
        for q in range(FT // 2):
            add_panel([(A["w_up"], 0, KD, 256 * q, 256 * q + 256, 512, 0),
                       (A["w_up"], 0, KD, FF + 256 * q, FF + 256 * q + 256, 512, 256)],
                      S("product"), PRODUCTS["up"] + 4 * q + 4)
        DOWN_K = [(0, 8), (8, 16), (16, 22)]
        down_panels, ada_panels = [], []
        for half in range(2):
            for k0, k1 in DOWN_K:
                down_panels.append(add_panel(one(A["w_down"], k0, k1, 512 * half, 512 * half + 512),
                                             S("product"), PRODUCTS["down"] + len(down_panels) + 1))
                for _ in range(2):
                    m = len(ada_panels)
                    ada_panels.append(add_panel(one(A["w_ada"], 0, KD, 512 * m, 512 * m + 512),
                                                S("ada_sum"), KD * (m + 1)))
        proj_panel = add_panel(one(A["w_ple_proj"], 0, 2, 0, D), S("product"), PRODUCTS["ple"] + 2 * KD)
        gate_panel = len(PANELS)
        for half in range(2):
            add_panel(one(A["w_ple_gate"], 0, KD, 512 * half, 512 * half + 512), S("product"), PRODUCTS["ple"] + 8 * half + 8)

        w_in2 = A["w_in_2"]
        x_panel = len(PANELS)
        for c0, c1, v in ((6144, 6560, 4), (6560, 6944, 7), (6944, 7200, 9)):
            add_panel(one(w_in2, 0, KD, c0, c1), S("product"), PRODUCTS["x"] + v)
        X_TILES = [(x_panel, SH + P * i, 416) for i in range(3)] + \
                  [(x_panel + 1, P * i, 384) for i in range(3)] + [(x_panel + 2, P * i, 256) for i in range(2)]
        pool_panel = add_panel(one(A["pool_w"], 0, KD, 0, 256), S("product"), PRODUCTS["pool"] + KD)
        ssd_panel = len(PANELS)
        for g in range(SG):
            add_panel([(w_in2, 0, KD, 256 * g, 256 * g + 256, 512, 0),
                       (w_in2, 0, KD, 2048 + 256 * g, 2048 + 256 * g + 256, 512, 256)],
                      S("product"), PRODUCTS["ssd"] + 6 * g + 4)
            add_panel([(w_in2, 0, KD, 4096 + P * g, 4096 + P * g + P, 256, 0),
                       (w_in2, 0, KD, 5120 + P * g, 5120 + P * g + P, 256, P)],
                      S("product"), PRODUCTS["ssd"] + 6 * g + 6)
        gts_panel = len(PANELS)
        for q in range(4):
            add_panel(one(w_in2, 0, KD, 7200 + 512 * q, 7712 + 512 * q), S("product"), PRODUCTS["gates"] + 4 * q + 4)
        br_panel = len(PANELS)
        for half in range(2):
            for kg in range(2):
                add_panel(one(A["w_br_ssd"], KD * kg, KD * kg + KD, 512 * half, 512 * half + 512),
                          S("product"), PRODUCTS["ssd_out"] + 2 * half + kg + 1)
        bp_panel = len(PANELS)
        for half in range(2):
            add_panel(one(A["w_br_pool"], 0, KD, 512 * half, 512 * half + 512), S("product"), PRODUCTS["pool_out"] + 4 * half + 4)
        wo2_panel = len(PANELS)
        for half in range(2):
            add_panel(one(A["w_out_2"], 0, KD, 512 * half, 512 * half + 512), S("product"), PRODUCTS["wo2"] + 4 * half + 4)
        router_panel = add_panel(one(A["w_router"], 0, KD, 0, E), S("product"), PRODUCTS["router"] + TT)

        ARRIVED, counted = [], [0] * NSLOT
        for i, (copies, _, _) in enumerate(PANELS):
            counted[i % NSLOT] += 16 * len(copies)
            ARRIVED.append(counted[i % NSLOT])

        def panel_here(eng, i):
            eng.wait_ge(S(f"panel_in_slot{i % NSLOT}"), ARRIVED[i])

        def s_freed(i):
            g, j = divmod(i, 6)
            return (S("z_read"), 2 * g + j + 1) if j < 2 else (S("s_taps"), 3 * (4 * g + j - 1))

        FILL = ((0, 1), (2,), (3, 4), (5,))

        UNITS, MAPS = [], []
        for hh in range(HEADS):
            for qt in range(TT):
                first = len(MAPS)
                if hh < N_DIFF:
                    MAPS += [(hh // 2, 4 + hh // 2), (2 + hh // 2, 6 + hh // 2)]
                elif hh < N_DIFF + N_FOX:
                    MAPS.append((8 + (hh - N_DIFF) // 2, 11 + (hh - N_DIFF) // 2))
                else:
                    MAPS.append((14 + (hh - N_DIFF - N_FOX) // 2, 17 + (hh - N_DIFF - N_FOX) // 2))
                UNITS.append((hh, qt, first, len(MAPS) - first))

        UNIT_OF = [u for u, (_, _, _, n) in enumerate(UNITS) for _ in range(n)]

        def table(hh, qt):
            if hh < N_DIFF:
                whole = att["tab_diff"][:, hh, :]
            elif hh < N_DIFF + N_FOX:
                whole = const("causal")
            else:
                whole = att["tab_chunk"][:, hh - N_DIFF - N_FOX, :]
            return whole[:, T - P * (qt + 1):T]

        block = ctx.enter_context(nc.Block())

        @block.sync
        def _(sp):
            for i, (copies, _, _) in enumerate(PANELS):
                if i >= NSLOT:
                    sp.wait_ge(PANELS[i - NSLOT][1], PANELS[i - NSLOT][2])
                for dst, src in copies:
                    sp.dma_start(dst, src).then_inc(S(f"panel_in_slot{i % NSLOT}"), 16)

            sp.wait_ge(S("product"), PRODUCTS["router"] + TT)
            sp.dma_start(moe["sgu"][:, :, 0:FE], A["ws_gate"].rearrange("(k p) n -> p k n", p=P)).then_inc(S("shared_in"), 16)
            sp.dma_start(moe["sgu"][:, :, FE:2 * FE], A["ws_up"].rearrange("(k p) n -> p k n", p=P)).then_inc(S("shared_in"), 16)
            sp.dma_start(moe["sdn"], A["ws_down"].rearrange("(k p) n -> p k n", p=P)).then_inc(S("shared_in"), 16)

            def load_up(b, p):
                e = sp.value_load(expert_of[0:1, bass.ds(b, 1)], min_val=0, max_val=E - 1)
                gu = moe["gu"][:, p, :].rearrange("p (k n) -> p k n", n=512)
                for name, c in (("we_gate", 0), ("we_up", FE)):
                    sp.dma_start(gu[:, :, c:c + FE], A[name][bass.ds(e, 1)].rearrange("a (k p) n -> p (a k) n", p=P))\
                      .then_inc(S(f"up_in{p}"), 16)
                return e

            def load_down(e, p):
                sp.dma_start(moe["dn"][:, p, :].rearrange("p (k n) -> p k n", n=D),
                             A["we_down"][bass.ds(e, 1)].rearrange("a (k p) n -> p (a k) n", p=P))\
                  .then_inc(S(f"down_in{p}"), 16)

            sp.wait_ge(S("blocks_known"), 2)
            pairs_but_one = sp.value_load(expert_of[0:1, MAX_BLOCKS:MAX_BLOCKS + 1], min_val=TT * TOP // 2 - 1,
                                            max_val=MAX_BLOCKS // 2 - 1)
            pairs = pairs_but_one + 1
            sp.wait_ge(S("u_stored"), 16 * TT)
            for p in range(2):
                load_down(load_up(p, p), p)
            with sp.Fori(1, pairs) as i:
                for p in range(2):
                    sp.wait_ge(S("moe_gu"), i * 2 + (p - 1))
                    e = load_up(i * 2 + p, p)
                    sp.wait_ge(S("moe_y"), i * 4 + (2 * p - 2))
                    load_down(e, p)

            for p in range(2):
                sp.wait_ge(S(f"y_added{p}"), pairs * 16 + 16)
            sp.dma_start(acc, y_rows[0:T, :].rearrange("(t p) n -> p t n", p=P)).then_inc(S("acc_in"), 16)

            for k in range(KD):
                sp.wait_ge(S("norm_out"), KD * NORMS["n6"] + k + 1)
                sp.dma_start(out_T[k * P:(k + 1) * P, :], hn[:, k, :]).then_inc(S("stored"), 16)
            sp.wait_ge(S("stored"), 16 * KD)

        @block.gpsimd
        def _(pool_eng):
            pool_eng.dma_start(cols[:, :], A["cols"]).then_inc(S("cols_in"), 16)
            for k in range(4):
                pool_eng.dma_start(h[:, 2 * k:2 * k + 2, :],
                                   A["x_T"][2 * k * P:(2 * k + 2) * P, :].rearrange("(k p) n -> p k n", p=P))\
                        .then_inc(S(f"x_in{k}"), 16)
                if k == 0:
                    pool_eng.dma_start(shp[:, :], A["shape_consts"]).then_inc(S("shp_in"), 16)
            for f in range(N_CHUNK):
                pool_eng.dma_start(att["tab_chunk"][:, f, :], A["rel_rows"][f]).then_inc(S("rel_in"), 16)
            pool_eng.wait_ge(S("product"), PRODUCTS["down"] + 6)
            pool_eng.dma_start(ple["pT"], A["p_T"].rearrange("(k p) n -> p k n", p=P)).then_inc(S("p_in"), 16)
            pool_eng.wait_ge(S("product"), PRODUCTS["ple"] + 2 * KD)
            pool_eng.memset(pool["x"][:, :, 0:PAD], 0.0).then_inc(S("pads"), 1)
            pool_eng.memset(pool["s"][:, :, 0:PAD], 0.0).then_inc(S("pads"), 1)
            pool_eng.wait_ge(S("product"), PRODUCTS["router"] + TT)
            pool_eng.memset(moe["zero"], 0.0).then_inc(S("zero_set"), 1)
            pool_eng.wait_ge(S("zero_set"), 1)
            pool_eng.dma_start(u_rows[T:T + P, :], moe["zero"]).then_inc(S("rows_zeroed"), 16)
            for p in range(2):
                pool_eng.dma_start(y_rows[T + HD * p:T + HD * (p + 1), :], moe["zero"][0:HD, :])\
                        .then_inc(S(f"y_added{p}"), 16)

            for tt in range(TT):
                pool_eng.wait_ge(S("sh_up"), tt + 1)
                if tt >= 2:
                    pool_eng.wait_ge(S("sh_ht"), tt - 1)
                pool_eng.tensor_tensor(moe["shid"][:, tt % 2, :], moe["ssg"][:, tt % 2, :], moe["sup"][:, tt % 2, :],
                                       ALU.mult).then_inc(S("sh_hid"), 1)
            for n in range(TT * TOP):
                pool_eng.wait_ge(S("spots"), 1)
                if n >= 4:
                    pool_eng.wait_ge(S("table_part"), n - 3)
                pool_eng.tensor_scalar(moe["OHs"][:, n % 4, :], const("iota"), moe["spot"][:, n:n + 1], None,
                                       ALU.is_equal).then_inc(S("OHs_done"), 1)

            def gather(b, p):
                pool_eng.tensor_copy(rows_in[p][:, :], moe["idx"][:, bass.ds(b, 1)]).then_inc(S("rows_known"), 1)
                pool_eng.wait_ge(S("rows_known"), b + 1)
                pool_eng.nop(nofuse=True)
                pool_eng.indirect_dma_start(moe["X"][:, p, :], None, u_rows, bass.IndirectOffsetOnAxis(rows_in[p][:, :], 0))\
                        .then_inc(S(f"x_gathered{p}"), 16)

            def scatter(b, p, added):
                pool_eng.tensor_copy(rows_out[p][:, :], moe["idx"][:, bass.ds(b, 1)]).then_inc(S("rows_back"), 1)
                pool_eng.wait_ge(S("rows_back"), b + 1)
                pool_eng.wait_ge(S("y_copied"), b * 2 + (2 * TT + 2))
                pool_eng.wait_ge(S(f"y_added{1 - p}"), added * 16)
                pool_eng.nop(nofuse=True)
                pool_eng.indirect_dma_start(y_rows, bass.IndirectOffsetOnAxis(rows_out[p][:, :], 0), moe["y"][:, p, :], None,
                                            compute_op=ALU.add).then_inc(S(f"y_added{p}"), 16)

            def weights(b, p):
                pool_eng.tensor_copy(moe["wcol"][:, p:p + 1], moe["ws"][:, bass.ds(b, 1)]).then_inc(S("w_known"), 1)

            pool_eng.wait_ge(S("blocks_known"), 2)
            pairs_but_one = pool_eng.value_load(expert_of[0:1, MAX_BLOCKS:MAX_BLOCKS + 1], min_val=TT * TOP // 2 - 1,
                                                max_val=MAX_BLOCKS // 2 - 1)
            pairs = pairs_but_one + 1
            pool_eng.wait_ge(S("u_stored"), 16 * TT)
            pool_eng.wait_ge(S("rows_zeroed"), 16)
            for p in range(2):
                gather(p, p)
                weights(p, p)
            for p in range(2):
                pool_eng.wait_ge(S("moe_tr"), 2 * p + 2)
                gather(2 + p, p)
            for p in range(2):
                pool_eng.wait_ge(S(f"shared_stored{p}"), 16 * TT // 2)
            scatter(0, 0, 1)
            weights(2, 0)
            with pool_eng.Fori(2, pairs) as i:
                pool_eng.wait_ge(S("moe_tr"), i * 4 + (-2))
                gather(i * 2, 0)
                scatter(i * 2 + (-3), 1, i)
                weights(i * 2 + (-1), 1)
                pool_eng.wait_ge(S("moe_tr"), i * 4)
                gather(i * 2 + 1, 1)
                scatter(i * 2 + (-2), 0, i)
                weights(i * 2, 0)
            scatter(pairs_but_one * 2 + (-1), 1, pairs)
            weights(pairs_but_one * 2 + 1, 1)
            scatter(pairs_but_one * 2, 0, pairs)
            scatter(pairs_but_one * 2 + 1, 1, pairs + 1)
        @block.tensor
        def _(pe):
            def product(out, w, rhs, nk, first=True, last=True):
                for k in range(nk):
                    ins = nc.tensor.matmul(out, w(k), rhs(k), start=first and k == 0, stop=last and k == nk - 1)
                return ins

            def norm_sum(name):
                for k in range(KD):
                    pe.wait_ge(S("norm_sq"), KD * NORMS[name] + k + 1)
                    nc.tensor.matmul(banks[NORM][:, :], const("ones_d"), sq[:, k % 4, :], start=k == 0,
                                     stop=k == KD - 1).then_inc(S("norm_sum"), 1)

            def normed(name, k):
                pe.wait_ge(S("norm_out"), KD * NORMS[name] + k + 1)

            pe.wait_ge(S("shp_in"), 16)
            norm_sum("n1")
            j = 0
            pending = None

            def head_sum(j):
                pe.wait_ge(S("qk_sq"), j + 1)
                if j >= 2:
                    pe.wait_ge(S("qk_root"), j - 1)
                nc.tensor.matmul(banks[6 + j % 2][:, :], const("ones_h"), sq[:, j % 4, :], start=True,
                                 stop=True).then_inc(S("qk_sum"), 1)

            for t, (kind, pn, c, width) in enumerate(Z_GROUPS):
                panel_here(pe, pn)
                if t == 0:
                    for k in range(KD):
                        normed("n1", k)
                if t >= 6:
                    pe.wait_ge(*Z_FREED[t - 6])
                w = slot(pn, Z_PANELS[pn][1] - Z_PANELS[pn][0])
                bank = banks[t % 6]
                if kind == "v":
                    ins = product(bank[:, 0:width], lambda k: hn[:, k, c * P:(c + 1) * P],
                                  lambda k: w[:, k, 0:width], KD)
                else:
                    ins = product(bank[0:width, :], lambda k: w[:, k, c:c + width], lambda k: hn[:, k, :], KD)
                ins.then_inc(S("product"), 1)
                if pending is not None:
                    head_sum(pending)
                    pending = None
                if kind == "qk":
                    pending, j = j, j + 1
            if pending is not None:
                head_sum(pending)

            pe.wait_ge(S("qk_done"), N_QK)
            pe.wait_ge(S("v_done"), 13)
            pe.wait_ge(S("F_done"), 1)

            def scores(u):
                hh, qt, first, n = UNITS[u]
                r = HD * (hh % 2)
                W = P * (qt + 1)
                fox = N_DIFF <= hh < N_DIFF + N_FOX
                for m in range(first, first + n):
                    if m >= 4:
                        pe.wait_ge(S("t_done"), m - 3)
                    out = banks[m % 4][:, 0:W]
                    qi, ki = MAPS[m]
                    ins = nc.tensor.matmul(out, att["qk"][r:r + HD, qi, P * qt:P * qt + P],
                                           att["qk"][r:r + HD, ki, 0:W], start=True, stop=not fox)
                    if fox:
                        f = hh - N_DIFF
                        ins = nc.tensor.matmul(out, ident[0:N_FOX, f:f + 1].to_broadcast([N_FOX, P]),
                                               att["F8"][0:N_FOX, 0:W], start=False, stop=True)
                    ins.then_inc(S("s_scores"), 1)

            def transposes(u):
                hh, qt, first, n = UNITS[u]
                pe.wait_ge(S("probs_done"), u + 1)
                if u >= 2:
                    pe.wait_ge(S("pt_done"), u - 1)
                for kt in range(qt + 1):
                    ins = nc.tensor.transpose(banks[4 + u % 2][:, kt * P:(kt + 1) * P],
                                              NORMED[:, u % 2, kt * P:(kt + 1) * P], ident)
                ins.then_inc(S("tr_ready"), 1)

            def values(hh):
                pe.wait_ge(S("pt_done"), 4 * hh + 4)
                if hh >= 2:
                    pe.wait_ge(S("o_done"), hh - 1)
                for kt in range(TT):
                    ins = nc.tensor.matmul(banks[6 + hh % 2][0:HD, kt * P:T], att["V"][:, kt, HD * hh:HD * hh + HD],
                                           PT[hh % 2][:, kt, kt * P:T], start=kt == 0, stop=kt == TT - 1)
                ins.then_inc(S("o_ready"), 1)

            for u in range(len(UNITS) + 3):
                if u < len(UNITS):
                    scores(u)
                if u >= 3 and (u - 3) % 4 == 3:
                    values((u - 3) // 4)
                if 2 <= u < len(UNITS) + 2:
                    transposes(u - 2)
            for i in range(2):
                pe.wait_ge(S("qk_sq"), N_QK + i + 1)
                nc.tensor.matmul(banks[i][:, :], const("ones_h"), sq[:, i, :], start=True,
                                 stop=True).then_inc(S("qk_sum"), 1)

            pe.wait_ge(S("o_done"), HEADS)
            pe.wait_ge(S("qk_done"), N_QK + 2)
            for t in range(KD):
                panel_here(pe, wo_panel + t // 4)
                if t >= 7:
                    pe.wait_ge(S("h_done"), t - 6)
                w = slot(wo_panel + t // 4, 512)
                product(banks[t % 7][:, :], lambda k: w[:, k, P * (t % 4):P * (t % 4) + P],
                        lambda k: hn[:, k, :], KD).then_inc(S("product"), 1)
            norm_sum("n2")

            for i in range(2 * FT):
                pn = up_panel + i // 4
                panel_here(pe, pn)
                if i == 0:
                    for k in range(KD):
                        normed("n2", k)
                if i >= 6:
                    pe.wait_ge(S("taps"), 2 * (i - 5))
                c = 256 * (i % 2) + P * ((i // 2) % 2)
                w = slot(pn, 512)
                product(banks[i % 6][:, :], lambda k: w[:, k, c:c + P], lambda k: hn[:, k, :],
                        KD).then_inc(S("product"), 1)
            pe.wait_ge(S("hid_done"), FT)
            for half in range(2):
                for n, (k0, k1) in enumerate(DOWN_K):
                    pn = down_panels[3 * half + n]
                    panel_here(pe, pn)
                    w = slot(pn, 512)
                    for i in range(4):
                        t = 4 * half + i
                        if t == 7 and n == 0:
                            pe.wait_ge(S("h_done"), KD + 1)
                        ins = product(banks[t % 7][:, :], lambda k: w[:, k, P * i:P * i + P],
                                      lambda k: ffn["hid"][:, k0 + k, :], k1 - k0, n == 0, n == 2)
                    ins.then_inc(S("product"), 1)
            norm_sum("n3")
            for m in range(12):
                pe.wait_ge(S("ada_sum"), KD * (m + 1))
                for i in range(4):
                    ins = nc.tensor.matmul(banks[6][:, 4 * m + i:4 * m + i + 1],
                                           ffn["ada"][:, m, P * i:P * i + P], ones[:, 0:1], start=True, stop=True)
            ins.then_inc(S("ada_ready"), 1)

            pe.wait_ge(S("p_in"), 16)
            for t in range(KD):
                panel_here(pe, proj_panel)
                panel_here(pe, gate_panel + t // 4)
                if t == 0:
                    for k in range(KD):
                        normed("n3", k)
                if t >= 3:
                    pe.wait_ge(S("h_done"), 2 * KD + t - 2)
                w = slot(gate_panel + t // 4, 512)
                product(banks[2 * (t % 3)][:, :], lambda k: w[:, k, P * (t % 4):P * (t % 4) + P],
                        lambda k: hn[:, k, :], KD).then_inc(S("product"), 1)
                v = slot(proj_panel, D)
                product(banks[2 * (t % 3) + 1][:, :], lambda k: v[:, k, P * t:P * t + P],
                        lambda k: ple["pT"][:, k, :], 2).then_inc(S("product"), 1)
            norm_sum("n4")

            for i in range(9):
                if i == 0:
                    for k in range(KD):
                        normed("n4", k)
                    panel_here(pe, x_panel)
                    w = slot(x_panel, 416)
                    product(banks[0][0:SH, :], lambda k: w[:, k, 0:SH], lambda k: hn[:, k, :],
                            KD).then_inc(S("product"), 1)
                    continue
                pn, c, width = X_TILES[i - 1]
                panel_here(pe, pn)
                if i >= 6:
                    pe.wait_ge(S("x_copied"), i - 5)
                w = slot(pn, width)
                product(banks[i % 6][:, :], lambda k: w[:, k, c:c + P], lambda k: hn[:, k, :],
                        KD).then_inc(S("product"), 1)
            pe.wait_ge(S("dtp_done"), 1)
            pe.wait_ge(S("dtp_sums"), 1)
            for c in range(TT):
                ins = nc.tensor.transpose(banks[6][:, 96 * c:96 * c + 96], dtk["dtp"][0:96, c * P:(c + 1) * P],
                                          ident[0:96, 0:96])
            ins.then_inc(S("tok_ready"), 1)
            panel_here(pe, pool_panel)
            w = slot(pool_panel, 256)
            pe.wait_ge(S("x_copied"), 9)
            for t in range(KD):
                gi = t // 2
                pe.wait_ge(S("pooled"), 2 * gi + 2)
                if t >= 6:
                    pe.wait_ge(S("pool_out"), t - 5)
                product(banks[t % 6][:, :], lambda k: w[:, 2 * gi + k, P * (t % 2):P * (t % 2) + P],
                        lambda k: mix["pooled"][:, 2 * gi + k, :], 2).then_inc(S("product"), 1)

            def project(i):
                g, j = divmod(i, 6)
                if j < 4:
                    pn, width, c = ssd_panel + 2 * g, 512, P * j
                else:
                    pn, width, c = ssd_panel + 2 * g + 1, 256, P * (j - 4)
                panel_here(pe, pn)
                if i >= 2:
                    pe.wait_ge(*s_freed(i - 2))
                w = slot(pn, width)
                product(banks[i % 2][:, :], lambda k: w[:, k, c:c + P], lambda k: hn[:, k, :],
                        KD).then_inc(S("product"), 1)

            pe.wait_ge(S("pool_out"), KD)
            pe.wait_ge(S("tok_done"), 1)
            for i in range(6):
                project(i)
            def y_sum(g):
                if g >= 1:
                    pe.wait_ge(S("y_root"), g)
                for i in range(2):
                    pe.wait_ge(S("y_sq"), 2 * g + i + 1)
                    ins = nc.tensor.matmul(banks[7][:, :], const("ones_g"), sq[:, 2 * (g % 2) + i, :],
                                           start=i == 0, stop=i == 1)
                ins.then_inc(S("y_sum"), 1)

            for g in range(SG):
                s = g % 2
                pe.wait_ge(S("xbc_done"), 4 * g + 4)
                for c in range(TT):
                    n = TT * g + c
                    now = slice(c * P, (c + 1) * P)
                    if n >= 1:
                        pe.wait_ge(S("xtok_done"), n)
                    for i in range(2):
                        nc.tensor.transpose(banks[2][:, i * P:(i + 1) * P], ssd["xs"][:, 2 * s + i, now], ident)
                    nc.tensor.transpose(banks[2][:, 2 * P:3 * P], ssd["B"][:, s, now], ident)\
                      .then_inc(S("tr2_ready"), 1)
                    if n >= 1:
                        pe.wait_ge(S("CB_done"), n)
                    nc.tensor.matmul(banks[3][:, 0:P], ssd["B"][:, s, now], ssd["C"][:, s, now], start=True,
                                     stop=True).then_inc(S("CB_ready"), 1)
                    if n >= 1:
                        pe.wait_ge(S("L0_done"), HPG * n)
                    for j in range(HPG):
                        hd = HPG * g + j
                        ins = nc.tensor.matmul(banks[4][:, j * P:(j + 1) * P],
                                               ident[SH:2 * SH, SH + hd:SH + hd + 1].to_broadcast([SH, P]),
                                               dtk["dtp"][SH:2 * SH, now], start=True, stop=True)
                    ins.then_inc(S("cum_ready"), 1)
                    if g + 1 < SG:
                        for i in FILL[c]:
                            project(6 * (g + 1) + i)
                    pe.wait_ge(S("M_done"), n + 1)
                    if c == 0 and g >= 1:
                        pe.wait_ge(S("y_read"), 2 * g)
                    if c >= 1:
                        pe.wait_ge(S("state_done"), 3 * g + c)
                    for j in range(HPG):
                        out = banks[5 + j // 2][HD * (j % 2):HD * (j % 2) + HD, now]
                        ins = nc.tensor.matmul(out, ssd["xdt"][:, n % 2, j * HD:(j + 1) * HD],
                                               ssd["L"][:, n % 2, j * P:(j + 1) * P], start=True, stop=c == 0)
                        if c > 0:
                            ins = nc.tensor.matmul(out, ssd["state"][:, j * HD:(j + 1) * HD],
                                                   ssd["CE"][:, n % 2, j * P:(j + 1) * P], start=False, stop=True)
                    ins.then_inc(S("y_ready"), 1)
                    if c < TT - 1:
                        if 3 * g + c >= 1:
                            pe.wait_ge(S("state_done"), 3 * g + c)
                        nc.tensor.matmul(banks[7][:, 0:HPG * HD], ssd["xtok"][:, n % 2, 2 * P:3 * P],
                                         ssd["xdec"][:, n % 2, :], start=True, stop=True)\
                          .then_inc(S("st_ready"), 1)
            for i in (6 * SG - 2, 6 * SG - 1):
                pe.wait_ge(*s_freed(i))
            pe.wait_ge(S("state_done"), 3 * SG)
            pe.wait_ge(S("y_read"), 2 * SG)
            for t in range(16):
                pn = gts_panel + t // 4
                panel_here(pe, pn)
                if t >= 7:
                    pe.wait_ge(S("gs_copied"), t - 6)
                w = slot(pn, 512)
                product(banks[t % 7][:, :], lambda k: w[:, k, P * (t % 4):P * (t % 4) + P],
                        lambda k: hn[:, k, :], KD).then_inc(S("product"), 1)
                if t % 2 == 1:
                    y_sum(t // 2)
            pe.wait_ge(S("gs_copied"), 16)
            pe.wait_ge(S("y_root"), SG)
            pe.wait_ge(S("yn_done"), 2 * SG)
            for half in range(2):
                for kg in range(2):
                    pn = br_panel + 2 * half + kg
                    panel_here(pe, pn)
                    w = slot(pn, 512)
                    for i in range(4):
                        ins = product(banks[4 * half + i][:, :], lambda k: w[:, k, P * i:P * i + P],
                                      lambda k: mix["yn"][:, KD * kg + k, :], KD, kg == 0, kg == 1)
                    ins.then_inc(S("product"), 1)
            for t in range(KD):
                panel_here(pe, bp_panel + t // 4)
                pe.wait_ge(S("mixed"), t + 1)
                w = slot(bp_panel + t // 4, 512)
                product(banks[t][:, :], lambda k: w[:, k, P * (t % 4):P * (t % 4) + P],
                        lambda k: mix["pooled"][:, k, :], KD).then_inc(S("product"), 1)
            pe.wait_ge(S("mixed"), 3 * KD)
            for t in range(KD):
                panel_here(pe, wo2_panel + t // 4)
                if t >= 7:
                    pe.wait_ge(S("h_done"), 3 * KD + t - 6)
                w = slot(wo2_panel + t // 4, 512)
                product(banks[t % 7][:, :], lambda k: w[:, k, P * (t % 4):P * (t % 4) + P],
                        lambda k: hn[:, k, :], KD).then_inc(S("product"), 1)
            norm_sum("n5")

            panel_here(pe, router_panel)
            w = slot(router_panel, E)
            for k in range(KD):
                normed("n5", k)
            for tt in range(TT):
                product(banks[tt][:, 0:E], lambda k: hn[:, k, tt * P:(tt + 1) * P], lambda k: w[:, k, :],
                        KD).then_inc(S("product"), 1)

            def row_transposes(tt):
                for half in range(2):
                    bank = banks[4 + (2 * tt + half) % 4]
                    if tt >= 2:
                        pe.wait_ge(S("ut_done"), 2 * (tt - 2) + half + 1)
                    for q in range(4):
                        ins = nc.tensor.transpose(bank[:, q * P:(q + 1) * P], hn[:, 4 * half + q, tt * P:(tt + 1) * P],
                                                  ident)
                    ins.then_inc(S("ut_ready"), 1)

            def shared_up(tt):
                if tt >= 2:
                    pe.wait_ge(S("sh_up"), tt - 1)
                product(banks[tt % 2][:, :], lambda k: hn[:, k, tt * P:(tt + 1) * P], lambda k: moe["sgu"][:, k, :],
                        KD).then_inc(S("sh_gu"), 1)

            def shared_transposes(tt):
                pe.wait_ge(S("sh_hid"), tt + 1)
                if tt >= 1:
                    pe.wait_ge(S("sh_hT"), tt)
                for f in range(2):
                    ins = nc.tensor.transpose(banks[2][:, f * P:(f + 1) * P],
                                              moe["shid"][:, tt % 2, f * P:(f + 1) * P], ident)
                ins.then_inc(S("sh_ht"), 1)

            def shared_down(tt):
                pe.wait_ge(S("sh_hT"), tt + 1)
                for half in range(2):
                    if tt >= 2:
                        pe.wait_ge(S("y_copied"), 2 * (tt - 2) + half + 1)
                    else:
                        pe.wait_ge(S("ut_done"), 2 * TT)
                    product(banks[4 + (2 * tt + half) % 4][:, :], lambda k: moe["shT"][:, tt % 2, k * P:(k + 1) * P],
                            lambda k: moe["sdn"][:, k, 512 * half:512 * half + 512], 2).then_inc(S("sh_y"), 1)

            def counts():
                pe.wait_ge(S("selected"), TT)
                for tt in range(TT):
                    for before in range(tt + 1):
                        nc.tensor.matmul(banks[3][:, tt * E:(tt + 1) * E], ones if before < tt else const("before"),
                                         moe["sel"][:, before, :], start=before == 0, stop=before == tt)
                for tt in range(TT):
                    ins = nc.tensor.matmul(banks[3][:, TT * E:(TT + 1) * E], ones, moe["sel"][:, tt, :], start=tt == 0,
                                           stop=tt == TT - 1)
                ins.then_inc(S("counted"), 1)

            for tt in range(TT):
                row_transposes(tt)
            pe.wait_ge(S("sc_done"), TT)
            pe.wait_ge(S("shared_in"), 48)
            shared_up(0)
            shared_up(1)
            shared_transposes(0)
            shared_up(2)
            shared_down(0)
            shared_transposes(1)
            shared_up(3)
            shared_down(1)
            counts()
            for tt in (2, 3):
                shared_transposes(tt)
                shared_down(tt)
            pe.wait_ge(S("ebcol_done"), 1)
            nc.tensor.matmul(banks[3][0:1, 384:512], moe["ebcol"][:, 0:1], ident, start=True, stop=True)\
              .then_inc(S("eb_ready"), 1)
            pe.wait_ge(S("sh_hT"), TT)
            for n in range(TT * TOP):
                pe.wait_ge(S("OHs_done"), n + 1)
                pe.wait_ge(S("OHb_done"), 3 * n + 3)
                nc.tensor.matmul(banks[2][:, 0:3 * MAX_BLOCKS], moe["OHs"][:, n % 4, :], moe["OHb"][:, n % 4, :],
                                 start=n == 0, stop=n == TT * TOP - 1).then_inc(S("table_part"), 1)

            def block_transposes(b, p, gathers):
                pe.wait_ge(S(f"x_gathered{p}"), gathers * 16)
                for half in range(2):
                    for q in range(4):
                        c = (4 * half + q) * P
                        ins = nc.tensor.transpose(banks[half][:, q * P:(q + 1) * P], moe["X"][:, p, c:c + P], ident)
                    ins.then_inc(S("moe_tr"), 1)

            def block_up(b, p, loads):
                pe.wait_ge(S("xT_done"), b * 2 + 2)
                pe.wait_ge(S(f"up_in{p}"), loads * 32)
                product(banks[2 + p][:, :], lambda k: moe["xT"][:, p, k * P:(k + 1) * P],
                        lambda k: moe["gu"][:, p, k * 512:(k + 1) * 512], KD).then_inc(S("moe_gu"), 1)

            def hidden_transposes(b, p):
                pe.wait_ge(S("moe_hid"), b + 1)
                for f in range(2):
                    ins = nc.tensor.transpose(banks[4][:, f * P:(f + 1) * P], moe["hid"][:, p, f * P:(f + 1) * P],
                                              ident)
                ins.then_inc(S("moe_ht"), 1)

            def block_down(b, p, loads):
                pe.wait_ge(S("hT_done"), b + 1)
                pe.wait_ge(S(f"down_in{p}"), loads * 16)
                for half in range(2):
                    pe.wait_ge(S("y_copied"), b * 2 + (2 * TT + half - 1))
                    product(banks[5 + half][:, :], lambda k: moe["hidT"][:, p, k * P:(k + 1) * P],
                            lambda k: moe["dn"][:, p, k * D + 512 * half:k * D + 512 * half + 512], 2)\
                        .then_inc(S("moe_y"), 1)

            pe.wait_ge(S("blocks_known"), 2)
            pairs_but_one = pe.value_load(expert_of[0:1, MAX_BLOCKS:MAX_BLOCKS + 1], min_val=TT * TOP // 2 - 1,
                                            max_val=MAX_BLOCKS // 2 - 1)
            pairs = pairs_but_one + 1
            block_transposes(0, 0, 1)
            pe.wait_ge(S("xT_done"), 2)
            block_transposes(1, 1, 1)
            block_up(0, 0, 1)
            with pe.Fori(1, pairs) as i:
                for b, p, loads, next_gathers, last_loads in ((i * 2 + (-1), 1, i, i + 1, i),
                                                              (i * 2, 0, i + 1, i + 1, i)):
                    hidden_transposes(b + (-1), 1 - p)
                    pe.wait_ge(S("xT_done"), b * 2 + 2)
                    block_transposes(b + 1, 1 - p, next_gathers)
                    block_up(b, p, loads)
                    block_down(b + (-1), 1 - p, last_loads)
            hidden_transposes(pairs_but_one * 2, 0)
            block_up(pairs_but_one * 2 + 1, 1, pairs)
            block_down(pairs_but_one * 2, 0, pairs)
            hidden_transposes(pairs_but_one * 2 + 1, 1)
            block_down(pairs_but_one * 2 + 1, 1, pairs)

            pe.wait_ge(S("acc_in"), 16)
            for d in range(KD):
                if d >= 7:
                    pe.wait_ge(S("h_done"), 4 * KD + d - 6)
                for tt in range(TT):
                    ins = nc.tensor.transpose(banks[d % 7][:, tt * P:(tt + 1) * P], acc[:, tt, d * P:(d + 1) * P], ident)
                ins.then_inc(S("acc_T"), 1)
            norm_sum("n6")

        @block.scalar
        def _(act):
            def root(out, bank):
                return nc.scalar.activation(out, bank[:, :], ACT.Sqrt, bias=EPS_COLUMN)

            def squares(name, ready):
                for k in range(KD):
                    act.wait_ge(*ready(k))
                    if k >= 4:
                        act.wait_ge(S("norm_sum"), KD * NORMS[name] + k - 3)
                    nc.scalar.activation(sq[:, k % 4, :], h[:, k, :], ACT.Square).then_inc(S("norm_sq"), 1)
                act.wait_ge(S("norm_sum"), KD * NORMS[name] + KD)
                root(inv[:, 0, :], banks[NORM]).then_inc(S("norm_root"), 1)

            def shifted(name, first):
                for k in range(KD):
                    act.wait_ge(S("norm_mul"), KD * (NORMS[name] - NORMS["n4"]) + k + 1)
                    nc.scalar.activation(hn[:, k, :], hn[:, k, :], ACT.Identity,
                                         bias=mod[:, first + k:first + k + 1]).then_inc(S("norm_out"), 1)

            act.wait_ge(S("cols_in"), 16)
            act.wait_ge(S("shp_in"), 16)
            squares("n1", lambda k: (S(f"x_in{k // 2}"), 16))
            act.wait_ge(S("prepared"), PREPARED["lam_dot"] + 2)
            nc.scalar.activation(LAM_EXP, LAM_DOT, ACT.Exp).then_inc(S("lam_exp"), 1)
            j = rooted = 0

            def head_root():
                nonlocal rooted
                if rooted < j:
                    act.wait_ge(S("qk_sum"), rooted + 1)
                    if rooted >= 2:
                        act.wait_ge(S("qk_done"), rooted - 1)
                    root(inv[:, rooted % 2, :], banks[6 + rooted % 2]).then_inc(S("qk_root"), 1)
                    rooted += 1

            for t, (kind, pn, c, width) in enumerate(Z_GROUPS):
                act.wait_ge(S("product"), PRODUCTS["z"] + t + 1)
                bank = banks[t % 6]
                if kind == "qk":
                    if j >= 4:
                        act.wait_ge(S("qk_sum"), j - 3)
                    nc.scalar.activation(sq[:, j % 4, :], bank[:, :], ACT.Square).then_inc(S("qk_sq"), 1)
                    head_root()
                    j += 1
                    continue
                head_root()
                if kind == "v":
                    v0 = V_PANELS[pn][0]
                    nc.scalar.activation(att["V"][:, c, v0:v0 + width], bank[:, 0:width], ACT.Copy)\
                      .then_inc(S("v_done"), 1)
                else:
                    nc.scalar.activation(fgt["x"][0:N_FOX, :], bank[0:N_FOX, :], ACT.Identity,
                                         bias=col("fgate")[0:N_FOX, :]).then_inc(S("v_done"), 1)
                    act.wait_ge(S("v_done"), 9)
                    nc.scalar.activation(fgt["a"][0:N_FOX, :], fgt["x"][0:N_FOX, :], ACT.Abs)\
                      .then_inc(S("act_step"), 1)
                    act.wait_ge(S("act_step"), 1)
                    nc.scalar.activation(fgt["e"][0:N_FOX, :], fgt["a"][0:N_FOX, :], ACT.Exp, scale=-1.0)\
                      .then_inc(S("act_step"), 1)
                    act.wait_ge(S("act_step"), 2)
                    nc.scalar.activation(fgt["l"][0:N_FOX, :], fgt["e"][0:N_FOX, :], ACT.Ln, bias=1.0)\
                      .then_inc(S("fg_ln"), 1)

            def exponentials(u):
                hh, qt, first, n = UNITS[u]
                for m in range(first, first + n):
                    act.wait_ge(S("t_done"), m + 1)
                    buf = att["t"][:, m % 4, 0:P * (qt + 1)]
                    nc.scalar.activation(buf, buf, ACT.Exp, bias=NEG_MAX[:, m:m + 1], scale=-1.0,
                                         accum_out=ROW_SUM[:, m:m + 1]).then_inc(S("e_done"), 1)

            def transposed(u):
                hh, qt, _, _ = UNITS[u]
                act.wait_ge(S("tr_ready"), u + 1)
                if hh >= 2:
                    act.wait_ge(S("o_ready"), hh - 1)
                nc.scalar.activation(PT[hh % 2][:, 0:qt + 1, qt * P:(qt + 1) * P],
                                     banks[4 + u % 2][:, 0:(qt + 1) * P].rearrange("p (k q) -> p k q", q=P),
                                     ACT.Copy).then_inc(S("pt_done"), 1)

            def head_out(hh):
                act.wait_ge(S("o_ready"), hh + 1)
                r = HD * (hh % 2)
                nc.scalar.activation(hn[r:r + HD, hh // 2, :], banks[6 + hh % 2][0:HD, :], ACT.Copy)\
                  .then_inc(S("o_done"), 1)

            for u in range(len(UNITS) + 3):
                if u < len(UNITS):
                    exponentials(u)
                if 2 <= u < len(UNITS) + 2:
                    transposed(u - 2)
                if u >= 3 and (u - 3) % 4 == 3:
                    head_out((u - 3) // 4)
            for i in range(2):
                act.wait_ge(S("o_done"), HEADS)
                nc.scalar.activation(sq[:, i, :], hn[:, i, :], ACT.Square).then_inc(S("qk_sq"), 1)
            for i in range(2):
                act.wait_ge(S("qk_sum"), N_QK + i + 1)
                root(inv[:, i, :], banks[i]).then_inc(S("qk_root"), 1)

            squares("n2", lambda k: (S("h_done"), k + 1))
            nc.scalar.activation(C_ACT, col("c", 0, KD), ACT.Silu).then_inc(S("c_act"), 1)

            def gate(p):
                act.wait_ge(S("taps"), 2 * (2 * p) + 2)
                if p >= 2:
                    act.wait_ge(S("hid_done"), p - 1)
                nc.scalar.activation(ffn["sg"][:, p % 2, :], ffn["cv"][:, 2 * (p % 3), :], ACT.Silu)\
                  .then_inc(S("sg_done"), 1)

            for p in range(FT):
                for part in range(2):
                    i = 2 * p + part
                    act.wait_ge(S("product"), PRODUCTS["up"] + i + 1)
                    if p >= 3:
                        act.wait_ge(S("hid_done"), p - 2)
                    ch = FT * part + p
                    nc.scalar.activation(ffn["cv"][:, i % 6, :], banks[i % 6][:, :], ACT.Identity,
                                         scale=col("conv_w", 2 * 2 * FT + ch), bias=col("conv_b", ch))\
                      .then_inc(S("tap2"), 1)
                if p >= 1:
                    gate(p - 1)
            gate(FT - 1)

            squares("n3", lambda k: (S("h_done"), KD + k + 1))
            for t in range(KD):
                act.wait_ge(S("product"), PRODUCTS["ple"] + 2 * t + 1)
                if t >= 2:
                    act.wait_ge(S("ple_mul"), t - 1)
                nc.scalar.activation(ple["gt"][:, t % 2, :], banks[2 * (t % 3)][:, :], ACT.Sigmoid)\
                  .then_inc(S("gt_done"), 1)
            squares("n4", lambda k: (S("h_done"), 2 * KD + k + 1))
            shifted("n4", 0)

            nc.scalar.activation(EXP_A, col("A_log")[0:SH, :], ACT.Exp).then_inc(S("expA"), 1)
            act.wait_ge(S("product"), PRODUCTS["x"] + 1)
            nc.scalar.activation(pool["raw"][0:SH, :], banks[0][0:SH, :], ACT.Identity,
                                 bias=col("dt_bias")[0:SH, :]).then_inc(S("x_copied"), 1)
            act.wait_ge(S("x_copied"), 1)
            nc.scalar.activation(pool["ab"][0:SH, :], pool["raw"][0:SH, :], ACT.Abs).then_inc(S("act_step"), 1)
            act.wait_ge(S("act_step"), 3)
            nc.scalar.activation(pool["l"][0:SH, :], pool["ab"][0:SH, :], ACT.Exp, scale=-1.0)\
              .then_inc(S("act_step"), 1)
            act.wait_ge(S("act_step"), 4)
            nc.scalar.activation(pool["ab"][0:SH, :], pool["l"][0:SH, :], ACT.Ln, bias=1.0)\
              .then_inc(S("dt_ln"), 1)
            act.wait_ge(S("pads"), 2)
            for i in range(1, 9):
                act.wait_ge(S("product"), PRODUCTS["x"] + i + 1)
                if i >= 3:
                    act.wait_ge(S("pooled"), i - 2)
                nc.scalar.activation(pool["x"][:, (i - 1) % 2, PAD:PAD + T], banks[i % 6][:, :], ACT.Copy)\
                  .then_inc(S("x_copied"), 1)
            act.wait_ge(S("dec_arg"), TT)
            nc.scalar.activation(dtk["dtp"][2 * SH:3 * SH, :], pool["a"][0:SH, :], ACT.Exp, scale=-1.0)\
              .then_inc(S("dtp_done"), 1)
            act.wait_ge(S("tok_ready"), 1)
            nc.scalar.activation(dtk["tok"], banks[6][:, 0:TT * 96].rearrange("p (c n) -> p c n", n=96),
                                 ACT.Copy).then_inc(S("tok_done"), 1)
            for t in range(KD):
                act.wait_ge(S("product"), PRODUCTS["pool"] + t + 1)
                act.wait_ge(S("product"), PRODUCTS["pool"] + 2 * (t // 2) + 2)
                nc.scalar.activation(mix["pooled"][:, t, :], banks[t % 6][:, :], ACT.Copy,
                                     scale=col("pool_scale", t)).then_inc(S("pool_out"), 1)

            waiting = []

            def xbc_silu():
                i, buf = waiting.pop(0)
                q = 4 * (i // 6) + i % 6 - 2
                act.wait_ge(*s_freed(i))
                if q >= 2:
                    act.wait_ge(S("xbc_done"), q - 1)
                nc.scalar.activation(ssd["th"][:, q % 2, :], buf, ACT.Tanh).then_inc(S("th_done"), 1)

            def read_tile(i):
                g, j = divmod(i, 6)
                s = g % 2
                act.wait_ge(S("product"), PRODUCTS["ssd"] + i + 1)
                if g >= 2:
                    act.wait_ge(S("y_gated"), 2 * (g - 1))
                if j < 2:
                    nc.scalar.activation(ssd["zs"][:, 2 * s + j, :], banks[i % 2][:, :], ACT.Tanh,
                                         scale=0.5).then_inc(S("z_tanh"), 1)
                    return
                ch = {2: 2 * g, 3: 2 * g + 1, 4: 16 + g, 5: 24 + g}[j]
                buf = {2: ssd["xs"][:, 2 * s, :], 3: ssd["xs"][:, 2 * s + 1, :], 4: ssd["B"][:, s, :],
                       5: ssd["C"][:, s, :]}[j]
                nc.scalar.activation(buf, banks[i % 2][:, :], ACT.Identity, scale=col("conv_w2", 3 * 32 + ch),
                                     bias=col("conv_b2", ch)).then_inc(S("s_tap3"), 1)
                if waiting:
                    xbc_silu()
                waiting.append((i, buf))

            act.wait_ge(S("prepared"), PREPARED["halved"] + 1)
            for i in range(6):
                read_tile(i)
            xbc_silu()
            for g in range(SG):
                for c in range(TT):
                    n = TT * g + c
                    act.wait_ge(S("tr2_ready"), n + 1)
                    if n >= 2:
                        act.wait_ge(S("st_ready"), 3 * ((n - 2) // TT) + min((n - 2) % TT + 1, TT - 1))
                        act.wait_ge(S("xdec_done"), n - 1)
                    nc.scalar.activation(ssd["xtok"][:, n % 2, :], banks[2][:, 0:3 * P], ACT.Copy)\
                      .then_inc(S("xtok_done"), 1)
                    act.wait_ge(S("cum_ready"), n + 1)
                    if n >= 2:
                        act.wait_ge(S("CE_done"), n - 1)
                        act.wait_ge(S("state_done"), 3 * ((n - 2) // TT) + min((n - 2) % TT + 1, TT - 1))
                    nc.scalar.activation(ssd["Ex"][:, n % 2, :], banks[4][:, :], ACT.Exp).then_inc(S("Ex_done"), 1)
                    act.wait_ge(S("L0_done"), HPG * (n + 1))
                    nc.scalar.activation(ssd["L"][:, n % 2, :], ssd["L"][:, n % 2, :], ACT.Exp)\
                      .then_inc(S("L_done"), 1)
                    if g + 1 < SG:
                        for i in FILL[c]:
                            read_tile(6 * (g + 1) + i)
                        if c == TT - 1:
                            xbc_silu()

            for g in range(SG):
                for i in range(2):
                    act.wait_ge(S("y_gated"), 2 * g + i + 1)
                    if g >= 2:
                        act.wait_ge(S("y_sum"), g - 1)
                    nc.scalar.activation(sq[:, 2 * (g % 2) + i, :], mix["yn"][:, 2 * g + i, :], ACT.Square)\
                      .then_inc(S("y_sq"), 1)
                for t in (2 * g, 2 * g + 1):
                    act.wait_ge(S("product"), PRODUCTS["gates"] + t + 1)
                    act.wait_ge(S("y_gated"), 2 * SG)
                    nc.scalar.activation(late["gs"][:, t, :], banks[t % 7][:, :], ACT.Copy)\
                      .then_inc(S("gs_copied"), 1)
                act.wait_ge(S("y_sum"), g + 1)
                if g >= 2:
                    act.wait_ge(S("yn_done"), 2 * (g - 1))
                root(inv[:, g % 2, :], banks[7]).then_inc(S("y_root"), 1)
            for t in range(16):
                act.wait_ge(S("gs_copied"), t + 1)
                nc.scalar.activation(late["gs"][:, t, :], late["gs"][:, t, :], ACT.Sigmoid).then_inc(S("gs_done"), 1)
            squares("n5", lambda k: (S("h_done"), 3 * KD + k + 1))
            shifted("n5", 3 * KD)

            for tt in range(TT):
                act.wait_ge(S("product"), PRODUCTS["router"] + TT)
                nc.scalar.activation(moe["sc"][:, tt, :], banks[tt][:, 0:E], ACT.Sigmoid).then_inc(S("sc_done"), 1)

            for tt in range(TT):
                for half in range(2):
                    act.wait_ge(S("ut_ready"), 2 * tt + half + 1)
                    nc.scalar.activation(moe["ut"][:, tt, 512 * half:512 * half + 512],
                                         banks[4 + (2 * tt + half) % 4][:, :], ACT.Copy).then_inc(S("ut_done"), 1)
                act.wait_ge(S("ut_done"), 2 * tt + 2)
                act.dma_start(u_rows[tt * P:(tt + 1) * P, :], moe["ut"][:, tt, :]).then_inc(S("u_stored"), 16)

            def shared_gate(tt):
                act.wait_ge(S("sh_gu"), tt + 1)
                if tt >= 2:
                    act.wait_ge(S("sh_hid"), tt - 1)
                nc.scalar.activation(moe["ssg"][:, tt % 2, :], banks[tt % 2][:, 0:FE], ACT.Silu).then_inc(S("sh_sg"), 1)
                nc.scalar.activation(moe["sup"][:, tt % 2, :], banks[tt % 2][:, FE:2 * FE], ACT.Copy)\
                  .then_inc(S("sh_up"), 1)

            def shared_hidden(tt):
                act.wait_ge(S("sh_ht"), tt + 1)
                if tt >= 2:
                    act.wait_ge(S("sh_y"), 2 * (tt - 1))
                nc.scalar.activation(moe["shT"][:, tt % 2, :], banks[2][:, 0:2 * P], ACT.Copy).then_inc(S("sh_hT"), 1)

            def shared_out(tt):
                if tt >= 2:
                    act.wait_ge(S(f"shared_stored{tt % 2}"), 16)
                for half in range(2):
                    act.wait_ge(S("sh_y"), 2 * tt + half + 1)
                    nc.scalar.activation(moe["sy"][:, tt % 2, 512 * half:512 * half + 512],
                                         banks[4 + (2 * tt + half) % 4][:, :], ACT.Copy).then_inc(S("y_copied"), 1)
                act.wait_ge(S("y_copied"), 2 * tt + 2)
                act.dma_start(y_rows[tt * P:(tt + 1) * P, :], moe["sy"][:, tt % 2, :])\
                   .then_inc(S(f"shared_stored{tt % 2}"), 16)

            shared_gate(0)
            shared_gate(1)
            shared_hidden(0)
            shared_gate(2)
            shared_out(0)
            shared_hidden(1)
            shared_gate(3)
            shared_out(1)
            for tt in (2, 3):
                shared_hidden(tt)
                shared_out(tt)

            def block_rows(b, p):
                for half in range(2):
                    act.wait_ge(S("moe_tr"), b * 2 + (half + 1))
                    nc.scalar.activation(moe["xT"][:, p, 512 * half:512 * half + 512], banks[half][:, :], ACT.Copy)\
                      .then_inc(S("xT_done"), 1)

            def block_gate(b, p):
                act.wait_ge(S("moe_gu"), b + 1)
                nc.scalar.activation(moe["sg"][:, p, :], banks[2 + p][:, 0:FE], ACT.Silu).then_inc(S("moe_sg"), 1)

            act.wait_ge(S("blocks_known"), 2)
            pairs_but_one = act.value_load(expert_of[0:1, MAX_BLOCKS:MAX_BLOCKS + 1], min_val=TT * TOP // 2 - 1,
                                            max_val=MAX_BLOCKS // 2 - 1)
            pairs = pairs_but_one + 1
            block_rows(0, 0)
            block_rows(1, 1)
            block_gate(0, 0)
            with act.Fori(1, pairs) as i:
                for b, p in ((i * 2 + (-1), 1), (i * 2, 0)):
                    block_rows(b + 1, 1 - p)
                    block_gate(b, p)
            block_gate(pairs_but_one * 2 + 1, 1)
            squares("n6", lambda k: (S("h_done"), 4 * KD + k + 1))

        @block.vector
        def _(dve):
            steps = 0

            def counted_step(ins):
                nonlocal steps
                steps += 1
                ins.then_inc(S("vector_step"), 1)

            def steps_done():
                dve.wait_ge(S("vector_step"), steps)

            def step(ins):
                counted_step(ins)
                steps_done()

            def apply_norm(name, gain, done):
                dve.wait_ge(S("norm_root"), NORMS[name] + 1)
                nc.vector.reciprocal(inv[:, 0, :], inv[:, 0, :]).then_inc(S("norm_inv"), 1)
                dve.wait_ge(S("norm_inv"), NORMS[name] + 1)
                for k in range(KD):
                    nc.vector.scalar_tensor_tensor(hn[:, k, :], h[:, k, :], gain(k), inv[:, 0, :], ALU.mult,
                                                   ALU.mult).then_inc(S("norm_" + done), 1)

            dve.wait_ge(S("cols_in"), 16)
            nc.vector.tensor_scalar(col("conv_w2", 0, 5 * 32), col("conv_w2", 0, 5 * 32), 0.5, None, ALU.mult)\
              .then_inc(S("prepared"), 1)
            for i in range(2):
                nc.vector.tensor_tensor_reduce(out=inv[:, 1, 64 * i:64 * i + 64], in0=col("lam", 128 * i, 64),
                                               in1=col("lam", 128 * i + 64, 64), scale=1.0, scalar=0.0,
                                               op0=ALU.mult, op1=ALU.add, accum_out=LAM_DOT[:, i:i + 1])\
                  .then_inc(S("prepared"), 1)
            nc.vector.tensor_scalar(SUBLN, col("subln"), 1.0 - LAM_INIT, None, ALU.mult).then_inc(S("prepared"), 1)
            apply_norm("n1", lambda k: col("ln_mix", k), "out")
            dve.wait_ge(S("lam_exp"), 1)
            nc.vector.tensor_scalar(NEG_LAM, LAM_EXP[:, 1:2], LAM_EXP[:, 0:1], LAM_INIT, ALU.subtract,
                                    ALU.subtract).then_inc(S("prepared"), 1)
            dve.wait_ge(S("shp_in"), 16)
            for i in range(N_DIFF):
                nc.vector.tensor_scalar(att["tab_diff"][:, i, :], const("dist"), 8.0 * 2.0 ** (-2.0 * (i + 1)), None,
                                        ALU.mult).then_inc(S("prepared"), 1)
            dve.wait_ge(S("rel_in"), 16 * N_CHUNK)
            for f in range(N_CHUNK):
                tab = att["tab_chunk"][:, f, :]
                nc.vector.scalar_tensor_tensor(tab, tab, 8.0, const("chunked"), ALU.mult, ALU.add)\
                  .then_inc(S("prepared"), 1)
            j = 0
            for t, (kind, *_) in enumerate(Z_GROUPS):
                if kind == "qk":
                    dve.wait_ge(S("qk_root"), j + 1)
                    nc.vector.reciprocal(inv[:, j % 2, :], inv[:, j % 2, :]).then_inc(S("qk_inv"), 1)
                    dve.wait_ge(S("qk_inv"), j + 1)
                    nc.vector.scalar_tensor_tensor(att["qk"][:, j, :], banks[t % 6][:, :],
                                                   col("qk_gain", QK_GAIN[j]), inv[:, j % 2, :], ALU.mult,
                                                   ALU.mult).then_inc(S("qk_done"), 1)
                    j += 1
                if kind == "fg":
                    dve.wait_ge(S("fg_ln"), 1)
                    step(nc.vector.scalar_tensor_tensor(fgt["lf"][0:N_FOX, :], fgt["x"][0:N_FOX, :], 0.0,
                                                        fgt["l"][0:N_FOX, :], ALU.min, ALU.subtract))
                    step(nc.vector.tensor_tensor_scan(fgt["F"][0:N_FOX, :],
                                                      ones[0:N_FOX, 0:1].to_broadcast([N_FOX, T]),
                                                      fgt["lf"][0:N_FOX, :], 0.0, ALU.mult, ALU.add))
                    nc.vector.tensor_scalar(att["F8"][0:N_FOX, :], fgt["F"][0:N_FOX, :], -8.0, None, ALU.mult)\
                      .then_inc(S("F_done"), 1)

            dve.wait_ge(S("prepared"), PREPARED["tables"] + N_DIFF + N_CHUNK)

            def logits(u):
                hh, qt, first, n = UNITS[u]
                W = P * (qt + 1)
                for m in range(first, first + n):
                    dve.wait_ge(S("s_scores"), m + 1)
                    if m >= 4:
                        dve.wait_ge(S("probs_done"), UNIT_OF[m - 4] + 1)
                    nc.vector.tensor_tensor_reduce(out=att["t"][:, m % 4, 0:W], in0=banks[m % 4][:, 0:W],
                                                   in1=table(hh, qt), scale=-0.125, scalar=3.0e38, op0=ALU.add,
                                                   op1=ALU.min, accum_out=NEG_MAX[:, m:m + 1])\
                      .then_inc(S("t_done"), 1)

            def probabilities(u):
                hh, qt, m, n = UNITS[u]
                W = P * (qt + 1)
                r = RECIP[:, 2 * (u % 2):2 * (u % 2) + n]
                out = NORMED[:, u % 2, 0:W]
                dve.wait_ge(S("e_done"), m + n)
                step(nc.vector.reciprocal(r, ROW_SUM[:, m:m + n]))
                if u >= 2:
                    dve.wait_ge(S("tr_ready"), u - 1)
                if n == 1:
                    nc.vector.tensor_scalar(out, att["t"][:, m % 4, 0:W], r, None, ALU.mult)\
                      .then_inc(S("probs_done"), 1)
                    return
                step(nc.vector.tensor_scalar(r[:, 1:2], r[:, 1:2], NEG_LAM, None, ALU.mult))
                step(nc.vector.tensor_scalar(out, att["t"][:, m % 4, 0:W], r[:, 0:1], None, ALU.mult))
                nc.vector.scalar_tensor_tensor(out, att["t"][:, (m + 1) % 4, 0:W], r[:, 1:2], out, ALU.mult,
                                               ALU.add).then_inc(S("probs_done"), 1)

            dve.wait_ge(S("prepared"), PREPARED["neg_lam"] + 1)
            for u in range(len(UNITS) + 1):
                if u < len(UNITS):
                    logits(u)
                if u >= 1:
                    probabilities(u - 1)
            dve.wait_ge(S("prepared"), PREPARED["subln"] + 1)
            for i in range(2):
                dve.wait_ge(S("qk_root"), N_QK + i + 1)
                nc.vector.reciprocal(inv[:, i, :], inv[:, i, :]).then_inc(S("qk_inv"), 1)
                dve.wait_ge(S("qk_inv"), N_QK + i + 1)
                nc.vector.scalar_tensor_tensor(hn[:, i, :], hn[:, i, :], SUBLN, inv[:, i, :], ALU.mult, ALU.mult)\
                  .then_inc(S("qk_done"), 1)
            for t in range(KD):
                dve.wait_ge(S("product"), PRODUCTS["wo"] + t + 1)
                nc.vector.tensor_tensor(h[:, t, :], h[:, t, :], banks[t % 7][:, :], ALU.add).then_inc(S("h_done"), 1)
            apply_norm("n2", lambda k: col("ln_ffn", k), "out")

            for i in range(2 * FT):
                p, part = divmod(i, 2)
                ch = FT * part + p
                cv, u = ffn["cv"][:, i % 6, :], banks[i % 6]
                dve.wait_ge(S("tap2"), i + 1)
                for back in (1, 2):
                    nc.vector.scalar_tensor_tensor(cv[:, back:T], u[:, 0:T - back],
                                                   col("conv_w", (2 - back) * 2 * FT + ch), cv[:, back:T],
                                                   ALU.mult, ALU.add).then_inc(S("taps"), 1)
                    dve.wait_ge(S("taps"), 2 * i + back)
                if part == 1:
                    dve.wait_ge(S("sg_done"), p + 1)
                    nc.vector.tensor_tensor(ffn["hid"][:, p, :], ffn["sg"][:, p % 2, :], cv, ALU.mult)\
                      .then_inc(S("hid_done"), 1)

            dve.wait_ge(S("c_act"), 1)
            for n in range(6):
                for m in (2 * n, 2 * n + 1):
                    panel_here(dve, ada_panels[m])
                    w = slot(ada_panels[m], 512)
                    out = ffn["ada"][:, m, :]
                    for k in range(KD):
                        if k == 0:
                            ins = nc.vector.tensor_scalar(out, w[:, k, :], C_ACT[:, 0:1], None, ALU.mult)
                        else:
                            ins = nc.vector.scalar_tensor_tensor(out, w[:, k, :], C_ACT[:, k:k + 1], out,
                                                                 ALU.mult, ALU.add)
                        ins.then_inc(S("ada_sum"), 1)
                        dve.wait_ge(S("ada_sum"), KD * m + k + 1)
                if n in (2, 5):
                    half = n // 3
                    dve.wait_ge(S("product"), PRODUCTS["down"] + 3 * half + 3)
                    for t in range(4 * half, 4 * half + 4):
                        nc.vector.tensor_tensor(h[:, t, :], h[:, t, :], banks[t % 7][:, :], ALU.add)\
                          .then_inc(S("h_done"), 1)
            apply_norm("n3", lambda k: col("ln_ple", k), "out")
            dve.wait_ge(S("ada_ready"), 1)
            nc.vector.tensor_tensor(mod[:, :], banks[6][:, 0:N_ADA * KD], col("b_ada", 0, N_ADA * KD), ALU.add)\
              .then_inc(S("mod_done"), 1)

            for t in range(KD):
                dve.wait_ge(S("gt_done"), t + 1)
                dve.wait_ge(S("product"), PRODUCTS["ple"] + 2 * t + 2)
                nc.vector.tensor_tensor(ple["tmp"][:, t % 2, :], ple["gt"][:, t % 2, :], banks[2 * (t % 3) + 1][:, :],
                                        ALU.mult).then_inc(S("ple_mul"), 1)
                dve.wait_ge(S("ple_mul"), t + 1)
                nc.vector.tensor_tensor(h[:, t, :], h[:, t, :], ple["tmp"][:, t % 2, :], ALU.add)\
                  .then_inc(S("h_done"), 1)

            def modulated(name, gain, first):
                dve.wait_ge(S("mod_done"), 1)
                nc.vector.scalar_tensor_tensor(GAIN1, mod[:, first:first + KD], 1.0, gain, ALU.add, ALU.mult)\
                  .then_inc(S("norm_gain"), 1)
                dve.wait_ge(S("norm_gain"), NORMS[name] - NORMS["n4"] + 1)
                apply_norm(name, lambda k: GAIN1[:, k:k + 1], "mul")

            modulated("n4", col("norm_mix", 0, KD), KD)

            dve.wait_ge(S("dt_ln"), 1)
            dve.wait_ge(S("expA"), 1)
            dt, sums = dtk["dtp"][0:SH, :], pool["acs"][0:SH, :]
            step(nc.vector.scalar_tensor_tensor(dt, pool["raw"][0:SH, :], 0.0, pool["ab"][0:SH, :], ALU.max, ALU.add))
            step(nc.vector.tensor_scalar(pool["a"][0:SH, :], dt, EXP_A, -1.0, ALU.mult, ALU.mult))
            for c in range(TT):
                now = slice(c * P, (c + 1) * P)
                counted_step(nc.vector.tensor_tensor_scan(sums[:, now], ones[0:SH, :], pool["a"][0:SH, now], 0.0,
                                                          ALU.mult, ALU.add))
            steps_done()
            for c in range(TT):
                now = slice(c * P, (c + 1) * P)
                nc.vector.tensor_scalar(pool["a"][0:SH, now], sums[:, now], sums[:, (c + 1) * P - 1:(c + 1) * P],
                                        None, ALU.subtract).then_inc(S("dec_arg"), 1)
            nc.vector.tensor_copy(dtk["dtp"][SH:2 * SH, :], sums).then_inc(S("dtp_sums"), 1)

            dve.wait_ge(S("pads"), 2)
            for i in range(KD):
                gi = i // 2
                w = WINDOWS[gi]
                x = pool["x"][:, i % 2, :]
                dve.wait_ge(S("x_copied"), i + 2)
                cur, back, a = x, 1, 0
                while back < w:
                    nxt = pool["s"][:, 2 * (i % 2) + a, :]
                    step(nc.vector.tensor_tensor(nxt[:, PAD:PAD + T], cur[:, PAD:PAD + T],
                                                 cur[:, PAD - back:PAD + T - back], ALU.add))
                    cur, back, a = nxt, 2 * back, 1 - a
                counted_step(nc.vector.tensor_tensor(pool["head"][:, i % 2, :], cur[:, PAD:2 * PAD],
                                                     const("inv_count")[:, PAD * gi:PAD * gi + PAD], ALU.mult))
                counted_step(nc.vector.scalar_tensor_tensor(mix["pooled"][:, i, PAD:T], cur[:, 2 * PAD:PAD + T],
                                                            1.0 / w, x[:, 2 * PAD:PAD + T], ALU.mult, ALU.subtract))
                steps_done()
                nc.vector.tensor_tensor(mix["pooled"][:, i, 0:PAD], pool["head"][:, i % 2, :], x[:, PAD:2 * PAD],
                                        ALU.subtract).then_inc(S("pooled"), 1)

            taps = 0
            waiting = []

            def xbc_silu():
                q, buf = waiting.pop(0)
                dve.wait_ge(S("th_done"), q + 1)
                nc.vector.scalar_tensor_tensor(buf, ssd["th"][:, q % 2, :], 1.0, buf, ALU.add, ALU.mult)\
                  .then_inc(S("xbc_done"), 1)

            def read_tile(i):
                nonlocal taps
                g, j = divmod(i, 6)
                s = g % 2
                if j < 2:
                    zs = ssd["zs"][:, 2 * s + j, :]
                    dve.wait_ge(S("z_tanh"), 2 * g + j + 1)
                    nc.vector.scalar_tensor_tensor(zs, zs, 1.0, banks[i % 2][:, :], ALU.add, ALU.mult)\
                      .then_inc(S("z_read"), 1)
                    return
                ch = {2: 2 * g, 3: 2 * g + 1, 4: 16 + g, 5: 24 + g}[j]
                buf = {2: ssd["xs"][:, 2 * s, :], 3: ssd["xs"][:, 2 * s + 1, :], 4: ssd["B"][:, s, :],
                       5: ssd["C"][:, s, :]}[j]
                dve.wait_ge(S("s_tap3"), 4 * g + j - 1)
                for back in (1, 2, 3):
                    nc.vector.scalar_tensor_tensor(buf[:, back:T], banks[i % 2][:, 0:T - back],
                                                   col("conv_w2", (3 - back) * 32 + ch), buf[:, back:T], ALU.mult,
                                                   ALU.add).then_inc(S("s_taps"), 1)
                    taps += 1
                    dve.wait_ge(S("s_taps"), taps)
                if waiting:
                    xbc_silu()
                waiting.append((4 * g + j - 2, buf))

            def heads(ap, width):
                return ap.rearrange("p (h n) -> p h n", n=width)

            dve.wait_ge(S("tok_done"), 1)
            for i in range(6):
                read_tile(i)
            xbc_silu()
            for g in range(SG):
                s = g % 2
                for c in range(TT):
                    n = TT * g + c
                    b = n % 2
                    now = slice(c * P, (c + 1) * P)
                    per_head = lambda first: dtk["tok"][:, c, first + HPG * g:first + HPG * g + HPG]\
                        .unsqueeze(2).to_broadcast([P, HPG, HD])
                    dve.wait_ge(S("xtok_done"), n + 1)
                    if n >= 2:
                        dve.wait_ge(S("y_ready"), n - 1)
                    nc.vector.tensor_tensor(heads(ssd["xdt"][:, b, :], HD), heads(ssd["xtok"][:, b, 0:2 * P], HD),
                                            per_head(0), ALU.mult).then_inc(S("xdt_done"), 1)
                    dve.wait_ge(S("xdt_done"), n + 1)
                    if n >= 2:
                        dve.wait_ge(S("st_ready"), 3 * ((n - 2) // TT) + min((n - 2) % TT + 1, TT - 1))
                    nc.vector.tensor_tensor(heads(ssd["xdec"][:, b, :], HD), heads(ssd["xdt"][:, b, :], HD),
                                            per_head(2 * SH), ALU.mult).then_inc(S("xdec_done"), 1)
                    dve.wait_ge(S("CB_ready"), n + 1)
                    nc.vector.tensor_tensor(ssd["CB"][:, b, :], banks[3][:, 0:P], tri, ALU.mult)\
                      .then_inc(S("CB_done"), 1)
                    dve.wait_ge(S("Ex_done"), n + 1)
                    for j in range(HPG):
                        a = SH + HPG * g + j
                        nc.vector.tensor_scalar(ssd["L"][:, b, j * P:(j + 1) * P], banks[4][:, j * P:(j + 1) * P],
                                                dtk["tok"][:, c, a:a + 1], 0.0, ALU.subtract, ALU.min)\
                          .then_inc(S("L0_done"), 1)
                    nc.vector.tensor_tensor(heads(ssd["CE"][:, b, :], P), heads(ssd["Ex"][:, b, :], P),
                                            ssd["C"][:, s, now].unsqueeze(1).to_broadcast([P, HPG, P]), ALU.mult)\
                      .then_inc(S("CE_done"), 1)
                    dve.wait_ge(S("L_done"), n + 1)
                    dve.wait_ge(S("CB_done"), n + 1)
                    nc.vector.tensor_tensor(heads(ssd["L"][:, b, :], P), heads(ssd["L"][:, b, :], P),
                                            ssd["CB"][:, b, :].unsqueeze(1).to_broadcast([P, HPG, P]), ALU.mult)\
                      .then_inc(S("M_done"), 1)
                    if g + 1 < SG:
                        for i in FILL[c]:
                            read_tile(6 * (g + 1) + i)
                        if c == TT - 1:
                            xbc_silu()
                    if c < TT - 1:
                        k = 3 * g + c
                        if c > 0:
                            dve.wait_ge(S("state_done"), k)
                            nc.vector.tensor_tensor(heads(ssd["carry"], HD), heads(ssd["state"], HD),
                                                    heads(ssd["Ex"][:, b, :], P)[:, :, P - 1:P]
                                                    .to_broadcast([P, HPG, HD]), ALU.mult)\
                              .then_inc(S("carried"), 1)
                            dve.wait_ge(S("carried"), 2 * g + c)
                        dve.wait_ge(S("st_ready"), k + 1)
                        if c > 0:
                            ins = nc.vector.tensor_tensor(ssd["state"], ssd["carry"], banks[7][:, 0:HPG * HD], ALU.add)
                        else:
                            ins = nc.vector.tensor_copy(ssd["state"], banks[7][:, 0:HPG * HD])
                        ins.then_inc(S("state_done"), 1)
                dve.wait_ge(S("y_ready"), TT * (g + 1))
                for i in range(2):
                    y = mix["yn"][:, 2 * g + i, :]
                    nc.vector.scalar_tensor_tensor(y, ssd["xs"][:, 2 * s + i, :], col("D_skip", 2 * g + i),
                                                   banks[5 + i][:, :], ALU.mult, ALU.add).then_inc(S("y_read"), 1)
                dve.wait_ge(S("y_read"), 2 * g + 2)
                for i in range(2):
                    y = mix["yn"][:, 2 * g + i, :]
                    nc.vector.scalar_tensor_tensor(y, y, 0.5, ssd["zs"][:, 2 * s + i, :], ALU.mult, ALU.mult)\
                      .then_inc(S("y_gated"), 1)
            for g in range(SG):
                dve.wait_ge(S("y_root"), g + 1)
                nc.vector.reciprocal(inv[:, g % 2, :], inv[:, g % 2, :]).then_inc(S("y_inv"), 1)
                dve.wait_ge(S("y_inv"), g + 1)
                for i in range(2):
                    y = mix["yn"][:, 2 * g + i, :]
                    nc.vector.scalar_tensor_tensor(y, y, col("ssd_norm", 2 * g + i), inv[:, g % 2, :], ALU.mult,
                                                   ALU.mult).then_inc(S("yn_done"), 1)

            for t in range(KD):
                dve.wait_ge(S("product"), PRODUCTS["ssd_out"] + 2 * (t // 4) + 2)
                dve.wait_ge(S("gs_done"), t + 1)
                nc.vector.tensor_tensor(hn[:, t, :], banks[t][:, :], late["gs"][:, t, :], ALU.mult)\
                  .then_inc(S("mixed"), 1)
            for t in range(KD):
                dve.wait_ge(S("product"), PRODUCTS["pool_out"] + t + 1)
                dve.wait_ge(S("gs_done"), KD + t + 1)
                nc.vector.tensor_tensor(late["tmp"][:, t % 2, :], banks[t][:, :], late["gs"][:, KD + t, :], ALU.mult)\
                  .then_inc(S("mixed"), 1)
                dve.wait_ge(S("mixed"), KD + 2 * t + 1)
                nc.vector.tensor_tensor(hn[:, t, :], hn[:, t, :], late["tmp"][:, t % 2, :], ALU.add)\
                  .then_inc(S("mixed"), 1)
            for t in range(KD):
                dve.wait_ge(S("product"), PRODUCTS["wo2"] + t + 1)
                nc.vector.scalar_tensor_tensor(h[:, t, :], banks[t % 7][:, :], mod[:, 2 * KD + t:2 * KD + t + 1],
                                               h[:, t, :], ALU.mult, ALU.add).then_inc(S("h_done"), 1)
            modulated("n5", col("norm_ffn", 0, KD), 4 * KD)

            iota = const("iota")
            dve.wait_ge(S("sc_done"), TT)
            for tt in range(TT):
                sc, ch, mk = moe["sc"][:, tt, :], moe["ch"][:, tt, :], moe["mk"][:, tt, :]
                best, gsum, gtop = moe["best"][:, tt, :], moe["gsum"][:, tt, :], moe["gtop"][:, tt, :]
                gm, gneg, top, gf = moe["gm"][:, tt, :], moe["gneg"][:, tt, :], moe["top"][:, tt, :], moe["gf"][:, tt, :]
                ef, sel, wk, wsum = moe["ef"][:, tt, :], moe["sel"][:, tt, :], moe["wk"][:, tt, :], moe["wsum"][:, tt:tt + 1]
                gix_t, eix_t = gix[:, tt * EG:(tt + 1) * EG], eix[:, tt * TOP:(tt + 1) * TOP]
                groups = lambda ap: ap.rearrange("p (g e) -> p g e", e=E // EG)
                over = lambda ap: ap.unsqueeze(2).to_broadcast([P, EG, E // EG])
                step(nc.vector.tensor_tensor(ch, sc, col("router_bias", 0, E), ALU.add))
                for g in range(EG):
                    counted_step(nc.vector.max(best[:, 8 * g:8 * g + 8], ch[:, 8 * g:8 * g + 8]))
                steps_done()
                step(nc.vector.tensor_tensor(gsum, groups(best)[:, :, 0], groups(best)[:, :, 1], ALU.add))
                step(nc.vector.max(gtop, gsum))
                step(nc.vector.max_index(gix_t, gtop, gsum))
                step(nc.vector.tensor_copy(gf, gix_t))
                step(nc.vector.tensor_scalar(gm, iota[:, 0:EG], gf[:, 0:1], None, ALU.is_equal))
                for g in range(1, 4):
                    step(nc.vector.scalar_tensor_tensor(gm, iota[:, 0:EG], gf[:, g:g + 1], gm, ALU.is_equal, ALU.add))
                step(nc.vector.tensor_scalar(gneg, gm, -1.0, 1e30, ALU.add, ALU.mult))
                step(nc.vector.tensor_tensor(groups(mk), groups(ch), over(gm), ALU.mult))
                step(nc.vector.tensor_tensor(groups(mk), groups(mk), over(gneg), ALU.add))
                step(nc.vector.max(top, mk))
                step(nc.vector.max_index(eix_t, top, mk))
                step(nc.vector.tensor_copy(ef, eix_t))
                step(nc.vector.tensor_scalar(sel, iota[:, 0:E], ef[:, 0:1], None, ALU.is_equal))
                for k in range(1, TOP):
                    ins = nc.vector.scalar_tensor_tensor(sel, iota[:, 0:E], ef[:, k:k + 1], sel, ALU.is_equal, ALU.add)
                    if k < TOP - 1:
                        step(ins)
                ins.then_inc(S("selected"), 1)
                for k in range(TOP):
                    step(nc.vector.scalar_tensor_tensor(moe["junk"], iota[:, 0:E], ef[:, k:k + 1], sc, ALU.is_equal,
                                                        ALU.mult, accum_out=wk[:, k:k + 1]))
                step(nc.vector.tensor_reduce(wsum, wk, AX.X, ALU.add))
                step(nc.vector.reciprocal(wsum, wsum))
                step(nc.vector.tensor_scalar(wk, wk, wsum, ROUTED_SCALE, ALU.mult, ALU.mult))

            dve.wait_ge(S("counted"), 1)
            count = banks[3][:, TT * E:(TT + 1) * E]
            step(nc.vector.tensor_scalar(moe["nb"], count, 0.0, None, ALU.is_gt))
            for j in range(1, T // P):
                step(nc.vector.scalar_tensor_tensor(moe["nb"], count, float(P * j), moe["nb"], ALU.is_gt, ALU.add))
            step(nc.vector.tensor_tensor_scan(moe["bend"], ones[:, 0:E], moe["nb"], 0.0, ALU.mult, ALU.add))
            step(nc.vector.tensor_tensor(moe["bstart"], moe["bend"], moe["nb"], ALU.subtract))
            for tt in range(TT):
                step(nc.vector.scalar_tensor_tensor(moe["start"][:, tt, :], moe["bstart"], float(P),
                                                    banks[3][:, tt * E:(tt + 1) * E], ALU.mult, ALU.add))
            nc.vector.tensor_scalar(moe["junk"], moe["bend"], const("row"), None, ALU.is_le, ALU.add,
                                    accum_out=moe["ebcol"][:, 0:1]).then_inc(S("ebcol_done"), 1)
            dve.wait_ge(S("ebcol_done"), 1)
            for tt in range(TT):
                for k in range(TOP):
                    n = tt * TOP + k
                    step(nc.vector.scalar_tensor_tensor(moe["junk"], iota[:, 0:E], moe["ef"][:, tt, k:k + 1],
                                                        moe["start"][:, tt, :], ALU.is_equal, ALU.mult,
                                                        accum_out=moe["place"][:, n:n + 1]))
            step(nc.vector.tensor_copy(place_i[:, :], moe["place"]))
            step(nc.vector.tensor_scalar(slot_i[:, :], place_i[:, :], P - 1, None, ALU.bitwise_and))
            step(nc.vector.tensor_scalar(block_i[:, :], place_i[:, :], 7, None, ALU.arith_shift_right))
            step(nc.vector.tensor_copy(moe["blk"], block_i[:, :]))
            nc.vector.tensor_copy(moe["spot"], slot_i[:, :]).then_inc(S("spots"), 1)
            for n in range(TT * TOP):
                tt, k = divmod(n, TOP)
                if n >= 4:
                    dve.wait_ge(S("table_part"), n - 3)
                block_n = moe["blk"][:, n:n + 1]
                for j, factor in enumerate((const("tokens")[:, tt:tt + 1], None, moe["wk"][:, tt, k:k + 1])):
                    nc.vector.tensor_scalar(moe["OHb"][:, n % 4, j * MAX_BLOCKS:(j + 1) * MAX_BLOCKS],
                                            iota[:, 0:MAX_BLOCKS], block_n, factor, ALU.is_equal,
                                            *(() if factor is None else (ALU.mult,))).then_inc(S("OHb_done"), 1)
            dve.wait_ge(S("eb_ready"), 1)
            row = moe["ebrow"][0:1, 0:MAX_BLOCKS]
            step(nc.vector.tensor_scalar(row, banks[3][0:1, 384:384 + MAX_BLOCKS], float(E - 1), None, ALU.min))
            step(nc.vector.tensor_copy(expert_of[0:1, 0:MAX_BLOCKS], row))
            step(nc.vector.tensor_scalar(moe["ebrow"][0:1, MAX_BLOCKS:MAX_BLOCKS + 1], moe["bend"][0:1, E - 1:E], -1.0,
                                         None, ALU.add))
            step(nc.vector.tensor_copy(place_i[0:1, 0:1], moe["ebrow"][0:1, MAX_BLOCKS:MAX_BLOCKS + 1]))
            counted_step(nc.vector.tensor_scalar(expert_of[0:1, MAX_BLOCKS:MAX_BLOCKS + 1], place_i[0:1, 0:1], 1, None,
                                                 ALU.arith_shift_right))
            dve.wait_ge(S("table_part"), TT * TOP)
            tab = banks[2]
            nc.vector.tensor_copy(moe["ws"], tab[:, 2 * MAX_BLOCKS:3 * MAX_BLOCKS]).then_inc(S("blocks_known"), 1)
            step(nc.vector.tensor_scalar(moe["free"], tab[:, MAX_BLOCKS:2 * MAX_BLOCKS], -1.0, 1.0, ALU.mult, ALU.add))
            nc.vector.scalar_tensor_tensor(moe["idx"], moe["free"], const("pad_row"), tab[:, 0:MAX_BLOCKS], ALU.mult,
                                           ALU.add).then_inc(S("blocks_known"), 1)

            def block_hidden(b, p):
                dve.wait_ge(S("moe_sg"), b + 1)
                nc.vector.tensor_tensor(moe["hid"][:, p, :], moe["sg"][:, p, :], banks[2 + p][:, FE:2 * FE], ALU.mult)\
                  .then_inc(S("moe_hid"), 1)

            def block_hidden_T(b, p):
                dve.wait_ge(S("moe_ht"), b + 1)
                nc.vector.tensor_copy(moe["hidT"][:, p, :], banks[4][:, 0:2 * P]).then_inc(S("hT_done"), 1)

            def block_out(b, p, added):
                dve.wait_ge(S("w_known"), b + 1)
                dve.wait_ge(S(f"y_added{p}"), added * 16)
                for half in range(2):
                    dve.wait_ge(S("moe_y"), b * 2 + (half + 1))
                    nc.vector.tensor_scalar(moe["y"][:, p, 512 * half:512 * half + 512], banks[5 + half][:, :],
                                            moe["wcol"][:, p:p + 1], None, ALU.mult).then_inc(S("y_copied"), 1)

            steps_done()
            dve.wait_ge(S("blocks_known"), 2)
            pairs_but_one = dve.value_load(expert_of[0:1, MAX_BLOCKS:MAX_BLOCKS + 1], min_val=TT * TOP // 2 - 1,
                                            max_val=MAX_BLOCKS // 2 - 1)
            pairs = pairs_but_one + 1
            block_hidden(0, 0)
            with dve.Fori(1, pairs) as i:
                for b, p in ((i * 2 + (-1), 1), (i * 2, 0)):
                    block_hidden_T(b + (-1), 1 - p)
                    block_hidden(b, p)
                    block_out(b + (-1), 1 - p, i)
            block_hidden_T(pairs_but_one * 2, 0)
            block_hidden(pairs_but_one * 2 + 1, 1)
            block_out(pairs_but_one * 2, 0, pairs)
            block_hidden_T(pairs_but_one * 2 + 1, 1)
            block_out(pairs_but_one * 2 + 1, 1, pairs)
            for k in range(KD):
                dve.wait_ge(S("acc_T"), k + 1)
                nc.vector.scalar_tensor_tensor(h[:, k, :], banks[k % 7][:, :], mod[:, 5 * KD + k:5 * KD + k + 1],
                                               h[:, k, :], ALU.mult, ALU.add).then_inc(S("h_done"), 1)
            apply_norm("n6", lambda k: col("final_norm", k), "out")


def shape_constants(np):
    p = np.arange(P)[:, None]
    j = np.arange(P)[None, :]
    key = np.arange(T)[None, :] - (T - P)
    parts = {
        "ident": (p == j) * 1.0,
        "ones_d": np.full((P, P), 1.0 / D),
        "ones_g": np.full((P, P), 1.0 / 256),
        "ones_h": (p // HD == j // HD) / float(HD),
        "tri": (p <= j) * 1.0,
        "ones": np.ones((P, P)),
        "dist": np.where(key // HD <= p // HD, -np.abs(p - key) * 1.0, MASKED),
        "causal": np.where(key <= p, 0.0, MASKED),
        "chunked": np.where(key // HD <= p // HD, 0.0, MASKED),
        "inv_count": np.concatenate([np.tile(1.0 / np.minimum(np.arange(1, PAD + 1), w), (P, 1))
                                     for w in WINDOWS], axis=1),
        "eps": np.full((P, 1), EPS),
        "before": (p < j) * 1.0,
        "iota": np.tile(j * 1.0, (P, 1)),
        "row": p * 1.0,
        "pad_row": p * 1.0 + PAD_ROW,
        "tokens": p + P * np.arange(TT)[None, :] * 1.0,
    }
    return np.concatenate([parts[name] for name, _ in SHAPE_SIZES], axis=1).astype(np.float32)


def kernel(**inputs):
    import numpy as np
    import concourse.bacc as bacc
    from concourse.bass_utils import run_bass_kernel_spmd

    x = {name: np.asarray(a) for name, a in inputs.items()}

    def tiles(v):
        v = v.reshape(-1, P)
        return np.ascontiguousarray(v.T)

    def padded(v):
        out = np.zeros((P, v.shape[1]), v.dtype)
        out[:v.shape[0]] = v
        return out

    def everywhere(v):
        return np.repeat(v.reshape(1, -1), P, axis=0)

    gain = x["qk_gain"][0]
    columns = {
        "ln_mix": tiles(x["ln_mix"]), "ln_ffn": tiles(x["ln_ffn"]), "ln_ple": tiles(x["ln_ple"]),
        "conv_w": tiles(x["conv_w"]), "conv_b": tiles(x["conv_b"]),
        "qk_gain": np.concatenate([gain, gain], axis=1).T,
        "subln": np.concatenate([x["subln_gain"][0]] * 2).reshape(P, 1),
        "fgate": padded(x["fgate_bias"].T), "lam": everywhere(x["lam_params"]),
        "c": tiles(x["c_2"]), "b_ada": tiles(x["b_ada_2"]), "norm_mix": tiles(x["norm_mix_g_2"]),
        "conv_w2": tiles(x["conv_w_2"]), "conv_b2": tiles(x["conv_b_2"]),
        "dt_bias": padded(x["dt_bias_2"].T), "A_log": padded(x["A_log_2"].T),
        "D_skip": tiles(np.repeat(x["D_skip_2"][0], HD)), "ssd_norm": tiles(x["ssd_norm_g_2"]),
        "pool_scale": tiles(x["pool_scale_2"]), "norm_ffn": tiles(x["norm_ffn_g_2"]),
        "router_bias": everywhere(x["router_bias_2"]), "final_norm": tiles(x["final_norm_g_2"]),
    }
    distance = np.clip(np.arange(P)[:, None] - (np.arange(T)[None, :] - (T - P)), -P, P) + P
    arrays = {
        "cols": np.concatenate([columns[name] for name, _ in COLUMN_SIZES], axis=1),
        "shape_consts": shape_constants(np),
        "x_T": np.ascontiguousarray(x["x"][0].T),
        "p_T": np.ascontiguousarray(x["p"][0, 0].T),
        "rel_rows": np.ascontiguousarray(x["rel_bias"][0][:, distance]),
        "w_in": x["w_in"][0], "w_out": x["w_out"][0], "w_up": x["w_up"][0], "w_down": x["w_down"][0],
        "w_ple_gate": x["w_ple_gate"][0], "w_ple_proj": x["w_ple_proj"][0], "w_ada": x["w_ada_2"][0],
        "w_in_2": x["w_in_2"][0], "pool_w": x["pool_w_2"][0].reshape(D, 256), "w_br_ssd": x["w_br_ssd_2"][0],
        "w_br_pool": x["w_br_pool_2"][0], "w_out_2": x["w_out_2"][0], "w_router": x["w_router_2"][0],
        "we_gate": x["we_gate_2"][0], "we_up": x["we_up_2"][0], "we_down": x["we_down_2"][0],
        "ws_gate": x["ws_gate_2"][0], "ws_up": x["ws_up_2"][0], "ws_down": x["ws_down_2"][0],
    }
    nc = bacc.Bacc("TRN2", target_bir_lowering=False, num_devices=1)
    feed, A = {}, {}
    for name, a in arrays.items():
        feed[f"in_{name}"] = np.ascontiguousarray(a)
        A[name] = nc.dram_tensor(f"in_{name}", a.shape, mybir.dt.from_np(a.dtype), kind="ExternalInput").ap()
    out_T = nc.dram_tensor("out_T", (D, T), mybir.dt.float32, kind="ExternalOutput").ap()
    u_rows = nc.dram_tensor("u_rows", (T + P, D), mybir.dt.float32, kind="Internal").ap()
    y_rows = nc.dram_tensor("y_rows", (T + P, D), mybir.dt.float32, kind="Internal").ap()
    two_blocks(nc, A, out_T, u_rows, y_rows)
    result = run_bass_kernel_spmd(nc, [feed], core_ids=[0])
    return np.ascontiguousarray(result.results[0]["out_T"].T).reshape(1, T, D)
```

```python
import math
from contextlib import ExitStack

import concourse.bass as bass
from concourse import mybir

P = 128
T = 512
D = 1024
KD = D // P
TT = T // P
HD = 64
N_DIFF, N_FOX, N_CHUNK = 4, 6, 6
HEADS = N_DIFF + N_FOX + N_CHUNK
FF = 2816
FT = FF // P
EPS = 1e-6
MASKED = -1e33
LAM_INIT = 0.8 - 0.6 * math.exp(-0.3 * 0)

N_ADA = 6
SG = 8
SH = 32
HPG = SH // SG
E = 64
EG = 8
FE = 256
ROUTED_SCALE = 2.5
WINDOWS = (2, 4, 8, 16)
PAD = 16

COLUMN_SIZES = [
    ("ln_mix", KD), ("ln_ffn", KD), ("ln_ple", KD), ("conv_w", 3 * 2 * FT), ("conv_b", 2 * FT),
    ("qk_gain", 6), ("subln", 1), ("fgate", 1), ("lam", 4 * HD),
    ("c", KD), ("b_ada", N_ADA * KD), ("norm_mix", KD), ("conv_w2", 4 * 32), ("conv_b2", 32),
    ("dt_bias", 1), ("A_log", 1), ("D_skip", 16), ("ssd_norm", 16), ("pool_scale", KD),
    ("norm_ffn", KD), ("router_bias", E), ("final_norm", KD),
]
SHAPE_SIZES = [("ident", P), ("ones_d", P), ("ones_g", P), ("ones_h", P), ("tri", P), ("ones", P),
               ("dist", T), ("causal", T), ("chunked", T), ("inv_count", len(WINDOWS) * PAD),
               ("eps", 1), ("before", P), ("iota", P), ("row", 1),
               ("pad_row", 1), ("tokens", TT)]


def places(sizes):
    at, found = 0, {}
    for name, n in sizes:
        found[name] = (at, n)
        at += n
    return found, at


COLS, N_COLS = places(COLUMN_SIZES)
SHAPES, N_SHAPES = places(SHAPE_SIZES)

NSLOT = 3
PANEL = KD * 512
RING = NSLOT * PANEL
ARENA = 25640
TOP = 8
MAX_BLOCKS = T * TOP // P + E
PAD_ROW = T


def two_blocks(nc, A, out_T, u_rows, y_rows):
    f32 = mybir.dt.float32
    f32r = mybir.dt.float32r
    ALU = mybir.AluOpType
    ACT = mybir.ActivationFunctionType
    AX = mybir.AxisListType

    ctx = ExitStack()
    with ctx:
        def sb(name, shape):
            return ctx.enter_context(nc.sbuf_tensor(name, shape, f32))

        sems = {}

        def S(name):
            if name not in sems:
                sems[name] = ctx.enter_context(nc.semaphore(name))
            return sems[name]

        cols = sb("cols", [P, N_COLS])
        shp = sb("shp", [P, N_SHAPES])
        h = sb("h", [P, KD, T])
        hn_at = nc.sbuf_base
        hn = sb("hn", [P, KD, T])
        sq_at = nc.sbuf_base
        sq = sb("sq", [P, 4, T])
        inv_at = nc.sbuf_base
        inv = sb("inv", [P, 2, T])
        mod = sb("mod", [P, N_ADA * KD])
        small = sb("small", [P, 192])
        arena_at = nc.sbuf_base
        arena = sb("arena", [P, RING + ARENA])
        banks = [ctx.enter_context(nc.psum_tensor(f"bank{i}", [P, 512], f32)) for i in range(8)]
        NORM = 7

        def lay(first, **shapes):
            made = {}
            for name, shape in shapes.items():
                n = 1
                for s in shape:
                    n *= s
                assert first + n <= RING + ARENA, (name, first + n - RING - ARENA)
                v = arena[:, first:first + n]
                if len(shape) == 2:
                    v = v.rearrange("p (a b) -> p a b", b=shape[1])
                if len(shape) == 3:
                    v = v.rearrange("p (a b c) -> p a b c", b=shape[1], c=shape[2])
                made[name] = v
                first += n
            made["end"] = first
            return made

        def col(name, i=0, n=1):
            return cols[:, COLS[name][0] + i:COLS[name][0] + i + n]

        def const(name):
            a, n = SHAPES[name]
            return shp[:, a:a + n]

        ident, ones, tri = const("ident"), const("ones"), const("tri")
        EPS_COLUMN = const("eps")
        LAM_DOT, LAM_EXP = small[:, 0:2], small[:, 2:4]
        NEG_LAM, SUBLN = small[:, 4:5], small[:, 5:6]
        NEG_MAX = small[:, 8:88]
        ROW_SUM = small[:, 88:168]
        RECIP = small[:, 168:172]
        C_ACT = small[:, 172:180]
        GAIN1 = small[:, 180:188]
        EXP_A = small[0:SH, 188:189]

        att = lay(RING, qk=(20, T), V=(TT, D), tab_diff=(N_DIFF, T), tab_chunk=(N_CHUNK, T),
                  F8=(T,), t=(4, T), pt2=(TT, T))
        TABLES = RING + 20 * T + TT * D
        F8_AT = TABLES + (N_DIFF + N_CHUNK) * T
        fgt = lay(F8_AT - 2 * T, x=(T,), l=(T,))
        PT = [sq, att["pt2"]]
        NORMED = inv
        ffn = lay(RING, hid=(FT, T), cv=(6, T), sg=(2, T), ada=(2, T))
        split_at = arena_at + 4 * ffn["end"]

        def rounded(name, shape, at):
            return nc.alloc_sbuf_tensor_at(name, shape, f32r, offset=at)

        z_x_high = rounded("z_x_high", [P, KD, T], arena_at + 4 * TABLES)
        z_w_high = rounded("z_w_high", [P, 2, 2 * KD * P], arena_at + 4 * (F8_AT + T))
        x_high = rounded("x_high", [P, KD, T], split_at)
        w_high = rounded("w_high", [P, 2, 2 * KD * P], split_at + 4 * KD * T)
        x_low = rounded("x_low", [P, KD, T], hn_at)
        w_low = rounded("w_low", [P, NSLOT, PANEL], arena_at)
        hid_low = rounded("hid_low", [P, FT, T], arena_at + 4 * RING)
        hid_high = [rounded("hid_high0", [P, 8, T], arena_at + 4 * (RING + FT * T)),
                    rounded("hid_high1", [P, FT - 8, T], split_at)]
        down_high = rounded("down_high", [P, 2, 2 * KD * P], hn_at)
        ple = lay(RING, pT=(2, T), gt=(2, T), tmp=(2, T))
        mix = lay(RING, yn=(16, T), pooled=(KD, T))
        dtk = lay(mix["end"], dtp=(T,), tok=(TT, 96))
        pool = lay(dtk["end"], x=(2, PAD + T), s=(4, PAD + T), head=(2, PAD), raw=(T,), ab=(T,), l=(T,),
                   a=(T,), acs=(T,))
        ssd = lay(dtk["end"], zs=(4, T), xs=(4, T), B=(2, T), C=(2, T), xtok=(2, 3 * P),
                  xdt=(2, 2 * P), xdec=(2, 2 * P), CB=(2, P), Ex=(2, HPG * P), L=(2, HPG * P),
                  CE=(2, HPG * P), state=(HPG * HD,), carry=(HPG * HD,))
        ssd["th"] = sq[:, 2:4, :]
        late = lay(dtk["end"], gs=(16, T), tmp=(2, T))
        wo_x_high = rounded("wo_x_high", [P, KD, T], arena_at + 4 * RING)
        wo_w_high = [rounded("wo_w_high0", [P, KD, 2 * P], arena_at + 4 * TABLES),
                     rounded("wo_w_high1", [P, KD, 2 * P], arena_at + 4 * (RING + 20 * T))]
        ple_x_high = rounded("ple_x_high", [P, KD, T], arena_at + 4 * ple["end"])
        pooled_low = rounded("pooled_low", [P, KD, T], arena_at + 4 * (RING + 16 * T))
        pooled_high = [rounded("pooled_high0", [P, 4, T], sq_at), rounded("pooled_high1", [P, 2, T], inv_at),
                       rounded("pooled_high2", [P, 2, T], arena_at + 4 * (late["end"] + 2 * KD * P))]
        mixed_high = rounded("mixed_high", [P, KD, T], arena_at + 4 * (RING + 2 * KD * P))
        ple_w_high = [rounded(f"ple_w_high{i}", [P, KD, 2 * P], arena_at + 4 * (ple["end"] + (KD * T) + i * 2 * KD * P))
                      for i in range(2)]
        late_w_high = [rounded("late_w_high0", [P, KD, 2 * P], arena_at + 4 * late["end"]),
                       rounded("late_w_high1", [P, KD, 2 * P], arena_at + 4 * RING)]
        moe = lay(0, gu=(2, KD * 512), dn=(2, 2 * D), X=(2, D), xT=(2, KD * P), sg=(2, FE), hid=(2, FE),
                  hidT=(2, 2 * P), y=(2, D), wcol=(2,), idx=(MAX_BLOCKS,), ws=(MAX_BLOCKS,),
                  sgu=(KD, 512), sdn=(2, D), ssg=(2, FE), sup=(2, FE), shid=(2, FE), shT=(2, 2 * P),
                  sy=(2, D),
                  sc=(TT, E), ch=(TT, E), mk=(TT, E), best=(TT, EG * 8), gsum=(TT, EG), gtop=(TT, EG), gf=(TT, EG),
                  gm=(TT, EG), gneg=(TT, EG), top=(TT, TOP), ef=(TT, TOP), sel=(TT, E), wk=(TT, TOP), wsum=(TT,),
                  junk=(E,), nb=(E,), bend=(E,), bstart=(E,), start=(TT, E), place=(TT * TOP,), blk=(TT * TOP,),
                  spot=(TT * TOP,), ebcol=(2,), ebrow=(MAX_BLOCKS + 1,), OHs=(4, P), OHb=(4, 3 * MAX_BLOCKS),
                  free=(MAX_BLOCKS,))
        moe["zero"] = moe["y"][:, 1, :]
        moe["ut"] = moe["dn"].rearrange("p a (b n) -> p (a b) n", n=D)
        acc = lay(0, acc=(TT, D))["acc"]
        u32, i32 = mybir.dt.uint32, mybir.dt.int32

        def ints(name, n, dt):
            return ctx.enter_context(nc.sbuf_tensor(name, [P, n], dt))

        gix = ints("gix", TT * 8, u32)
        eix = ints("eix", TT * TOP, u32)
        place_i, slot_i = ints("place_i", TT * TOP, i32), ints("slot_i", TT * TOP, i32)
        block_i = ints("block_i", TT * TOP, i32)
        expert_of = ints("expert_of", MAX_BLOCKS + 1, i32)
        rows_in = [ints(f"rows_in{i}", 1, u32) for i in range(2)]
        rows_out = [ints(f"rows_out{i}", 1, u32) for i in range(2)]

        NORMS = {"n1": 0, "n2": 1, "n3": 2, "n4": 3, "n5": 4, "n6": 5}

        N_QK = 20
        PRODUCTS, _ = places([("z", N_QK + 5 * TT + 1), ("wo", KD), ("up", 2 * FT), ("down", 12), ("ple", 2 * KD),
                              ("x", 9), ("pool", KD), ("ssd", 6 * SG), ("gates", 16), ("ssd_out", 4),
                              ("pool_out", KD), ("wo2", KD), ("router", TT)])
        PRODUCTS = {name: first for name, (first, _) in PRODUCTS.items()}
        PREPARED = {"halved": 0, "lam_dot": 1, "subln": 3, "neg_lam": 4, "tables": 5}

        PANELS = []
        SLOT_OF, BEFORE, latest = [], [], [-1] * NSLOT

        def slot(i, w):
            v = arena[:, SLOT_OF[i] * PANEL:SLOT_OF[i] * PANEL + KD * w]
            return v.rearrange("p (k n) -> p k n", n=w)

        def rows(W, k0, k1, c0, c1):
            return W[k0 * P:k1 * P, c0:c1].rearrange("(k p) n -> p k n", p=P)

        def add_panel(copies, semaphore, value, chosen=None):
            i = len(PANELS)
            s = latest.index(min(latest)) if chosen is None else chosen
            SLOT_OF.append(s)
            BEFORE.append(latest[s])
            latest[s] = i
            PANELS.append(([(slot(i, w)[:, 0:b - a, d0:d0 + c1 - c0], rows(W, a, b, c0, c1))
                            for W, a, b, c0, c1, w, d0 in copies], semaphore, value))
            return i

        def one(W, k0, k1, c0, c1):
            return [(W, k0, k1, c0, c1, c1 - c0, 0)]

        Z_PANELS = [(0, 256), (256, 512), (512, 768), (768, 1024), (1024, 1280), (1280, 1536), (1536, 1792),
                    (1792, 2048), (2048, 2304), (2304, 2438), (2438, 2694), (2694, 2950), (2950, 3206),
                    (3206, 3462), (3462, 3590)]
        V_PANELS = {4: (0, 256), 8: (256, 256), 9: (512, 128), 13: (640, 256), 14: (896, 128)}
        FORGET_PANEL = 9
        Z_GROUPS = []
        for pn, (c0, c1) in enumerate(Z_PANELS):
            if pn in V_PANELS:
                Z_GROUPS += [("v", pn, tt, V_PANELS[pn][1]) for tt in range(TT)]
                if pn == FORGET_PANEL:
                    Z_GROUPS.append(("fg", pn, P, N_FOX))
            else:
                Z_GROUPS += [("qk", pn, c, P) for c in range(0, c1 - c0, P)]
            add_panel(one(A["w_in"], 0, KD, c0, c1), S("product"), PRODUCTS["z"] + len(Z_GROUPS))
        QK_GAIN = [0, 0, 0, 0, 1, 1, 1, 1, 2, 2, 2, 3, 3, 3, 4, 4, 4, 5, 5, 5]
        Z_FREED = []
        n_qk = n_v = 0
        for kind, *_ in Z_GROUPS:
            if kind == "qk":
                n_qk += 1
                Z_FREED.append((S("qk_done"), n_qk))
            else:
                n_v += 1
                Z_FREED.append((S("v_done"), n_v))

        wo_panel = len(PANELS)
        for half in range(2):
            add_panel(one(A["w_out"], 0, KD, 512 * half, 512 * half + 512), S("product"), PRODUCTS["wo"] + 4 * half + 4)
        up_panels, ada_panels, down_panels = [], [], []
        mlp_slots = sorted(range(NSLOT), key=lambda s: latest[s])
        ada_slot = mlp_slots.pop()

        def add_ada_panel():
            m = len(ada_panels)
            ada_panels.append(add_panel(one(A["w_ada"], 0, KD, 512 * m, 512 * m + 512), S("ada_sum"), KD * (m + 1), ada_slot))

        for q in range(FT // 2):
            up_panels.append(add_panel([(A["w_up"], 0, KD, 256 * q, 256 * q + 256, 512, 0),
                                        (A["w_up"], 0, KD, FF + 256 * q, FF + 256 * q + 256, 512, 256)],
                                       S("product"), PRODUCTS["up"] + 4 * q + 4, mlp_slots[q % 2]))
            if q >= 1:
                add_ada_panel()
        DOWN_K = [(0, 8), (8, 16), (16, 22)]
        for half in range(2):
            for k0, k1 in DOWN_K:
                down_panels.append(add_panel(one(A["w_down"], k0, k1, 512 * half, 512 * half + 512),
                                             S("product"), PRODUCTS["down"] + 2 * len(down_panels) + 2))
                if len(ada_panels) < 2 * N_ADA:
                    add_ada_panel()
        proj_panel = add_panel(one(A["w_ple_proj"], 0, 2, 0, D), S("product"), PRODUCTS["ple"] + 2 * KD)
        gate_panel = len(PANELS)
        for half in range(2):
            add_panel(one(A["w_ple_gate"], 0, KD, 512 * half, 512 * half + 512), S("product"), PRODUCTS["ple"] + 8 * half + 8)

        w_in2 = A["w_in_2"]
        x_panel = len(PANELS)
        for c0, c1, v in ((6144, 6560, 4), (6560, 6944, 7), (6944, 7200, 9)):
            add_panel(one(w_in2, 0, KD, c0, c1), S("product"), PRODUCTS["x"] + v)
        X_TILES = [(x_panel, SH + P * i, 416) for i in range(3)] + \
                  [(x_panel + 1, P * i, 384) for i in range(3)] + [(x_panel + 2, P * i, 256) for i in range(2)]
        pool_panel = add_panel(one(A["pool_w"], 0, KD, 0, 256), S("product"), PRODUCTS["pool"] + KD)
        ssd_panel = len(PANELS)
        for g in range(SG):
            add_panel([(w_in2, 0, KD, 256 * g, 256 * g + 256, 512, 0),
                       (w_in2, 0, KD, 2048 + 256 * g, 2048 + 256 * g + 256, 512, 256)],
                      S("product"), PRODUCTS["ssd"] + 6 * g + 4)
            add_panel([(w_in2, 0, KD, 4096 + P * g, 4096 + P * g + P, 256, 0),
                       (w_in2, 0, KD, 5120 + P * g, 5120 + P * g + P, 256, P)],
                      S("product"), PRODUCTS["ssd"] + 6 * g + 6)
        gts_panel = len(PANELS)
        for q in range(4):
            add_panel(one(w_in2, 0, KD, 7200 + 512 * q, 7712 + 512 * q), S("product"), PRODUCTS["gates"] + 4 * q + 4)
        br_panel = len(PANELS)
        for half in range(2):
            for kg in range(2):
                add_panel(one(A["w_br_ssd"], KD * kg, KD * kg + KD, 512 * half, 512 * half + 512),
                          S("product"), PRODUCTS["ssd_out"] + 2 * half + kg + 1)
        bp_panel = len(PANELS)
        for half in range(2):
            add_panel(one(A["w_br_pool"], 0, KD, 512 * half, 512 * half + 512), S("product"), PRODUCTS["pool_out"] + 4 * half + 4)
        wo2_panel = len(PANELS)
        for half in range(2):
            add_panel(one(A["w_out_2"], 0, KD, 512 * half, 512 * half + 512), S("product"), PRODUCTS["wo2"] + 4 * half + 4)
        router_panel = add_panel(one(A["w_router"], 0, KD, 0, E), S("product"), PRODUCTS["router"] + TT)

        ARRIVED, counted = [], [0] * NSLOT
        for i, (copies, _, _) in enumerate(PANELS):
            counted[SLOT_OF[i]] += 16 * len(copies)
            ARRIVED.append(counted[SLOT_OF[i]])

        W_UNITS, _ = places([("z", len(Z_PANELS)), ("wo", 4), ("up", FT), ("down", 12), ("ple", 4), ("pool_out", 4),
                             ("wo2", 4)])
        W_UNITS = {name: first for name, (first, _) in W_UNITS.items()}
        def up_columns(pair, parts):
            return parts.rearrange("p k (t c) -> p k t c", t=2)[:, :, :, P * (pair % 2):P * (pair % 2) + P]

        def z_weights(pn, of):
            n = Z_PANELS[pn][1] - Z_PANELS[pn][0]
            v = {"whole": arena[:, SLOT_OF[pn] * PANEL:(SLOT_OF[pn] + 1) * PANEL], "high": z_w_high[:, pn % 2, :],
                 "low": w_low[:, SLOT_OF[pn], :]}[of]
            return v[:, 0:KD * n].rearrange("p (k n) -> p k n", n=n)

        def up_high(pair):
            return w_high[:, pair % 2, :].rearrange("p (k t c) -> p k t c", t=2, c=P)

        def up_low(pair):
            return up_columns(pair, w_low[:, SLOT_OF[up_panels[pair // 2]], :].rearrange("p (k n) -> p k n", n=512))

        DOWN_UNITS = [(down_panels[3 * half + n], k0, k1, 4 * half + 2 * pair)
                      for half in range(2) for n, (k0, k1) in enumerate(DOWN_K) for pair in range(2)]

        def unit_weights(j, of):
            pn, k0, k1, t = DOWN_UNITS[j]
            if of == "high":
                return down_high[:, j % 2, :].rearrange("p (k n) -> p k n", n=2 * P)[:, 0:k1 - k0, :]
            panel = slot(pn, 512) if of == "whole" else w_low[:, SLOT_OF[pn], :].rearrange("p (k n) -> p k n", n=512)
            return panel[:, 0:k1 - k0, P * (t % 4):P * (t % 4) + 2 * P]

        def square_weights(name, u, of):
            if of == "high":
                return {"wo": wo_w_high, "ple": ple_w_high}.get(name, late_w_high)[u % 2][:, :, :]
            pn = {"wo": wo_panel, "ple": gate_panel, "pool_out": bp_panel, "wo2": wo2_panel}[name] + u // 2
            panel = slot(pn, 512) if of == "whole" else w_low[:, SLOT_OF[pn], :].rearrange("p (k n) -> p k n", n=512)
            return panel[:, :, 2 * P * (u % 2):2 * P * (u % 2) + 2 * P]

        def pooled_high_tile(k):
            return pooled_high[0][:, k, :] if k < 4 else pooled_high[(k - 2) // 2][:, k % 2, :]

        def hidden_high(k):
            return hid_high[k // 8 > 0][:, k if k < 8 else k - 8, :]

        def panel_here(eng, i):
            eng.wait_ge(S(f"panel_in_slot{SLOT_OF[i]}"), ARRIVED[i])

        def s_freed(i):
            g, j = divmod(i, 6)
            return (S("z_read"), 2 * g + j + 1) if j < 2 else (S("s_taps"), 3 * (4 * g + j - 1))

        FILL = ((0, 1), (2,), (3, 4), (5,))

        UNITS, MAPS = [], []
        for hh in range(HEADS):
            for qt in range(TT):
                first = len(MAPS)
                if hh < N_DIFF:
                    MAPS += [(hh // 2, 4 + hh // 2), (2 + hh // 2, 6 + hh // 2)]
                elif hh < N_DIFF + N_FOX:
                    MAPS.append((8 + (hh - N_DIFF) // 2, 11 + (hh - N_DIFF) // 2))
                else:
                    MAPS.append((14 + (hh - N_DIFF - N_FOX) // 2, 17 + (hh - N_DIFF - N_FOX) // 2))
                UNITS.append((hh, qt, first, len(MAPS) - first))

        UNIT_OF = [u for u, (_, _, _, n) in enumerate(UNITS) for _ in range(n)]

        def table(hh, qt):
            if hh < N_DIFF:
                whole = att["tab_diff"][:, hh, :]
            elif hh < N_DIFF + N_FOX:
                whole = const("causal")
            else:
                whole = att["tab_chunk"][:, hh - N_DIFF - N_FOX, :]
            return whole[:, T - P * (qt + 1):T]

        block = ctx.enter_context(nc.Block())

        @block.sync
        def _(sp):
            for i, (copies, _, _) in enumerate(PANELS):
                if BEFORE[i] >= 0:
                    sp.wait_ge(PANELS[BEFORE[i]][1], PANELS[BEFORE[i]][2])
                for dst, src in copies:
                    sp.dma_start(dst, src).then_inc(S(f"panel_in_slot{SLOT_OF[i]}"), 16)

            sp.wait_ge(S("product"), PRODUCTS["router"] + TT)
            sp.dma_start(moe["sgu"][:, :, 0:FE], A["ws_gate"].rearrange("(k p) n -> p k n", p=P)).then_inc(S("shared_in"), 16)
            sp.dma_start(moe["sgu"][:, :, FE:2 * FE], A["ws_up"].rearrange("(k p) n -> p k n", p=P)).then_inc(S("shared_in"), 16)
            sp.dma_start(moe["sdn"], A["ws_down"].rearrange("(k p) n -> p k n", p=P)).then_inc(S("shared_in"), 16)

            def load_up(b, p):
                e = sp.value_load(expert_of[0:1, bass.ds(b, 1)], min_val=0, max_val=E - 1)
                gu = moe["gu"][:, p, :].rearrange("p (k n) -> p k n", n=512)
                for name, c in (("we_gate", 0), ("we_up", FE)):
                    sp.dma_start(gu[:, :, c:c + FE], A[name][bass.ds(e, 1)].rearrange("a (k p) n -> p (a k) n", p=P))\
                      .then_inc(S(f"up_in{p}"), 16)
                return e

            def load_down(e, p):
                sp.dma_start(moe["dn"][:, p, :].rearrange("p (k n) -> p k n", n=D),
                             A["we_down"][bass.ds(e, 1)].rearrange("a (k p) n -> p (a k) n", p=P))\
                  .then_inc(S(f"down_in{p}"), 16)

            sp.wait_ge(S("blocks_known"), 2)
            pairs_but_one = sp.value_load(expert_of[0:1, MAX_BLOCKS:MAX_BLOCKS + 1], min_val=TT * TOP // 2 - 1,
                                            max_val=MAX_BLOCKS // 2 - 1)
            pairs = pairs_but_one + 1
            sp.wait_ge(S("u_stored"), 16 * TT)
            for p in range(2):
                load_down(load_up(p, p), p)
            with sp.Fori(1, pairs) as i:
                for p in range(2):
                    sp.wait_ge(S("moe_gu"), i * 2 + (p - 1))
                    e = load_up(i * 2 + p, p)
                    sp.wait_ge(S("moe_y"), i * 4 + (2 * p - 2))
                    load_down(e, p)

            for p in range(2):
                sp.wait_ge(S(f"y_added{p}"), pairs * 16 + 16)
            sp.dma_start(acc, y_rows[0:T, :].rearrange("(t p) n -> p t n", p=P)).then_inc(S("acc_in"), 16)

            for k in range(KD):
                sp.wait_ge(S("norm_out"), KD * NORMS["n6"] + k + 1)
                sp.dma_start(out_T[k * P:(k + 1) * P, :], hn[:, k, :]).then_inc(S("stored"), 16)
            sp.wait_ge(S("stored"), 16 * KD)

        @block.gpsimd
        def _(pool_eng):
            pool_eng.dma_start(cols[:, :], A["cols"]).then_inc(S("cols_in"), 16)
            for k in range(4):
                pool_eng.dma_start(h[:, 2 * k:2 * k + 2, :],
                                   A["x_T"][2 * k * P:(2 * k + 2) * P, :].rearrange("(k p) n -> p k n", p=P))\
                        .then_inc(S(f"x_in{k}"), 16)
                if k == 0:
                    pool_eng.dma_start(shp[:, :], A["shape_consts"]).then_inc(S("shp_in"), 16)
            for pn in range(len(Z_PANELS)):
                pool_eng.wait_ge(S("w_high"), pn + 1)
                pool_eng.tensor_tensor(z_weights(pn, "low"), z_weights(pn, "whole"), z_weights(pn, "high").bitcast(f32),
                                       ALU.subtract).then_inc(S("w_low"), 1)
            pool_eng.wait_ge(S("product"), PRODUCTS["z"] + len(Z_GROUPS))
            pool_eng.wait_ge(S("F_done"), 1)
            for f in range(N_CHUNK):
                pool_eng.dma_start(att["tab_chunk"][:, f, :], A["rel_rows"][f]).then_inc(S("rel_in"), 16)
            def low_weights(name):
                for u in range(4):
                    pool_eng.wait_ge(S("w_high"), W_UNITS[name] + u + 1)
                    pool_eng.tensor_tensor(square_weights(name, u, "low"), square_weights(name, u, "whole"),
                                           square_weights(name, u, "high").bitcast(f32), ALU.subtract)\
                            .then_inc(S("w_low"), 1)

            low_weights("wo")
            for pair in range(FT):
                w = up_columns(pair, slot(up_panels[pair // 2], 512))
                pool_eng.wait_ge(S("w_high"), W_UNITS["up"] + pair + 1)
                pool_eng.tensor_tensor(up_low(pair), w, up_high(pair).bitcast(f32), ALU.subtract)\
                        .then_inc(S("w_low"), 1)
            for j in range(len(DOWN_UNITS)):
                pool_eng.wait_ge(S("w_high"), W_UNITS["down"] + j + 1)
                pool_eng.tensor_tensor(unit_weights(j, "low"), unit_weights(j, "whole"),
                                       unit_weights(j, "high").bitcast(f32), ALU.subtract).then_inc(S("w_low"), 1)
            pool_eng.wait_ge(S("product"), PRODUCTS["down"] + 12)
            pool_eng.dma_start(ple["pT"], A["p_T"].rearrange("(k p) n -> p k n", p=P)).then_inc(S("p_in"), 16)
            low_weights("ple")
            pool_eng.wait_ge(S("product"), PRODUCTS["ple"] + 2 * KD)
            pool_eng.memset(pool["x"][:, :, 0:PAD], 0.0).then_inc(S("pads"), 1)
            pool_eng.memset(pool["s"][:, :, 0:PAD], 0.0).then_inc(S("pads"), 1)
            for k in range(KD):
                pool_eng.wait_ge(S("pooled_high"), k + 1)
                pool_eng.tensor_tensor(pooled_low[:, k, :], mix["pooled"][:, k, :], pooled_high_tile(k).bitcast(f32),
                                       ALU.subtract).then_inc(S("pooled_low"), 1)
            low_weights("pool_out")
            low_weights("wo2")
            pool_eng.wait_ge(S("product"), PRODUCTS["router"] + TT)
            pool_eng.memset(moe["zero"], 0.0).then_inc(S("zero_set"), 1)
            pool_eng.wait_ge(S("zero_set"), 1)
            pool_eng.dma_start(u_rows[T:T + P, :], moe["zero"]).then_inc(S("rows_zeroed"), 16)
            for p in range(2):
                pool_eng.dma_start(y_rows[T + HD * p:T + HD * (p + 1), :], moe["zero"][0:HD, :])\
                        .then_inc(S(f"y_added{p}"), 16)

            for tt in range(TT):
                pool_eng.wait_ge(S("sh_up"), tt + 1)
                if tt >= 2:
                    pool_eng.wait_ge(S("sh_ht"), tt - 1)
                pool_eng.tensor_tensor(moe["shid"][:, tt % 2, :], moe["ssg"][:, tt % 2, :], moe["sup"][:, tt % 2, :],
                                       ALU.mult).then_inc(S("sh_hid"), 1)
            for n in range(TT * TOP):
                pool_eng.wait_ge(S("spots"), 1)
                if n >= 4:
                    pool_eng.wait_ge(S("table_part"), n - 3)
                pool_eng.tensor_scalar(moe["OHs"][:, n % 4, :], const("iota"), moe["spot"][:, n:n + 1], None,
                                       ALU.is_equal).then_inc(S("OHs_done"), 1)

            def gather(b, p):
                pool_eng.tensor_copy(rows_in[p][:, :], moe["idx"][:, bass.ds(b, 1)]).then_inc(S("rows_known"), 1)
                pool_eng.wait_ge(S("rows_known"), b + 1)
                pool_eng.nop(nofuse=True)
                pool_eng.indirect_dma_start(moe["X"][:, p, :], None, u_rows, bass.IndirectOffsetOnAxis(rows_in[p][:, :], 0))\
                        .then_inc(S(f"x_gathered{p}"), 16)

            def scatter(b, p, added):
                pool_eng.tensor_copy(rows_out[p][:, :], moe["idx"][:, bass.ds(b, 1)]).then_inc(S("rows_back"), 1)
                pool_eng.wait_ge(S("rows_back"), b + 1)
                pool_eng.wait_ge(S("y_copied"), b * 2 + (2 * TT + 2))
                pool_eng.wait_ge(S(f"y_added{1 - p}"), added * 16)
                pool_eng.nop(nofuse=True)
                pool_eng.indirect_dma_start(y_rows, bass.IndirectOffsetOnAxis(rows_out[p][:, :], 0), moe["y"][:, p, :], None,
                                            compute_op=ALU.add).then_inc(S(f"y_added{p}"), 16)

            def weights(b, p):
                pool_eng.tensor_copy(moe["wcol"][:, p:p + 1], moe["ws"][:, bass.ds(b, 1)]).then_inc(S("w_known"), 1)

            pool_eng.wait_ge(S("blocks_known"), 2)
            pairs_but_one = pool_eng.value_load(expert_of[0:1, MAX_BLOCKS:MAX_BLOCKS + 1], min_val=TT * TOP // 2 - 1,
                                                max_val=MAX_BLOCKS // 2 - 1)
            pairs = pairs_but_one + 1
            pool_eng.wait_ge(S("u_stored"), 16 * TT)
            pool_eng.wait_ge(S("rows_zeroed"), 16)
            for p in range(2):
                gather(p, p)
                weights(p, p)
            for p in range(2):
                pool_eng.wait_ge(S("moe_tr"), 2 * p + 2)
                gather(2 + p, p)
            for p in range(2):
                pool_eng.wait_ge(S(f"shared_stored{p}"), 16 * TT // 2)
            scatter(0, 0, 1)
            weights(2, 0)
            with pool_eng.Fori(2, pairs) as i:
                pool_eng.wait_ge(S("moe_tr"), i * 4 + (-2))
                gather(i * 2, 0)
                scatter(i * 2 + (-3), 1, i)
                weights(i * 2 + (-1), 1)
                pool_eng.wait_ge(S("moe_tr"), i * 4)
                gather(i * 2 + 1, 1)
                scatter(i * 2 + (-2), 0, i)
                weights(i * 2, 0)
            scatter(pairs_but_one * 2 + (-1), 1, pairs)
            weights(pairs_but_one * 2 + 1, 1)
            scatter(pairs_but_one * 2, 0, pairs)
            scatter(pairs_but_one * 2 + 1, 1, pairs + 1)
        @block.tensor
        def _(pe):
            def product(out, w, rhs, nk, first=True, last=True):
                for k in range(nk):
                    ins = nc.tensor.matmul(out, w(k), rhs(k), start=first and k == 0, stop=last and k == nk - 1)
                return ins

            def split_product(out, w_high, w_low, x_high, x_low, ready=None):
                for k in range(KD):
                    if ready is not None:
                        ready(k)
                    for n, (w, x) in enumerate(((w_high(k), x_high(k)), (w_high(k), x_low(k)), (w_low(k), x_high(k)))):
                        ins = nc.tensor.matmul(out, w, x, start=k == 0 and n == 0, stop=k == KD - 1 and n == 2)
                return ins

            def both_parts(first):
                return lambda k: pe.wait_ge(S("x_low"), first + k + 1)

            def square_product(name, t, bank, x_high, x_low, ready):
                high, low = (square_weights(name, t // 2, of)[:, :, P * (t % 2):P * (t % 2) + P] for of in ("high", "low"))
                split_product(bank[:, :], lambda k: high[:, k, :], lambda k: low[:, k, :], x_high, x_low,
                              ready if t == 0 else None).then_inc(S("product"), 1)

            def norm_sum(name):
                for k in range(KD):
                    pe.wait_ge(S("norm_sq"), KD * NORMS[name] + k + 1)
                    nc.tensor.matmul(banks[NORM][:, :], const("ones_d"), sq[:, k % 4, :], start=k == 0,
                                     stop=k == KD - 1).then_inc(S("norm_sum"), 1)

            def normed(name, k):
                pe.wait_ge(S("norm_out"), KD * NORMS[name] + k + 1)

            pe.wait_ge(S("shp_in"), 16)
            norm_sum("n1")
            j = 0
            pending = None

            def head_sum(j):
                pe.wait_ge(S("qk_sq"), j + 1)
                if j >= 2:
                    pe.wait_ge(S("qk_root"), j - 1)
                nc.tensor.matmul(banks[6 + j % 2][:, :], const("ones_h"), sq[:, j % 4, :], start=True,
                                 stop=True).then_inc(S("qk_sum"), 1)

            for t, (kind, pn, c, width) in enumerate(Z_GROUPS):
                pe.wait_ge(S("w_low"), pn + 1)
                ready = both_parts(0) if t == 0 else None
                if t >= 6:
                    pe.wait_ge(*Z_FREED[t - 6])
                high, low = z_weights(pn, "high"), z_weights(pn, "low")
                bank = banks[t % 6]
                if kind == "v":
                    now = slice(c * P, (c + 1) * P)
                    ins = split_product(bank[:, 0:width], lambda k: z_x_high[:, k, now], lambda k: x_low[:, k, now],
                                        lambda k: high[:, k, 0:width], lambda k: low[:, k, 0:width])
                else:
                    ins = split_product(bank[0:width, :], lambda k: high[:, k, c:c + width],
                                        lambda k: low[:, k, c:c + width], lambda k: z_x_high[:, k, :],
                                        lambda k: x_low[:, k, :], ready)
                ins.then_inc(S("product"), 1)
                if pending is not None:
                    head_sum(pending)
                    pending = None
                if kind == "qk":
                    pending, j = j, j + 1
            if pending is not None:
                head_sum(pending)

            pe.wait_ge(S("qk_done"), N_QK)
            pe.wait_ge(S("v_done"), len(Z_GROUPS) - N_QK)
            pe.wait_ge(S("F_done"), 1)

            def scores(u):
                hh, qt, first, n = UNITS[u]
                r = HD * (hh % 2)
                W = P * (qt + 1)
                fox = N_DIFF <= hh < N_DIFF + N_FOX
                for m in range(first, first + n):
                    if m >= 4:
                        pe.wait_ge(S("t_done"), m - 3)
                    out = banks[m % 4][:, 0:W]
                    qi, ki = MAPS[m]
                    ins = nc.tensor.matmul(out, att["qk"][r:r + HD, qi, P * qt:P * qt + P],
                                           att["qk"][r:r + HD, ki, 0:W], start=True, stop=not fox)
                    if fox:
                        f = hh - N_DIFF
                        ins = nc.tensor.matmul(out, ident[0:N_FOX, f:f + 1].to_broadcast([N_FOX, P]),
                                               att["F8"][0:N_FOX, 0:W], start=False, stop=True)
                    ins.then_inc(S("s_scores"), 1)

            def transposes(u):
                hh, qt, first, n = UNITS[u]
                pe.wait_ge(S("probs_done"), u + 1)
                if u >= 2:
                    pe.wait_ge(S("pt_done"), u - 1)
                for kt in range(qt + 1):
                    ins = nc.tensor.transpose(banks[4 + u % 2][:, kt * P:(kt + 1) * P],
                                              NORMED[:, u % 2, kt * P:(kt + 1) * P], ident)
                ins.then_inc(S("tr_ready"), 1)

            def values(hh):
                pe.wait_ge(S("pt_done"), 4 * hh + 4)
                if hh >= 2:
                    pe.wait_ge(S("o_done"), hh - 1)
                for kt in range(TT):
                    ins = nc.tensor.matmul(banks[6 + hh % 2][0:HD, kt * P:T], att["V"][:, kt, HD * hh:HD * hh + HD],
                                           PT[hh % 2][:, kt, kt * P:T], start=kt == 0, stop=kt == TT - 1)
                ins.then_inc(S("o_ready"), 1)

            for u in range(len(UNITS) + 3):
                if u < len(UNITS):
                    scores(u)
                if u >= 3 and (u - 3) % 4 == 3:
                    values((u - 3) // 4)
                if 2 <= u < len(UNITS) + 2:
                    transposes(u - 2)
            for i in range(2):
                pe.wait_ge(S("qk_sq"), N_QK + i + 1)
                nc.tensor.matmul(banks[i][:, :], const("ones_h"), sq[:, i, :], start=True,
                                 stop=True).then_inc(S("qk_sum"), 1)

            pe.wait_ge(S("o_done"), HEADS)
            pe.wait_ge(S("qk_done"), N_QK + 2)
            for t in range(KD):
                pe.wait_ge(S("w_low"), W_UNITS["wo"] + t // 2 + 1)
                if t >= 7:
                    pe.wait_ge(S("h_done"), t - 6)
                square_product("wo", t, banks[t % 7], lambda k: wo_x_high[:, k, :], lambda k: x_low[:, k, :],
                               lambda k: pe.wait_ge(S("x_low"), KD + (k - 2) % KD + 1))
            norm_sum("n2")

            def ada_columns(m):
                pe.wait_ge(S("ada_sum"), KD * (m + 1))
                for i in range(4):
                    ins = nc.tensor.matmul(banks[NORM][:, 4 * m + i:4 * m + i + 1],
                                           ffn["ada"][:, m % 2, P * i:P * i + P], ones[:, 0:1], start=True, stop=True)
                ins.then_inc(S("ada_columns"), 1)

            for i in range(2 * FT):
                pair = i // 2
                pe.wait_ge(S("w_low"), W_UNITS["up"] + pair + 1)
                if i >= 6:
                    pe.wait_ge(S("taps"), 2 * (i - 5))
                high, low = up_high(pair)[:, :, i % 2, :], up_low(pair)[:, :, i % 2, :]
                split_product(banks[i % 6][:, :], lambda k: high[:, k, :], lambda k: low[:, k, :],
                              lambda k: x_high[:, k, :], lambda k: x_low[:, k, :],
                              both_parts(2 * KD) if i == 0 else None).then_inc(S("product"), 1)
                if i % 4 == 1 and i > 8:
                    ada_columns(i // 4 - 2)
            ada_columns(FT // 2 - 2)
            for j, (pn, k0, k1, t0) in enumerate(DOWN_UNITS):
                pe.wait_ge(S("w_low"), W_UNITS["down"] + j + 1)
                for t in (t0, t0 + 1):
                    if t == 7 and k0 == 0:
                        pe.wait_ge(S("h_done"), KD + 1)
                    for k in range(k0, k1):
                        if t == 0:
                            pe.wait_ge(S("hid_low"), k + 1)
                        w_high_k, w_low_k = (unit_weights(j, of)[:, k - k0, P * (t - t0):P * (t - t0) + P]
                                             for of in ("high", "low"))
                        for n, (w, x) in enumerate(((w_high_k, hidden_high(k)), (w_high_k, hid_low[:, k, :]),
                                                    (w_low_k, hidden_high(k)))):
                            ins = nc.tensor.matmul(banks[t % 7][:, :], w, x, start=k == 0 and n == 0,
                                                   stop=k == FT - 1 and n == 2)
                ins.then_inc(S("product"), 1)
                if j in (4, 5):
                    ada_columns(FT // 2 - 1 + j - 4)
            pe.wait_ge(S("mod_done"), 1)
            norm_sum("n3")

            pe.wait_ge(S("p_in"), 16)
            for t in range(KD):
                panel_here(pe, proj_panel)
                pe.wait_ge(S("w_low"), W_UNITS["ple"] + t // 2 + 1)
                if t >= 3:
                    pe.wait_ge(S("h_done"), 2 * KD + t - 2)
                square_product("ple", t, banks[2 * (t % 3)], lambda k: ple_x_high[:, k, :], lambda k: x_low[:, k, :],
                               both_parts(3 * KD))
                v = slot(proj_panel, D)
                product(banks[2 * (t % 3) + 1][:, :], lambda k: v[:, k, P * t:P * t + P],
                        lambda k: ple["pT"][:, k, :], 2).then_inc(S("product"), 1)
            norm_sum("n4")

            for i in range(9):
                if i == 0:
                    for k in range(KD):
                        normed("n4", k)
                    panel_here(pe, x_panel)
                    w = slot(x_panel, 416)
                    product(banks[0][0:SH, :], lambda k: w[:, k, 0:SH], lambda k: hn[:, k, :],
                            KD).then_inc(S("product"), 1)
                    continue
                pn, c, width = X_TILES[i - 1]
                panel_here(pe, pn)
                if i >= 6:
                    pe.wait_ge(S("x_copied"), i - 5)
                w = slot(pn, width)
                product(banks[i % 6][:, :], lambda k: w[:, k, c:c + P], lambda k: hn[:, k, :],
                        KD).then_inc(S("product"), 1)
            pe.wait_ge(S("dtp_done"), 1)
            pe.wait_ge(S("dtp_sums"), 1)
            for c in range(TT):
                ins = nc.tensor.transpose(banks[6][:, 96 * c:96 * c + 96], dtk["dtp"][0:96, c * P:(c + 1) * P],
                                          ident[0:96, 0:96])
            ins.then_inc(S("tok_ready"), 1)
            panel_here(pe, pool_panel)
            w = slot(pool_panel, 256)
            pe.wait_ge(S("x_copied"), 9)
            for t in range(KD):
                gi = t // 2
                pe.wait_ge(S("pooled"), 2 * gi + 2)
                if t >= 6:
                    pe.wait_ge(S("pool_out"), t - 5)
                product(banks[t % 6][:, :], lambda k: w[:, 2 * gi + k, P * (t % 2):P * (t % 2) + P],
                        lambda k: mix["pooled"][:, 2 * gi + k, :], 2).then_inc(S("product"), 1)

            def project(i):
                g, j = divmod(i, 6)
                if j < 4:
                    pn, width, c = ssd_panel + 2 * g, 512, P * j
                else:
                    pn, width, c = ssd_panel + 2 * g + 1, 256, P * (j - 4)
                panel_here(pe, pn)
                if i >= 2:
                    pe.wait_ge(*s_freed(i - 2))
                w = slot(pn, width)
                product(banks[i % 2][:, :], lambda k: w[:, k, c:c + P], lambda k: hn[:, k, :],
                        KD).then_inc(S("product"), 1)

            pe.wait_ge(S("pool_out"), KD)
            pe.wait_ge(S("tok_done"), 1)
            for i in range(6):
                project(i)
            def y_sum(g):
                if g >= 1:
                    pe.wait_ge(S("y_root"), g)
                for i in range(2):
                    pe.wait_ge(S("y_sq"), 2 * g + i + 1)
                    ins = nc.tensor.matmul(banks[7][:, :], const("ones_g"), sq[:, 2 * (g % 2) + i, :],
                                           start=i == 0, stop=i == 1)
                ins.then_inc(S("y_sum"), 1)

            for g in range(SG):
                s = g % 2
                pe.wait_ge(S("xbc_done"), 4 * g + 4)
                for c in range(TT):
                    n = TT * g + c
                    now = slice(c * P, (c + 1) * P)
                    if n >= 1:
                        pe.wait_ge(S("xtok_done"), n)
                    for i in range(2):
                        nc.tensor.transpose(banks[2][:, i * P:(i + 1) * P], ssd["xs"][:, 2 * s + i, now], ident)
                    nc.tensor.transpose(banks[2][:, 2 * P:3 * P], ssd["B"][:, s, now], ident)\
                      .then_inc(S("tr2_ready"), 1)
                    if n >= 1:
                        pe.wait_ge(S("CB_done"), n)
                    nc.tensor.matmul(banks[3][:, 0:P], ssd["B"][:, s, now], ssd["C"][:, s, now], start=True,
                                     stop=True).then_inc(S("CB_ready"), 1)
                    if n >= 1:
                        pe.wait_ge(S("L0_done"), HPG * n)
                    for j in range(HPG):
                        hd = HPG * g + j
                        ins = nc.tensor.matmul(banks[4][:, j * P:(j + 1) * P],
                                               ident[SH:2 * SH, SH + hd:SH + hd + 1].to_broadcast([SH, P]),
                                               dtk["dtp"][SH:2 * SH, now], start=True, stop=True)
                    ins.then_inc(S("cum_ready"), 1)
                    if g + 1 < SG:
                        for i in FILL[c]:
                            project(6 * (g + 1) + i)
                    pe.wait_ge(S("M_done"), n + 1)
                    if c == 0 and g >= 1:
                        pe.wait_ge(S("y_read"), 2 * g)
                    if c >= 1:
                        pe.wait_ge(S("state_done"), 3 * g + c)
                    for j in range(HPG):
                        out = banks[5 + j // 2][HD * (j % 2):HD * (j % 2) + HD, now]
                        ins = nc.tensor.matmul(out, ssd["xdt"][:, n % 2, j * HD:(j + 1) * HD],
                                               ssd["L"][:, n % 2, j * P:(j + 1) * P], start=True, stop=c == 0)
                        if c > 0:
                            ins = nc.tensor.matmul(out, ssd["state"][:, j * HD:(j + 1) * HD],
                                                   ssd["CE"][:, n % 2, j * P:(j + 1) * P], start=False, stop=True)
                    ins.then_inc(S("y_ready"), 1)
                    if c < TT - 1:
                        if 3 * g + c >= 1:
                            pe.wait_ge(S("state_done"), 3 * g + c)
                        nc.tensor.matmul(banks[7][:, 0:HPG * HD], ssd["xtok"][:, n % 2, 2 * P:3 * P],
                                         ssd["xdec"][:, n % 2, :], start=True, stop=True)\
                          .then_inc(S("st_ready"), 1)
            for i in (6 * SG - 2, 6 * SG - 1):
                pe.wait_ge(*s_freed(i))
            pe.wait_ge(S("state_done"), 3 * SG)
            pe.wait_ge(S("y_read"), 2 * SG)
            for t in range(16):
                pn = gts_panel + t // 4
                panel_here(pe, pn)
                if t >= 7:
                    pe.wait_ge(S("gs_copied"), t - 6)
                w = slot(pn, 512)
                product(banks[t % 7][:, :], lambda k: w[:, k, P * (t % 4):P * (t % 4) + P],
                        lambda k: hn[:, k, :], KD).then_inc(S("product"), 1)
                if t % 2 == 1:
                    y_sum(t // 2)
            pe.wait_ge(S("gs_copied"), 16)
            pe.wait_ge(S("y_root"), SG)
            pe.wait_ge(S("yn_done"), 2 * SG)
            for half in range(2):
                for kg in range(2):
                    pn = br_panel + 2 * half + kg
                    panel_here(pe, pn)
                    w = slot(pn, 512)
                    for i in range(4):
                        ins = product(banks[4 * half + i][:, :], lambda k: w[:, k, P * i:P * i + P],
                                      lambda k: mix["yn"][:, KD * kg + k, :], KD, kg == 0, kg == 1)
                    ins.then_inc(S("product"), 1)
            for t in range(KD):
                pe.wait_ge(S("w_low"), W_UNITS["pool_out"] + t // 2 + 1)
                pe.wait_ge(S("mixed"), t + 1)
                square_product("pool_out", t, banks[t], pooled_high_tile, lambda k: pooled_low[:, k, :],
                               lambda k: pe.wait_ge(S("pooled_low"), k + 1))
            pe.wait_ge(S("mixed"), 3 * KD)
            for t in range(KD):
                pe.wait_ge(S("w_low"), W_UNITS["wo2"] + t // 2 + 1)
                if t >= 7:
                    pe.wait_ge(S("h_done"), 3 * KD + t - 6)
                square_product("wo2", t, banks[t % 7], lambda k: mixed_high[:, k, :], lambda k: x_low[:, k, :],
                               both_parts(4 * KD))
            norm_sum("n5")

            panel_here(pe, router_panel)
            w = slot(router_panel, E)
            for k in range(KD):
                normed("n5", k)
            for tt in range(TT):
                product(banks[tt][:, 0:E], lambda k: hn[:, k, tt * P:(tt + 1) * P], lambda k: w[:, k, :],
                        KD).then_inc(S("product"), 1)

            def row_transposes(tt):
                for half in range(2):
                    bank = banks[4 + (2 * tt + half) % 4]
                    if tt >= 2:
                        pe.wait_ge(S("ut_done"), 2 * (tt - 2) + half + 1)
                    for q in range(4):
                        ins = nc.tensor.transpose(bank[:, q * P:(q + 1) * P], hn[:, 4 * half + q, tt * P:(tt + 1) * P],
                                                  ident)
                    ins.then_inc(S("ut_ready"), 1)

            def shared_up(tt):
                if tt >= 2:
                    pe.wait_ge(S("sh_up"), tt - 1)
                product(banks[tt % 2][:, :], lambda k: hn[:, k, tt * P:(tt + 1) * P], lambda k: moe["sgu"][:, k, :],
                        KD).then_inc(S("sh_gu"), 1)

            def shared_transposes(tt):
                pe.wait_ge(S("sh_hid"), tt + 1)
                if tt >= 1:
                    pe.wait_ge(S("sh_hT"), tt)
                for f in range(2):
                    ins = nc.tensor.transpose(banks[2][:, f * P:(f + 1) * P],
                                              moe["shid"][:, tt % 2, f * P:(f + 1) * P], ident)
                ins.then_inc(S("sh_ht"), 1)

            def shared_down(tt):
                pe.wait_ge(S("sh_hT"), tt + 1)
                for half in range(2):
                    if tt >= 2:
                        pe.wait_ge(S("y_copied"), 2 * (tt - 2) + half + 1)
                    else:
                        pe.wait_ge(S("ut_done"), 2 * TT)
                    product(banks[4 + (2 * tt + half) % 4][:, :], lambda k: moe["shT"][:, tt % 2, k * P:(k + 1) * P],
                            lambda k: moe["sdn"][:, k, 512 * half:512 * half + 512], 2).then_inc(S("sh_y"), 1)

            def counts():
                pe.wait_ge(S("selected"), TT)
                for tt in range(TT):
                    for before in range(tt + 1):
                        nc.tensor.matmul(banks[3][:, tt * E:(tt + 1) * E], ones if before < tt else const("before"),
                                         moe["sel"][:, before, :], start=before == 0, stop=before == tt)
                for tt in range(TT):
                    ins = nc.tensor.matmul(banks[3][:, TT * E:(TT + 1) * E], ones, moe["sel"][:, tt, :], start=tt == 0,
                                           stop=tt == TT - 1)
                ins.then_inc(S("counted"), 1)

            for tt in range(TT):
                row_transposes(tt)
            pe.wait_ge(S("sc_done"), TT)
            pe.wait_ge(S("shared_in"), 48)
            shared_up(0)
            shared_up(1)
            shared_transposes(0)
            shared_up(2)
            shared_down(0)
            shared_transposes(1)
            shared_up(3)
            shared_down(1)
            counts()
            for tt in (2, 3):
                shared_transposes(tt)
                shared_down(tt)
            pe.wait_ge(S("ebcol_done"), 1)
            nc.tensor.matmul(banks[3][0:1, 384:512], moe["ebcol"][:, 0:1], ident, start=True, stop=True)\
              .then_inc(S("eb_ready"), 1)
            pe.wait_ge(S("sh_hT"), TT)
            for n in range(TT * TOP):
                pe.wait_ge(S("OHs_done"), n + 1)
                pe.wait_ge(S("OHb_done"), 3 * n + 3)
                nc.tensor.matmul(banks[2][:, 0:3 * MAX_BLOCKS], moe["OHs"][:, n % 4, :], moe["OHb"][:, n % 4, :],
                                 start=n == 0, stop=n == TT * TOP - 1).then_inc(S("table_part"), 1)

            def block_transposes(b, p, gathers):
                pe.wait_ge(S(f"x_gathered{p}"), gathers * 16)
                for half in range(2):
                    for q in range(4):
                        c = (4 * half + q) * P
                        ins = nc.tensor.transpose(banks[half][:, q * P:(q + 1) * P], moe["X"][:, p, c:c + P], ident)
                    ins.then_inc(S("moe_tr"), 1)

            def block_up(b, p, loads):
                pe.wait_ge(S("xT_done"), b * 2 + 2)
                pe.wait_ge(S(f"up_in{p}"), loads * 32)
                product(banks[2 + p][:, :], lambda k: moe["xT"][:, p, k * P:(k + 1) * P],
                        lambda k: moe["gu"][:, p, k * 512:(k + 1) * 512], KD).then_inc(S("moe_gu"), 1)

            def hidden_transposes(b, p):
                pe.wait_ge(S("moe_hid"), b + 1)
                for f in range(2):
                    ins = nc.tensor.transpose(banks[4][:, f * P:(f + 1) * P], moe["hid"][:, p, f * P:(f + 1) * P],
                                              ident)
                ins.then_inc(S("moe_ht"), 1)

            def block_down(b, p, loads):
                pe.wait_ge(S("hT_done"), b + 1)
                pe.wait_ge(S(f"down_in{p}"), loads * 16)
                for half in range(2):
                    pe.wait_ge(S("y_copied"), b * 2 + (2 * TT + half - 1))
                    product(banks[5 + half][:, :], lambda k: moe["hidT"][:, p, k * P:(k + 1) * P],
                            lambda k: moe["dn"][:, p, k * D + 512 * half:k * D + 512 * half + 512], 2)\
                        .then_inc(S("moe_y"), 1)

            pe.wait_ge(S("blocks_known"), 2)
            pairs_but_one = pe.value_load(expert_of[0:1, MAX_BLOCKS:MAX_BLOCKS + 1], min_val=TT * TOP // 2 - 1,
                                            max_val=MAX_BLOCKS // 2 - 1)
            pairs = pairs_but_one + 1
            block_transposes(0, 0, 1)
            pe.wait_ge(S("xT_done"), 2)
            block_transposes(1, 1, 1)
            block_up(0, 0, 1)
            with pe.Fori(1, pairs) as i:
                for b, p, loads, next_gathers, last_loads in ((i * 2 + (-1), 1, i, i + 1, i),
                                                              (i * 2, 0, i + 1, i + 1, i)):
                    hidden_transposes(b + (-1), 1 - p)
                    pe.wait_ge(S("xT_done"), b * 2 + 2)
                    block_transposes(b + 1, 1 - p, next_gathers)
                    block_up(b, p, loads)
                    block_down(b + (-1), 1 - p, last_loads)
            hidden_transposes(pairs_but_one * 2, 0)
            block_up(pairs_but_one * 2 + 1, 1, pairs)
            block_down(pairs_but_one * 2, 0, pairs)
            hidden_transposes(pairs_but_one * 2 + 1, 1)
            block_down(pairs_but_one * 2 + 1, 1, pairs)

            pe.wait_ge(S("acc_in"), 16)
            for d in range(KD):
                if d >= 7:
                    pe.wait_ge(S("h_done"), 4 * KD + d - 6)
                for tt in range(TT):
                    ins = nc.tensor.transpose(banks[d % 7][:, tt * P:(tt + 1) * P], acc[:, tt, d * P:(d + 1) * P], ident)
                ins.then_inc(S("acc_T"), 1)
            norm_sum("n6")

        @block.scalar
        def _(act):
            def root(out, bank):
                return nc.scalar.activation(out, bank[:, :], ACT.Sqrt, bias=EPS_COLUMN)

            def squares(name, ready):
                for k in range(KD):
                    act.wait_ge(*ready(k))
                    if k >= 4:
                        act.wait_ge(S("norm_sum"), KD * NORMS[name] + k - 3)
                    nc.scalar.activation(sq[:, k % 4, :], h[:, k, :], ACT.Square).then_inc(S("norm_sq"), 1)
                act.wait_ge(S("norm_sum"), KD * NORMS[name] + KD)
                root(inv[:, 0, :], banks[NORM]).then_inc(S("norm_root"), 1)

            def shifted(name, first):
                for k in range(KD):
                    act.wait_ge(S("norm_mul"), KD * (NORMS[name] - NORMS["n4"]) + k + 1)
                    nc.scalar.activation(hn[:, k, :], hn[:, k, :], ACT.Identity,
                                         bias=mod[:, first + k:first + k + 1]).then_inc(S("norm_out"), 1)

            act.wait_ge(S("cols_in"), 16)
            act.wait_ge(S("shp_in"), 16)
            squares("n1", lambda k: (S(f"x_in{k // 2}"), 16))
            z_panel_end = [max(t for t, g in enumerate(Z_GROUPS) if g[1] == pn) + 1 for pn in range(len(Z_PANELS))]

            def z_high_part(pn):
                if pn < len(Z_PANELS):
                    panel_here(act, pn)
                    if pn >= 2:
                        act.wait_ge(S("product"), PRODUCTS["z"] + z_panel_end[pn - 2])
                    nc.scalar.activation(z_weights(pn, "high"), z_weights(pn, "whole"), ACT.Copy)\
                      .then_inc(S("w_high"), 1)

            def rounded_tiles(name, out):
                for k in range(KD):
                    act.wait_ge(S("norm_out"), KD * NORMS[name] + k + 1)
                    nc.scalar.activation(out[:, k, :], hn[:, k, :], ACT.Copy).then_inc(S("x_high"), 1)

            z_high_part(0)
            z_high_part(1)
            rounded_tiles("n1", z_x_high)
            act.wait_ge(S("prepared"), PREPARED["lam_dot"] + 2)
            nc.scalar.activation(LAM_EXP, LAM_DOT, ACT.Exp).then_inc(S("lam_exp"), 1)
            j = rooted = 0

            def head_root():
                nonlocal rooted
                if rooted < j:
                    act.wait_ge(S("qk_sum"), rooted + 1)
                    if rooted >= 2:
                        act.wait_ge(S("qk_done"), rooted - 1)
                    root(inv[:, rooted % 2, :], banks[6 + rooted % 2]).then_inc(S("qk_root"), 1)
                    rooted += 1

            for t, (kind, pn, c, width) in enumerate(Z_GROUPS):
                if pn >= 1 and t == z_panel_end[pn - 1]:
                    z_high_part(pn + 1)
                act.wait_ge(S("product"), PRODUCTS["z"] + t + 1)
                bank = banks[t % 6]
                if kind == "qk":
                    if j >= 4:
                        act.wait_ge(S("qk_sum"), j - 3)
                    nc.scalar.activation(sq[:, j % 4, :], bank[:, :], ACT.Square).then_inc(S("qk_sq"), 1)
                    head_root()
                    j += 1
                    continue
                head_root()
                if kind == "v":
                    v0 = V_PANELS[pn][0]
                    nc.scalar.activation(att["V"][:, c, v0:v0 + width], bank[:, 0:width], ACT.Copy)\
                      .then_inc(S("v_done"), 1)
                else:
                    nc.scalar.activation(fgt["x"][0:N_FOX, :], bank[0:N_FOX, :], ACT.Identity,
                                         bias=col("fgate")[0:N_FOX, :]).then_inc(S("v_done"), 1)
                    act.wait_ge(S("v_done"), 3 * TT + 1)
                    nc.scalar.activation(fgt["l"][0:N_FOX, :], fgt["x"][0:N_FOX, :], ACT.Abs)\
                      .then_inc(S("act_step"), 1)
                    act.wait_ge(S("act_step"), 1)
                    nc.scalar.activation(fgt["l"][0:N_FOX, :], fgt["l"][0:N_FOX, :], ACT.Exp, scale=-1.0)\
                      .then_inc(S("act_step"), 1)
                    act.wait_ge(S("act_step"), 2)
                    nc.scalar.activation(fgt["l"][0:N_FOX, :], fgt["l"][0:N_FOX, :], ACT.Ln, bias=1.0)\
                      .then_inc(S("fg_ln"), 1)

            def exponentials(u):
                hh, qt, first, n = UNITS[u]
                for m in range(first, first + n):
                    act.wait_ge(S("t_done"), m + 1)
                    buf = att["t"][:, m % 4, 0:P * (qt + 1)]
                    nc.scalar.activation(buf, buf, ACT.Exp, bias=NEG_MAX[:, m:m + 1], scale=-1.0,
                                         accum_out=ROW_SUM[:, m:m + 1]).then_inc(S("e_done"), 1)

            def transposed(u):
                hh, qt, _, _ = UNITS[u]
                act.wait_ge(S("tr_ready"), u + 1)
                if hh >= 2:
                    act.wait_ge(S("o_ready"), hh - 1)
                nc.scalar.activation(PT[hh % 2][:, 0:qt + 1, qt * P:(qt + 1) * P],
                                     banks[4 + u % 2][:, 0:(qt + 1) * P].rearrange("p (k q) -> p k q", q=P),
                                     ACT.Copy).then_inc(S("pt_done"), 1)

            def head_out(hh):
                act.wait_ge(S("o_ready"), hh + 1)
                r = HD * (hh % 2)
                nc.scalar.activation(hn[r:r + HD, hh // 2, :], banks[6 + hh % 2][0:HD, :], ACT.Copy)\
                  .then_inc(S("o_done"), 1)

            for u in range(len(UNITS) + 3):
                if u < len(UNITS):
                    exponentials(u)
                if 2 <= u < len(UNITS) + 2:
                    transposed(u - 2)
                if u >= 3 and (u - 3) % 4 == 3:
                    head_out((u - 3) // 4)
            def high_weights(name, u, *free):
                if u % 2 == 0:
                    panel_here(act, {"wo": wo_panel, "ple": gate_panel, "pool_out": bp_panel, "wo2": wo2_panel}[name] + u // 2)
                if free:
                    act.wait_ge(*free)
                nc.scalar.activation(square_weights(name, u, "high"), square_weights(name, u, "whole"), ACT.Copy)\
                  .then_inc(S("w_high"), 1)

            for i in range(2):
                act.wait_ge(S("o_done"), HEADS)
                nc.scalar.activation(sq[:, i, :], hn[:, i, :], ACT.Square).then_inc(S("qk_sq"), 1)
            high_weights("wo", 0)
            for i in range(2):
                act.wait_ge(S("qk_sum"), N_QK + i + 1)
                root(inv[:, i, :], banks[i]).then_inc(S("qk_root"), 1)

            def high_part(pair):
                panel_here(act, up_panels[pair // 2])
                if pair >= 2:
                    act.wait_ge(S("product"), PRODUCTS["up"] + 2 * (pair - 1))
                nc.scalar.activation(up_high(pair), up_columns(pair, slot(up_panels[pair // 2], 512)), ACT.Copy)\
                  .then_inc(S("w_high"), 1)

            high_weights("wo", 1)
            for k in range(2, KD + 2):
                if k >= KD:
                    act.wait_ge(S("qk_done"), N_QK + k - KD + 1)
                nc.scalar.activation(wo_x_high[:, k % KD, :], hn[:, k % KD, :], ACT.Copy).then_inc(S("x_high"), 1)
            for u in (2, 3):
                high_weights("wo", u, S("product"), PRODUCTS["wo"] + 2 * u - 2)
            act.wait_ge(S("product"), PRODUCTS["wo"] + 1)
            high_part(0)
            squares("n2", lambda k: (S("h_done"), k + 1))
            high_part(1)
            rounded_tiles("n2", x_high)
            nc.scalar.activation(C_ACT, col("c", 0, KD), ACT.Silu).then_inc(S("c_act"), 1)

            def gate(p):
                act.wait_ge(S("taps"), 2 * (2 * p) + 2)
                if p >= 2:
                    act.wait_ge(S("hid_done"), p - 1)
                nc.scalar.activation(ffn["sg"][:, p % 2, :], ffn["cv"][:, 2 * (p % 3), :], ACT.Silu)\
                  .then_inc(S("sg_done"), 1)

            for p in range(FT):
                for part in range(2):
                    i = 2 * p + part
                    act.wait_ge(S("product"), PRODUCTS["up"] + i + 1)
                    if p >= 3:
                        act.wait_ge(S("hid_done"), p - 2)
                    ch = FT * part + p
                    nc.scalar.activation(ffn["cv"][:, i % 6, :], banks[i % 6][:, :], ACT.Identity,
                                         scale=col("conv_w", 2 * 2 * FT + ch), bias=col("conv_b", ch))\
                      .then_inc(S("tap2"), 1)
                if p >= 1:
                    gate(p - 1)
                if p + 2 < FT:
                    high_part(p + 2)

            def unit_high(j):
                if j % 2 == 0:
                    panel_here(act, DOWN_UNITS[j][0])
                act.wait_ge(S("product"), PRODUCTS["down"] + max(j - 1, 0))
                nc.scalar.activation(unit_weights(j, "high"), unit_weights(j, "whole"), ACT.Copy)\
                  .then_inc(S("w_high"), 1)

            def hidden_parts(k0, k1):
                for k in range(k0, k1):
                    act.wait_ge(S("hid_done"), FT)
                    nc.scalar.activation(hidden_high(k), ffn["hid"][:, k, :], ACT.Copy).then_inc(S("hid_high"), 1)

            unit_high(0)
            gate(FT - 1)
            hidden_parts(0, 8)
            unit_high(1)
            hidden_parts(8, FT)
            for j in range(2, len(DOWN_UNITS)):
                unit_high(j)

            squares("n3", lambda k: (S("h_done"), KD + k + 1))
            high_weights("ple", 0)
            high_weights("ple", 1)
            rounded_tiles("n3", ple_x_high)
            for t in range(KD):
                if t in (2, 4):
                    high_weights("ple", t // 2 + 1, S("product"), PRODUCTS["ple"] + 2 * t)
                act.wait_ge(S("product"), PRODUCTS["ple"] + 2 * t + 1)
                if t >= 2:
                    act.wait_ge(S("ple_mul"), t - 1)
                nc.scalar.activation(ple["gt"][:, t % 2, :], banks[2 * (t % 3)][:, :], ACT.Sigmoid)\
                  .then_inc(S("gt_done"), 1)
            squares("n4", lambda k: (S("h_done"), 2 * KD + k + 1))
            shifted("n4", 0)

            nc.scalar.activation(EXP_A, col("A_log")[0:SH, :], ACT.Exp).then_inc(S("expA"), 1)
            act.wait_ge(S("product"), PRODUCTS["x"] + 1)
            nc.scalar.activation(pool["raw"][0:SH, :], banks[0][0:SH, :], ACT.Identity,
                                 bias=col("dt_bias")[0:SH, :]).then_inc(S("x_copied"), 1)
            act.wait_ge(S("x_copied"), 1)
            nc.scalar.activation(pool["ab"][0:SH, :], pool["raw"][0:SH, :], ACT.Abs).then_inc(S("act_step"), 1)
            act.wait_ge(S("act_step"), 3)
            nc.scalar.activation(pool["l"][0:SH, :], pool["ab"][0:SH, :], ACT.Exp, scale=-1.0)\
              .then_inc(S("act_step"), 1)
            act.wait_ge(S("act_step"), 4)
            nc.scalar.activation(pool["ab"][0:SH, :], pool["l"][0:SH, :], ACT.Ln, bias=1.0)\
              .then_inc(S("dt_ln"), 1)
            act.wait_ge(S("pads"), 2)
            for i in range(1, 9):
                act.wait_ge(S("product"), PRODUCTS["x"] + i + 1)
                if i >= 3:
                    act.wait_ge(S("pooled"), i - 2)
                nc.scalar.activation(pool["x"][:, (i - 1) % 2, PAD:PAD + T], banks[i % 6][:, :], ACT.Copy)\
                  .then_inc(S("x_copied"), 1)
            act.wait_ge(S("dec_arg"), TT)
            nc.scalar.activation(dtk["dtp"][2 * SH:3 * SH, :], pool["a"][0:SH, :], ACT.Exp, scale=-1.0)\
              .then_inc(S("dtp_done"), 1)
            act.wait_ge(S("tok_ready"), 1)
            nc.scalar.activation(dtk["tok"], banks[6][:, 0:TT * 96].rearrange("p (c n) -> p c n", n=96),
                                 ACT.Copy).then_inc(S("tok_done"), 1)
            for t in range(KD):
                act.wait_ge(S("product"), PRODUCTS["pool"] + t + 1)
                act.wait_ge(S("product"), PRODUCTS["pool"] + 2 * (t // 2) + 2)
                nc.scalar.activation(mix["pooled"][:, t, :], banks[t % 6][:, :], ACT.Copy,
                                     scale=col("pool_scale", t)).then_inc(S("pool_out"), 1)

            waiting = []

            def xbc_silu():
                i, buf = waiting.pop(0)
                q = 4 * (i // 6) + i % 6 - 2
                act.wait_ge(*s_freed(i))
                if q >= 2:
                    act.wait_ge(S("xbc_done"), q - 1)
                nc.scalar.activation(ssd["th"][:, q % 2, :], buf, ACT.Tanh).then_inc(S("th_done"), 1)

            def read_tile(i):
                g, j = divmod(i, 6)
                s = g % 2
                act.wait_ge(S("product"), PRODUCTS["ssd"] + i + 1)
                if g >= 2:
                    act.wait_ge(S("y_gated"), 2 * (g - 1))
                if j < 2:
                    nc.scalar.activation(ssd["zs"][:, 2 * s + j, :], banks[i % 2][:, :], ACT.Tanh,
                                         scale=0.5).then_inc(S("z_tanh"), 1)
                    return
                ch = {2: 2 * g, 3: 2 * g + 1, 4: 16 + g, 5: 24 + g}[j]
                buf = {2: ssd["xs"][:, 2 * s, :], 3: ssd["xs"][:, 2 * s + 1, :], 4: ssd["B"][:, s, :],
                       5: ssd["C"][:, s, :]}[j]
                nc.scalar.activation(buf, banks[i % 2][:, :], ACT.Identity, scale=col("conv_w2", 3 * 32 + ch),
                                     bias=col("conv_b2", ch)).then_inc(S("s_tap3"), 1)
                if waiting:
                    xbc_silu()
                waiting.append((i, buf))

            act.wait_ge(S("prepared"), PREPARED["halved"] + 1)
            for i in range(6):
                read_tile(i)
            xbc_silu()
            for g in range(SG):
                for c in range(TT):
                    n = TT * g + c
                    act.wait_ge(S("tr2_ready"), n + 1)
                    if n >= 2:
                        act.wait_ge(S("st_ready"), 3 * ((n - 2) // TT) + min((n - 2) % TT + 1, TT - 1))
                        act.wait_ge(S("xdec_done"), n - 1)
                    nc.scalar.activation(ssd["xtok"][:, n % 2, :], banks[2][:, 0:3 * P], ACT.Copy)\
                      .then_inc(S("xtok_done"), 1)
                    act.wait_ge(S("cum_ready"), n + 1)
                    if n >= 2:
                        act.wait_ge(S("CE_done"), n - 1)
                        act.wait_ge(S("state_done"), 3 * ((n - 2) // TT) + min((n - 2) % TT + 1, TT - 1))
                    nc.scalar.activation(ssd["Ex"][:, n % 2, :], banks[4][:, :], ACT.Exp).then_inc(S("Ex_done"), 1)
                    act.wait_ge(S("L0_done"), HPG * (n + 1))
                    nc.scalar.activation(ssd["L"][:, n % 2, :], ssd["L"][:, n % 2, :], ACT.Exp)\
                      .then_inc(S("L_done"), 1)
                    if g + 1 < SG:
                        for i in FILL[c]:
                            read_tile(6 * (g + 1) + i)
                        if c == TT - 1:
                            xbc_silu()

            for g in range(SG):
                for i in range(2):
                    act.wait_ge(S("y_gated"), 2 * g + i + 1)
                    if g >= 2:
                        act.wait_ge(S("y_sum"), g - 1)
                    nc.scalar.activation(sq[:, 2 * (g % 2) + i, :], mix["yn"][:, 2 * g + i, :], ACT.Square)\
                      .then_inc(S("y_sq"), 1)
                for t in (2 * g, 2 * g + 1):
                    act.wait_ge(S("product"), PRODUCTS["gates"] + t + 1)
                    act.wait_ge(S("y_gated"), 2 * SG)
                    nc.scalar.activation(late["gs"][:, t, :], banks[t % 7][:, :], ACT.Copy)\
                      .then_inc(S("gs_copied"), 1)
                act.wait_ge(S("y_sum"), g + 1)
                if g >= 2:
                    act.wait_ge(S("yn_done"), 2 * (g - 1))
                root(inv[:, g % 2, :], banks[7]).then_inc(S("y_root"), 1)
            act.wait_ge(S("yn_done"), 2 * SG)
            for k in range(KD):
                nc.scalar.activation(pooled_high_tile(k), mix["pooled"][:, k, :], ACT.Copy)\
                  .then_inc(S("pooled_high"), 1)
            high_weights("pool_out", 0)
            for t in range(16):
                act.wait_ge(S("gs_copied"), t + 1)
                nc.scalar.activation(late["gs"][:, t, :], late["gs"][:, t, :], ACT.Sigmoid).then_inc(S("gs_done"), 1)
            high_weights("pool_out", 1, S("product"), PRODUCTS["ssd_out"] + 4)
            for u in (2, 3):
                high_weights("pool_out", u, S("product"), PRODUCTS["pool_out"] + 2 * u - 2)
            for u in (0, 1):
                high_weights("wo2", u, S("product"), PRODUCTS["pool_out"] + 2 * u + 6)
            for k in range(KD):
                act.wait_ge(S("mixed"), KD + 2 * k + 2)
                nc.scalar.activation(mixed_high[:, k, :], hn[:, k, :], ACT.Copy).then_inc(S("x_high"), 1)
            for u in (2, 3):
                high_weights("wo2", u, S("product"), PRODUCTS["wo2"] + 2 * u - 2)
            squares("n5", lambda k: (S("h_done"), 3 * KD + k + 1))
            shifted("n5", 3 * KD)

            for tt in range(TT):
                act.wait_ge(S("product"), PRODUCTS["router"] + TT)
                nc.scalar.activation(moe["sc"][:, tt, :], banks[tt][:, 0:E], ACT.Sigmoid).then_inc(S("sc_done"), 1)

            for tt in range(TT):
                for half in range(2):
                    act.wait_ge(S("ut_ready"), 2 * tt + half + 1)
                    nc.scalar.activation(moe["ut"][:, tt, 512 * half:512 * half + 512],
                                         banks[4 + (2 * tt + half) % 4][:, :], ACT.Copy).then_inc(S("ut_done"), 1)
                act.wait_ge(S("ut_done"), 2 * tt + 2)
                act.dma_start(u_rows[tt * P:(tt + 1) * P, :], moe["ut"][:, tt, :]).then_inc(S("u_stored"), 16)

            def shared_gate(tt):
                act.wait_ge(S("sh_gu"), tt + 1)
                if tt >= 2:
                    act.wait_ge(S("sh_hid"), tt - 1)
                nc.scalar.activation(moe["ssg"][:, tt % 2, :], banks[tt % 2][:, 0:FE], ACT.Silu).then_inc(S("sh_sg"), 1)
                nc.scalar.activation(moe["sup"][:, tt % 2, :], banks[tt % 2][:, FE:2 * FE], ACT.Copy)\
                  .then_inc(S("sh_up"), 1)

            def shared_hidden(tt):
                act.wait_ge(S("sh_ht"), tt + 1)
                if tt >= 2:
                    act.wait_ge(S("sh_y"), 2 * (tt - 1))
                nc.scalar.activation(moe["shT"][:, tt % 2, :], banks[2][:, 0:2 * P], ACT.Copy).then_inc(S("sh_hT"), 1)

            def shared_out(tt):
                if tt >= 2:
                    act.wait_ge(S(f"shared_stored{tt % 2}"), 16)
                for half in range(2):
                    act.wait_ge(S("sh_y"), 2 * tt + half + 1)
                    nc.scalar.activation(moe["sy"][:, tt % 2, 512 * half:512 * half + 512],
                                         banks[4 + (2 * tt + half) % 4][:, :], ACT.Copy).then_inc(S("y_copied"), 1)
                act.wait_ge(S("y_copied"), 2 * tt + 2)
                act.dma_start(y_rows[tt * P:(tt + 1) * P, :], moe["sy"][:, tt % 2, :])\
                   .then_inc(S(f"shared_stored{tt % 2}"), 16)

            shared_gate(0)
            shared_gate(1)
            shared_hidden(0)
            shared_gate(2)
            shared_out(0)
            shared_hidden(1)
            shared_gate(3)
            shared_out(1)
            for tt in (2, 3):
                shared_hidden(tt)
                shared_out(tt)

            def block_rows(b, p):
                for half in range(2):
                    act.wait_ge(S("moe_tr"), b * 2 + (half + 1))
                    nc.scalar.activation(moe["xT"][:, p, 512 * half:512 * half + 512], banks[half][:, :], ACT.Copy)\
                      .then_inc(S("xT_done"), 1)

            def block_gate(b, p):
                act.wait_ge(S("moe_gu"), b + 1)
                nc.scalar.activation(moe["sg"][:, p, :], banks[2 + p][:, 0:FE], ACT.Silu).then_inc(S("moe_sg"), 1)

            act.wait_ge(S("blocks_known"), 2)
            pairs_but_one = act.value_load(expert_of[0:1, MAX_BLOCKS:MAX_BLOCKS + 1], min_val=TT * TOP // 2 - 1,
                                            max_val=MAX_BLOCKS // 2 - 1)
            pairs = pairs_but_one + 1
            block_rows(0, 0)
            block_rows(1, 1)
            block_gate(0, 0)
            with act.Fori(1, pairs) as i:
                for b, p in ((i * 2 + (-1), 1), (i * 2, 0)):
                    block_rows(b + 1, 1 - p)
                    block_gate(b, p)
            block_gate(pairs_but_one * 2 + 1, 1)
            squares("n6", lambda k: (S("h_done"), 4 * KD + k + 1))

        @block.vector
        def _(dve):
            steps = 0

            def counted_step(ins):
                nonlocal steps
                steps += 1
                ins.then_inc(S("vector_step"), 1)

            def steps_done():
                dve.wait_ge(S("vector_step"), steps)

            def step(ins):
                counted_step(ins)
                steps_done()

            def apply_norm(name, gain, done):
                dve.wait_ge(S("norm_root"), NORMS[name] + 1)
                nc.vector.reciprocal(inv[:, 0, :], inv[:, 0, :]).then_inc(S("norm_inv"), 1)
                dve.wait_ge(S("norm_inv"), NORMS[name] + 1)
                for k in range(KD):
                    nc.vector.scalar_tensor_tensor(hn[:, k, :], h[:, k, :], gain(k), inv[:, 0, :], ALU.mult,
                                                   ALU.mult).then_inc(S("norm_" + done), 1)

            def low_parts(high, first):
                for k in range(KD):
                    dve.wait_ge(S("x_high"), first + k + 1)
                    nc.vector.tensor_tensor(x_low[:, k, :], hn[:, k, :], high[:, k, :].bitcast(f32), ALU.subtract)\
                      .then_inc(S("x_low"), 1)

            dve.wait_ge(S("cols_in"), 16)
            nc.vector.tensor_scalar(col("conv_w2", 0, 5 * 32), col("conv_w2", 0, 5 * 32), 0.5, None, ALU.mult)\
              .then_inc(S("prepared"), 1)
            for i in range(2):
                nc.vector.tensor_tensor_reduce(out=inv[:, 1, 64 * i:64 * i + 64], in0=col("lam", 128 * i, 64),
                                               in1=col("lam", 128 * i + 64, 64), scale=1.0, scalar=0.0,
                                               op0=ALU.mult, op1=ALU.add, accum_out=LAM_DOT[:, i:i + 1])\
                  .then_inc(S("prepared"), 1)
            nc.vector.tensor_scalar(SUBLN, col("subln"), 1.0 - LAM_INIT, None, ALU.mult).then_inc(S("prepared"), 1)
            apply_norm("n1", lambda k: col("ln_mix", k), "out")
            low_parts(z_x_high, 0)
            dve.wait_ge(S("lam_exp"), 1)
            nc.vector.tensor_scalar(NEG_LAM, LAM_EXP[:, 1:2], LAM_EXP[:, 0:1], LAM_INIT, ALU.subtract,
                                    ALU.subtract).then_inc(S("prepared"), 1)
            j = 0
            for t, (kind, *_) in enumerate(Z_GROUPS):
                if kind == "qk":
                    dve.wait_ge(S("qk_root"), j + 1)
                    nc.vector.reciprocal(inv[:, j % 2, :], inv[:, j % 2, :]).then_inc(S("qk_inv"), 1)
                    dve.wait_ge(S("qk_inv"), j + 1)
                    nc.vector.scalar_tensor_tensor(att["qk"][:, j, :], banks[t % 6][:, :],
                                                   col("qk_gain", QK_GAIN[j]), inv[:, j % 2, :], ALU.mult,
                                                   ALU.mult).then_inc(S("qk_done"), 1)
                    j += 1
                if kind == "fg":
                    dve.wait_ge(S("fg_ln"), 1)
                    x, l = fgt["x"][0:N_FOX, :], fgt["l"][0:N_FOX, :]
                    step(nc.vector.scalar_tensor_tensor(x, x, 0.0, l, ALU.min, ALU.subtract))
                    step(nc.vector.tensor_tensor_scan(l, ones[0:N_FOX, 0:1].to_broadcast([N_FOX, T]), x, 0.0, ALU.mult,
                                                      ALU.add))
                    nc.vector.tensor_scalar(att["F8"][0:N_FOX, :], l, -8.0, None, ALU.mult)\
                      .then_inc(S("F_done"), 1)

            dve.wait_ge(S("shp_in"), 16)
            dve.wait_ge(S("product"), PRODUCTS["z"] + len(Z_GROUPS))
            for i in range(N_DIFF):
                nc.vector.tensor_scalar(att["tab_diff"][:, i, :], const("dist"), 8.0 * 2.0 ** (-2.0 * (i + 1)), None,
                                        ALU.mult).then_inc(S("prepared"), 1)
            dve.wait_ge(S("prepared"), PREPARED["tables"] + N_DIFF)

            def chunk_tables():
                dve.wait_ge(S("rel_in"), 16 * N_CHUNK)
                for f in range(N_CHUNK):
                    tab = att["tab_chunk"][:, f, :]
                    nc.vector.scalar_tensor_tensor(tab, tab, 8.0, const("chunked"), ALU.mult, ALU.add)\
                      .then_inc(S("prepared"), 1)
                dve.wait_ge(S("prepared"), PREPARED["tables"] + N_DIFF + N_CHUNK)

            def logits(u):
                hh, qt, first, n = UNITS[u]
                W = P * (qt + 1)
                if hh == N_DIFF and qt == 0:
                    chunk_tables()
                for m in range(first, first + n):
                    dve.wait_ge(S("s_scores"), m + 1)
                    if m >= 4:
                        dve.wait_ge(S("probs_done"), UNIT_OF[m - 4] + 1)
                    nc.vector.tensor_tensor_reduce(out=att["t"][:, m % 4, 0:W], in0=banks[m % 4][:, 0:W],
                                                   in1=table(hh, qt), scale=-0.125, scalar=3.0e38, op0=ALU.add,
                                                   op1=ALU.min, accum_out=NEG_MAX[:, m:m + 1])\
                      .then_inc(S("t_done"), 1)

            def probabilities(u):
                hh, qt, m, n = UNITS[u]
                W = P * (qt + 1)
                r = RECIP[:, 2 * (u % 2):2 * (u % 2) + n]
                out = NORMED[:, u % 2, 0:W]
                dve.wait_ge(S("e_done"), m + n)
                step(nc.vector.reciprocal(r, ROW_SUM[:, m:m + n]))
                if u >= 2:
                    dve.wait_ge(S("tr_ready"), u - 1)
                if n == 1:
                    nc.vector.tensor_scalar(out, att["t"][:, m % 4, 0:W], r, None, ALU.mult)\
                      .then_inc(S("probs_done"), 1)
                    return
                step(nc.vector.tensor_scalar(r[:, 1:2], r[:, 1:2], NEG_LAM, None, ALU.mult))
                step(nc.vector.tensor_scalar(out, att["t"][:, m % 4, 0:W], r[:, 0:1], None, ALU.mult))
                nc.vector.scalar_tensor_tensor(out, att["t"][:, (m + 1) % 4, 0:W], r[:, 1:2], out, ALU.mult,
                                               ALU.add).then_inc(S("probs_done"), 1)

            dve.wait_ge(S("prepared"), PREPARED["neg_lam"] + 1)
            for u in range(len(UNITS) + 1):
                if u < len(UNITS):
                    logits(u)
                if u >= 1:
                    probabilities(u - 1)
            dve.wait_ge(S("prepared"), PREPARED["subln"] + 1)
            for i in range(2):
                dve.wait_ge(S("qk_root"), N_QK + i + 1)
                nc.vector.reciprocal(inv[:, i, :], inv[:, i, :]).then_inc(S("qk_inv"), 1)
                dve.wait_ge(S("qk_inv"), N_QK + i + 1)
                nc.vector.scalar_tensor_tensor(hn[:, i, :], hn[:, i, :], SUBLN, inv[:, i, :], ALU.mult, ALU.mult)\
                  .then_inc(S("qk_done"), 1)
            for n in range(KD):
                k = (n + 2) % KD
                dve.wait_ge(S("x_high"), KD + n + 1)
                nc.vector.tensor_tensor(x_low[:, k, :], hn[:, k, :], wo_x_high[:, k, :].bitcast(f32), ALU.subtract)\
                  .then_inc(S("x_low"), 1)
            for t in range(KD):
                dve.wait_ge(S("product"), PRODUCTS["wo"] + t + 1)
                nc.vector.tensor_tensor(h[:, t, :], h[:, t, :], banks[t % 7][:, :], ALU.add).then_inc(S("h_done"), 1)
            apply_norm("n2", lambda k: col("ln_ffn", k), "out")
            low_parts(x_high, 2 * KD)

            def ada_rows(m):
                panel_here(dve, ada_panels[m])
                if m >= 2:
                    dve.wait_ge(S("ada_columns"), m - 1)
                w = slot(ada_panels[m], 512)
                out = ffn["ada"][:, m % 2, :]
                for k in range(KD):
                    if k == 0:
                        ins = nc.vector.tensor_scalar(out, w[:, k, :], C_ACT[:, 0:1], None, ALU.mult)
                    else:
                        ins = nc.vector.scalar_tensor_tensor(out, w[:, k, :], C_ACT[:, k:k + 1], out, ALU.mult,
                                                             ALU.add)
                    ins.then_inc(S("ada_sum"), 1)
                    dve.wait_ge(S("ada_sum"), KD * m + k + 1)

            dve.wait_ge(S("c_act"), 1)
            for i in range(2 * FT):
                p, part = divmod(i, 2)
                ch = FT * part + p
                cv, u = ffn["cv"][:, i % 6, :], banks[i % 6]
                dve.wait_ge(S("tap2"), i + 1)
                for back in (1, 2):
                    nc.vector.scalar_tensor_tensor(cv[:, back:T], u[:, 0:T - back],
                                                   col("conv_w", (2 - back) * 2 * FT + ch), cv[:, back:T],
                                                   ALU.mult, ALU.add).then_inc(S("taps"), 1)
                    dve.wait_ge(S("taps"), 2 * i + back)
                if part == 1:
                    dve.wait_ge(S("sg_done"), p + 1)
                    nc.vector.tensor_tensor(ffn["hid"][:, p, :], ffn["sg"][:, p % 2, :], cv, ALU.mult)\
                      .then_inc(S("hid_done"), 1)
                if i % 4 == 0 and i >= 4:
                    ada_rows(i // 4 - 1)
            for k in range(FT):
                dve.wait_ge(S("hid_high"), k + 1)
                nc.vector.tensor_tensor(hid_low[:, k, :], ffn["hid"][:, k, :], hidden_high(k).bitcast(f32),
                                        ALU.subtract).then_inc(S("hid_low"), 1)
            for m in (FT // 2 - 1, FT // 2):
                ada_rows(m)
            for half in range(2):
                dve.wait_ge(S("product"), PRODUCTS["down"] + 6 * half + 6)
                for t in range(4 * half, 4 * half + 4):
                    nc.vector.tensor_tensor(h[:, t, :], h[:, t, :], banks[t % 7][:, :], ALU.add)\
                      .then_inc(S("h_done"), 1)
                if half == 0:
                    dve.wait_ge(S("ada_columns"), 2 * N_ADA)
                    nc.vector.tensor_tensor(mod[:, :], banks[NORM][:, 0:N_ADA * KD], col("b_ada", 0, N_ADA * KD),
                                            ALU.add).then_inc(S("mod_done"), 1)
            apply_norm("n3", lambda k: col("ln_ple", k), "out")
            low_parts(ple_x_high, 3 * KD)

            for t in range(KD):
                dve.wait_ge(S("gt_done"), t + 1)
                dve.wait_ge(S("product"), PRODUCTS["ple"] + 2 * t + 2)
                nc.vector.tensor_tensor(ple["tmp"][:, t % 2, :], ple["gt"][:, t % 2, :], banks[2 * (t % 3) + 1][:, :],
                                        ALU.mult).then_inc(S("ple_mul"), 1)
                dve.wait_ge(S("ple_mul"), t + 1)
                nc.vector.tensor_tensor(h[:, t, :], h[:, t, :], ple["tmp"][:, t % 2, :], ALU.add)\
                  .then_inc(S("h_done"), 1)

            def modulated(name, gain, first):
                dve.wait_ge(S("mod_done"), 1)
                nc.vector.scalar_tensor_tensor(GAIN1, mod[:, first:first + KD], 1.0, gain, ALU.add, ALU.mult)\
                  .then_inc(S("norm_gain"), 1)
                dve.wait_ge(S("norm_gain"), NORMS[name] - NORMS["n4"] + 1)
                apply_norm(name, lambda k: GAIN1[:, k:k + 1], "mul")

            modulated("n4", col("norm_mix", 0, KD), KD)

            dve.wait_ge(S("dt_ln"), 1)
            dve.wait_ge(S("expA"), 1)
            dt, sums = dtk["dtp"][0:SH, :], pool["acs"][0:SH, :]
            step(nc.vector.scalar_tensor_tensor(dt, pool["raw"][0:SH, :], 0.0, pool["ab"][0:SH, :], ALU.max, ALU.add))
            step(nc.vector.tensor_scalar(pool["a"][0:SH, :], dt, EXP_A, -1.0, ALU.mult, ALU.mult))
            for c in range(TT):
                now = slice(c * P, (c + 1) * P)
                counted_step(nc.vector.tensor_tensor_scan(sums[:, now], ones[0:SH, :], pool["a"][0:SH, now], 0.0,
                                                          ALU.mult, ALU.add))
            steps_done()
            for c in range(TT):
                now = slice(c * P, (c + 1) * P)
                nc.vector.tensor_scalar(pool["a"][0:SH, now], sums[:, now], sums[:, (c + 1) * P - 1:(c + 1) * P],
                                        None, ALU.subtract).then_inc(S("dec_arg"), 1)
            nc.vector.tensor_copy(dtk["dtp"][SH:2 * SH, :], sums).then_inc(S("dtp_sums"), 1)

            dve.wait_ge(S("pads"), 2)
            for i in range(KD):
                gi = i // 2
                w = WINDOWS[gi]
                x = pool["x"][:, i % 2, :]
                dve.wait_ge(S("x_copied"), i + 2)
                cur, back, a = x, 1, 0
                while back < w:
                    nxt = pool["s"][:, 2 * (i % 2) + a, :]
                    step(nc.vector.tensor_tensor(nxt[:, PAD:PAD + T], cur[:, PAD:PAD + T],
                                                 cur[:, PAD - back:PAD + T - back], ALU.add))
                    cur, back, a = nxt, 2 * back, 1 - a
                counted_step(nc.vector.tensor_tensor(pool["head"][:, i % 2, :], cur[:, PAD:2 * PAD],
                                                     const("inv_count")[:, PAD * gi:PAD * gi + PAD], ALU.mult))
                counted_step(nc.vector.scalar_tensor_tensor(mix["pooled"][:, i, PAD:T], cur[:, 2 * PAD:PAD + T],
                                                            1.0 / w, x[:, 2 * PAD:PAD + T], ALU.mult, ALU.subtract))
                steps_done()
                nc.vector.tensor_tensor(mix["pooled"][:, i, 0:PAD], pool["head"][:, i % 2, :], x[:, PAD:2 * PAD],
                                        ALU.subtract).then_inc(S("pooled"), 1)

            taps = 0
            waiting = []

            def xbc_silu():
                q, buf = waiting.pop(0)
                dve.wait_ge(S("th_done"), q + 1)
                nc.vector.scalar_tensor_tensor(buf, ssd["th"][:, q % 2, :], 1.0, buf, ALU.add, ALU.mult)\
                  .then_inc(S("xbc_done"), 1)

            def read_tile(i):
                nonlocal taps
                g, j = divmod(i, 6)
                s = g % 2
                if j < 2:
                    zs = ssd["zs"][:, 2 * s + j, :]
                    dve.wait_ge(S("z_tanh"), 2 * g + j + 1)
                    nc.vector.scalar_tensor_tensor(zs, zs, 1.0, banks[i % 2][:, :], ALU.add, ALU.mult)\
                      .then_inc(S("z_read"), 1)
                    return
                ch = {2: 2 * g, 3: 2 * g + 1, 4: 16 + g, 5: 24 + g}[j]
                buf = {2: ssd["xs"][:, 2 * s, :], 3: ssd["xs"][:, 2 * s + 1, :], 4: ssd["B"][:, s, :],
                       5: ssd["C"][:, s, :]}[j]
                dve.wait_ge(S("s_tap3"), 4 * g + j - 1)
                for back in (1, 2, 3):
                    nc.vector.scalar_tensor_tensor(buf[:, back:T], banks[i % 2][:, 0:T - back],
                                                   col("conv_w2", (3 - back) * 32 + ch), buf[:, back:T], ALU.mult,
                                                   ALU.add).then_inc(S("s_taps"), 1)
                    taps += 1
                    dve.wait_ge(S("s_taps"), taps)
                if waiting:
                    xbc_silu()
                waiting.append((4 * g + j - 2, buf))

            def heads(ap, width):
                return ap.rearrange("p (h n) -> p h n", n=width)

            dve.wait_ge(S("tok_done"), 1)
            for i in range(6):
                read_tile(i)
            xbc_silu()
            for g in range(SG):
                s = g % 2
                for c in range(TT):
                    n = TT * g + c
                    b = n % 2
                    now = slice(c * P, (c + 1) * P)
                    per_head = lambda first: dtk["tok"][:, c, first + HPG * g:first + HPG * g + HPG]\
                        .unsqueeze(2).to_broadcast([P, HPG, HD])
                    dve.wait_ge(S("xtok_done"), n + 1)
                    if n >= 2:
                        dve.wait_ge(S("y_ready"), n - 1)
                    nc.vector.tensor_tensor(heads(ssd["xdt"][:, b, :], HD), heads(ssd["xtok"][:, b, 0:2 * P], HD),
                                            per_head(0), ALU.mult).then_inc(S("xdt_done"), 1)
                    dve.wait_ge(S("xdt_done"), n + 1)
                    if n >= 2:
                        dve.wait_ge(S("st_ready"), 3 * ((n - 2) // TT) + min((n - 2) % TT + 1, TT - 1))
                    nc.vector.tensor_tensor(heads(ssd["xdec"][:, b, :], HD), heads(ssd["xdt"][:, b, :], HD),
                                            per_head(2 * SH), ALU.mult).then_inc(S("xdec_done"), 1)
                    dve.wait_ge(S("CB_ready"), n + 1)
                    nc.vector.tensor_tensor(ssd["CB"][:, b, :], banks[3][:, 0:P], tri, ALU.mult)\
                      .then_inc(S("CB_done"), 1)
                    dve.wait_ge(S("Ex_done"), n + 1)
                    for j in range(HPG):
                        a = SH + HPG * g + j
                        nc.vector.tensor_scalar(ssd["L"][:, b, j * P:(j + 1) * P], banks[4][:, j * P:(j + 1) * P],
                                                dtk["tok"][:, c, a:a + 1], 0.0, ALU.subtract, ALU.min)\
                          .then_inc(S("L0_done"), 1)
                    nc.vector.tensor_tensor(heads(ssd["CE"][:, b, :], P), heads(ssd["Ex"][:, b, :], P),
                                            ssd["C"][:, s, now].unsqueeze(1).to_broadcast([P, HPG, P]), ALU.mult)\
                      .then_inc(S("CE_done"), 1)
                    dve.wait_ge(S("L_done"), n + 1)
                    dve.wait_ge(S("CB_done"), n + 1)
                    nc.vector.tensor_tensor(heads(ssd["L"][:, b, :], P), heads(ssd["L"][:, b, :], P),
                                            ssd["CB"][:, b, :].unsqueeze(1).to_broadcast([P, HPG, P]), ALU.mult)\
                      .then_inc(S("M_done"), 1)
                    if g + 1 < SG:
                        for i in FILL[c]:
                            read_tile(6 * (g + 1) + i)
                        if c == TT - 1:
                            xbc_silu()
                    if c < TT - 1:
                        k = 3 * g + c
                        if c > 0:
                            dve.wait_ge(S("state_done"), k)
                            nc.vector.tensor_tensor(heads(ssd["carry"], HD), heads(ssd["state"], HD),
                                                    heads(ssd["Ex"][:, b, :], P)[:, :, P - 1:P]
                                                    .to_broadcast([P, HPG, HD]), ALU.mult)\
                              .then_inc(S("carried"), 1)
                            dve.wait_ge(S("carried"), 2 * g + c)
                        dve.wait_ge(S("st_ready"), k + 1)
                        if c > 0:
                            ins = nc.vector.tensor_tensor(ssd["state"], ssd["carry"], banks[7][:, 0:HPG * HD], ALU.add)
                        else:
                            ins = nc.vector.tensor_copy(ssd["state"], banks[7][:, 0:HPG * HD])
                        ins.then_inc(S("state_done"), 1)
                dve.wait_ge(S("y_ready"), TT * (g + 1))
                for i in range(2):
                    y = mix["yn"][:, 2 * g + i, :]
                    nc.vector.scalar_tensor_tensor(y, ssd["xs"][:, 2 * s + i, :], col("D_skip", 2 * g + i),
                                                   banks[5 + i][:, :], ALU.mult, ALU.add).then_inc(S("y_read"), 1)
                dve.wait_ge(S("y_read"), 2 * g + 2)
                for i in range(2):
                    y = mix["yn"][:, 2 * g + i, :]
                    nc.vector.scalar_tensor_tensor(y, y, 0.5, ssd["zs"][:, 2 * s + i, :], ALU.mult, ALU.mult)\
                      .then_inc(S("y_gated"), 1)
            for g in range(SG):
                dve.wait_ge(S("y_root"), g + 1)
                nc.vector.reciprocal(inv[:, g % 2, :], inv[:, g % 2, :]).then_inc(S("y_inv"), 1)
                dve.wait_ge(S("y_inv"), g + 1)
                for i in range(2):
                    y = mix["yn"][:, 2 * g + i, :]
                    nc.vector.scalar_tensor_tensor(y, y, col("ssd_norm", 2 * g + i), inv[:, g % 2, :], ALU.mult,
                                                   ALU.mult).then_inc(S("yn_done"), 1)

            for t in range(KD):
                dve.wait_ge(S("product"), PRODUCTS["ssd_out"] + 2 * (t // 4) + 2)
                dve.wait_ge(S("gs_done"), t + 1)
                nc.vector.tensor_tensor(hn[:, t, :], banks[t][:, :], late["gs"][:, t, :], ALU.mult)\
                  .then_inc(S("mixed"), 1)
            for t in range(KD):
                dve.wait_ge(S("product"), PRODUCTS["pool_out"] + t + 1)
                dve.wait_ge(S("gs_done"), KD + t + 1)
                nc.vector.tensor_tensor(late["tmp"][:, t % 2, :], banks[t][:, :], late["gs"][:, KD + t, :], ALU.mult)\
                  .then_inc(S("mixed"), 1)
                dve.wait_ge(S("mixed"), KD + 2 * t + 1)
                nc.vector.tensor_tensor(hn[:, t, :], hn[:, t, :], late["tmp"][:, t % 2, :], ALU.add)\
                  .then_inc(S("mixed"), 1)
            low_parts(mixed_high, 4 * KD)
            for t in range(KD):
                dve.wait_ge(S("product"), PRODUCTS["wo2"] + t + 1)
                nc.vector.scalar_tensor_tensor(h[:, t, :], banks[t % 7][:, :], mod[:, 2 * KD + t:2 * KD + t + 1],
                                               h[:, t, :], ALU.mult, ALU.add).then_inc(S("h_done"), 1)
            modulated("n5", col("norm_ffn", 0, KD), 4 * KD)

            iota = const("iota")
            dve.wait_ge(S("sc_done"), TT)
            for tt in range(TT):
                sc, ch, mk = moe["sc"][:, tt, :], moe["ch"][:, tt, :], moe["mk"][:, tt, :]
                best, gsum, gtop = moe["best"][:, tt, :], moe["gsum"][:, tt, :], moe["gtop"][:, tt, :]
                gm, gneg, top, gf = moe["gm"][:, tt, :], moe["gneg"][:, tt, :], moe["top"][:, tt, :], moe["gf"][:, tt, :]
                ef, sel, wk, wsum = moe["ef"][:, tt, :], moe["sel"][:, tt, :], moe["wk"][:, tt, :], moe["wsum"][:, tt:tt + 1]
                gix_t, eix_t = gix[:, tt * EG:(tt + 1) * EG], eix[:, tt * TOP:(tt + 1) * TOP]
                groups = lambda ap: ap.rearrange("p (g e) -> p g e", e=E // EG)
                over = lambda ap: ap.unsqueeze(2).to_broadcast([P, EG, E // EG])
                step(nc.vector.tensor_tensor(ch, sc, col("router_bias", 0, E), ALU.add))
                for g in range(EG):
                    counted_step(nc.vector.max(best[:, 8 * g:8 * g + 8], ch[:, 8 * g:8 * g + 8]))
                steps_done()
                step(nc.vector.tensor_tensor(gsum, groups(best)[:, :, 0], groups(best)[:, :, 1], ALU.add))
                step(nc.vector.max(gtop, gsum))
                step(nc.vector.max_index(gix_t, gtop, gsum))
                step(nc.vector.tensor_copy(gf, gix_t))
                step(nc.vector.tensor_scalar(gm, iota[:, 0:EG], gf[:, 0:1], None, ALU.is_equal))
                for g in range(1, 4):
                    step(nc.vector.scalar_tensor_tensor(gm, iota[:, 0:EG], gf[:, g:g + 1], gm, ALU.is_equal, ALU.add))
                step(nc.vector.tensor_scalar(gneg, gm, -1.0, 1e30, ALU.add, ALU.mult))
                step(nc.vector.tensor_tensor(groups(mk), groups(ch), over(gm), ALU.mult))
                step(nc.vector.tensor_tensor(groups(mk), groups(mk), over(gneg), ALU.add))
                step(nc.vector.max(top, mk))
                step(nc.vector.max_index(eix_t, top, mk))
                step(nc.vector.tensor_copy(ef, eix_t))
                step(nc.vector.tensor_scalar(sel, iota[:, 0:E], ef[:, 0:1], None, ALU.is_equal))
                for k in range(1, TOP):
                    ins = nc.vector.scalar_tensor_tensor(sel, iota[:, 0:E], ef[:, k:k + 1], sel, ALU.is_equal, ALU.add)
                    if k < TOP - 1:
                        step(ins)
                ins.then_inc(S("selected"), 1)
                for k in range(TOP):
                    step(nc.vector.scalar_tensor_tensor(moe["junk"], iota[:, 0:E], ef[:, k:k + 1], sc, ALU.is_equal,
                                                        ALU.mult, accum_out=wk[:, k:k + 1]))
                step(nc.vector.tensor_reduce(wsum, wk, AX.X, ALU.add))
                step(nc.vector.reciprocal(wsum, wsum))
                step(nc.vector.tensor_scalar(wk, wk, wsum, ROUTED_SCALE, ALU.mult, ALU.mult))

            dve.wait_ge(S("counted"), 1)
            count = banks[3][:, TT * E:(TT + 1) * E]
            step(nc.vector.tensor_scalar(moe["nb"], count, 0.0, None, ALU.is_gt))
            for j in range(1, T // P):
                step(nc.vector.scalar_tensor_tensor(moe["nb"], count, float(P * j), moe["nb"], ALU.is_gt, ALU.add))
            step(nc.vector.tensor_tensor_scan(moe["bend"], ones[:, 0:E], moe["nb"], 0.0, ALU.mult, ALU.add))
            step(nc.vector.tensor_tensor(moe["bstart"], moe["bend"], moe["nb"], ALU.subtract))
            for tt in range(TT):
                step(nc.vector.scalar_tensor_tensor(moe["start"][:, tt, :], moe["bstart"], float(P),
                                                    banks[3][:, tt * E:(tt + 1) * E], ALU.mult, ALU.add))
            nc.vector.tensor_scalar(moe["junk"], moe["bend"], const("row"), None, ALU.is_le, ALU.add,
                                    accum_out=moe["ebcol"][:, 0:1]).then_inc(S("ebcol_done"), 1)
            dve.wait_ge(S("ebcol_done"), 1)
            for tt in range(TT):
                for k in range(TOP):
                    n = tt * TOP + k
                    step(nc.vector.scalar_tensor_tensor(moe["junk"], iota[:, 0:E], moe["ef"][:, tt, k:k + 1],
                                                        moe["start"][:, tt, :], ALU.is_equal, ALU.mult,
                                                        accum_out=moe["place"][:, n:n + 1]))
            step(nc.vector.tensor_copy(place_i[:, :], moe["place"]))
            step(nc.vector.tensor_scalar(slot_i[:, :], place_i[:, :], P - 1, None, ALU.bitwise_and))
            step(nc.vector.tensor_scalar(block_i[:, :], place_i[:, :], 7, None, ALU.arith_shift_right))
            step(nc.vector.tensor_copy(moe["blk"], block_i[:, :]))
            nc.vector.tensor_copy(moe["spot"], slot_i[:, :]).then_inc(S("spots"), 1)
            for n in range(TT * TOP):
                tt, k = divmod(n, TOP)
                if n >= 4:
                    dve.wait_ge(S("table_part"), n - 3)
                block_n = moe["blk"][:, n:n + 1]
                for j, factor in enumerate((const("tokens")[:, tt:tt + 1], None, moe["wk"][:, tt, k:k + 1])):
                    nc.vector.tensor_scalar(moe["OHb"][:, n % 4, j * MAX_BLOCKS:(j + 1) * MAX_BLOCKS],
                                            iota[:, 0:MAX_BLOCKS], block_n, factor, ALU.is_equal,
                                            *(() if factor is None else (ALU.mult,))).then_inc(S("OHb_done"), 1)
            dve.wait_ge(S("eb_ready"), 1)
            row = moe["ebrow"][0:1, 0:MAX_BLOCKS]
            step(nc.vector.tensor_scalar(row, banks[3][0:1, 384:384 + MAX_BLOCKS], float(E - 1), None, ALU.min))
            step(nc.vector.tensor_copy(expert_of[0:1, 0:MAX_BLOCKS], row))
            step(nc.vector.tensor_scalar(moe["ebrow"][0:1, MAX_BLOCKS:MAX_BLOCKS + 1], moe["bend"][0:1, E - 1:E], -1.0,
                                         None, ALU.add))
            step(nc.vector.tensor_copy(place_i[0:1, 0:1], moe["ebrow"][0:1, MAX_BLOCKS:MAX_BLOCKS + 1]))
            counted_step(nc.vector.tensor_scalar(expert_of[0:1, MAX_BLOCKS:MAX_BLOCKS + 1], place_i[0:1, 0:1], 1, None,
                                                 ALU.arith_shift_right))
            dve.wait_ge(S("table_part"), TT * TOP)
            tab = banks[2]
            nc.vector.tensor_copy(moe["ws"], tab[:, 2 * MAX_BLOCKS:3 * MAX_BLOCKS]).then_inc(S("blocks_known"), 1)
            step(nc.vector.tensor_scalar(moe["free"], tab[:, MAX_BLOCKS:2 * MAX_BLOCKS], -1.0, 1.0, ALU.mult, ALU.add))
            nc.vector.scalar_tensor_tensor(moe["idx"], moe["free"], const("pad_row"), tab[:, 0:MAX_BLOCKS], ALU.mult,
                                           ALU.add).then_inc(S("blocks_known"), 1)

            def block_hidden(b, p):
                dve.wait_ge(S("moe_sg"), b + 1)
                nc.vector.tensor_tensor(moe["hid"][:, p, :], moe["sg"][:, p, :], banks[2 + p][:, FE:2 * FE], ALU.mult)\
                  .then_inc(S("moe_hid"), 1)

            def block_hidden_T(b, p):
                dve.wait_ge(S("moe_ht"), b + 1)
                nc.vector.tensor_copy(moe["hidT"][:, p, :], banks[4][:, 0:2 * P]).then_inc(S("hT_done"), 1)

            def block_out(b, p, added):
                dve.wait_ge(S("w_known"), b + 1)
                dve.wait_ge(S(f"y_added{p}"), added * 16)
                for half in range(2):
                    dve.wait_ge(S("moe_y"), b * 2 + (half + 1))
                    nc.vector.tensor_scalar(moe["y"][:, p, 512 * half:512 * half + 512], banks[5 + half][:, :],
                                            moe["wcol"][:, p:p + 1], None, ALU.mult).then_inc(S("y_copied"), 1)

            steps_done()
            dve.wait_ge(S("blocks_known"), 2)
            pairs_but_one = dve.value_load(expert_of[0:1, MAX_BLOCKS:MAX_BLOCKS + 1], min_val=TT * TOP // 2 - 1,
                                            max_val=MAX_BLOCKS // 2 - 1)
            pairs = pairs_but_one + 1
            block_hidden(0, 0)
            with dve.Fori(1, pairs) as i:
                for b, p in ((i * 2 + (-1), 1), (i * 2, 0)):
                    block_hidden_T(b + (-1), 1 - p)
                    block_hidden(b, p)
                    block_out(b + (-1), 1 - p, i)
            block_hidden_T(pairs_but_one * 2, 0)
            block_hidden(pairs_but_one * 2 + 1, 1)
            block_out(pairs_but_one * 2, 0, pairs)
            block_hidden_T(pairs_but_one * 2 + 1, 1)
            block_out(pairs_but_one * 2 + 1, 1, pairs)
            for k in range(KD):
                dve.wait_ge(S("acc_T"), k + 1)
                nc.vector.scalar_tensor_tensor(h[:, k, :], banks[k % 7][:, :], mod[:, 5 * KD + k:5 * KD + k + 1],
                                               h[:, k, :], ALU.mult, ALU.add).then_inc(S("h_done"), 1)
            apply_norm("n6", lambda k: col("final_norm", k), "out")


def shape_constants(np):
    p = np.arange(P)[:, None]
    j = np.arange(P)[None, :]
    key = np.arange(T)[None, :] - (T - P)
    parts = {
        "ident": (p == j) * 1.0,
        "ones_d": np.full((P, P), 1.0 / D),
        "ones_g": np.full((P, P), 1.0 / 256),
        "ones_h": (p // HD == j // HD) / float(HD),
        "tri": (p <= j) * 1.0,
        "ones": np.ones((P, P)),
        "dist": np.where(key // HD <= p // HD, -np.abs(p - key) * 1.0, MASKED),
        "causal": np.where(key <= p, 0.0, MASKED),
        "chunked": np.where(key // HD <= p // HD, 0.0, MASKED),
        "inv_count": np.concatenate([np.tile(1.0 / np.minimum(np.arange(1, PAD + 1), w), (P, 1))
                                     for w in WINDOWS], axis=1),
        "eps": np.full((P, 1), EPS),
        "before": (p < j) * 1.0,
        "iota": np.tile(j * 1.0, (P, 1)),
        "row": p * 1.0,
        "pad_row": p * 1.0 + PAD_ROW,
        "tokens": p + P * np.arange(TT)[None, :] * 1.0,
    }
    return np.concatenate([parts[name] for name, _ in SHAPE_SIZES], axis=1).astype(np.float32)


def kernel(**inputs):
    import numpy as np
    import concourse.bacc as bacc
    from concourse.bass_utils import run_bass_kernel_spmd

    x = {name: np.asarray(a) for name, a in inputs.items()}

    def tiles(v):
        v = v.reshape(-1, P)
        return np.ascontiguousarray(v.T)

    def padded(v):
        out = np.zeros((P, v.shape[1]), v.dtype)
        out[:v.shape[0]] = v
        return out

    def everywhere(v):
        return np.repeat(v.reshape(1, -1), P, axis=0)

    gain = x["qk_gain"][0]
    columns = {
        "ln_mix": tiles(x["ln_mix"]), "ln_ffn": tiles(x["ln_ffn"]), "ln_ple": tiles(x["ln_ple"]),
        "conv_w": tiles(x["conv_w"]), "conv_b": tiles(x["conv_b"]),
        "qk_gain": np.concatenate([gain, gain], axis=1).T,
        "subln": np.concatenate([x["subln_gain"][0]] * 2).reshape(P, 1),
        "fgate": padded(x["fgate_bias"].T), "lam": everywhere(x["lam_params"]),
        "c": tiles(x["c_2"]), "b_ada": tiles(x["b_ada_2"]), "norm_mix": tiles(x["norm_mix_g_2"]),
        "conv_w2": tiles(x["conv_w_2"]), "conv_b2": tiles(x["conv_b_2"]),
        "dt_bias": padded(x["dt_bias_2"].T), "A_log": padded(x["A_log_2"].T),
        "D_skip": tiles(np.repeat(x["D_skip_2"][0], HD)), "ssd_norm": tiles(x["ssd_norm_g_2"]),
        "pool_scale": tiles(x["pool_scale_2"]), "norm_ffn": tiles(x["norm_ffn_g_2"]),
        "router_bias": everywhere(x["router_bias_2"]), "final_norm": tiles(x["final_norm_g_2"]),
    }
    distance = np.clip(np.arange(P)[:, None] - (np.arange(T)[None, :] - (T - P)), -P, P) + P
    arrays = {
        "cols": np.concatenate([columns[name] for name, _ in COLUMN_SIZES], axis=1),
        "shape_consts": shape_constants(np),
        "x_T": np.ascontiguousarray(x["x"][0].T),
        "p_T": np.ascontiguousarray(x["p"][0, 0].T),
        "rel_rows": np.ascontiguousarray(x["rel_bias"][0][:, distance]),
        "w_in": x["w_in"][0], "w_out": x["w_out"][0], "w_up": x["w_up"][0], "w_down": x["w_down"][0],
        "w_ple_gate": x["w_ple_gate"][0], "w_ple_proj": x["w_ple_proj"][0], "w_ada": x["w_ada_2"][0],
        "w_in_2": x["w_in_2"][0], "pool_w": x["pool_w_2"][0].reshape(D, 256), "w_br_ssd": x["w_br_ssd_2"][0],
        "w_br_pool": x["w_br_pool_2"][0], "w_out_2": x["w_out_2"][0], "w_router": x["w_router_2"][0],
        "we_gate": x["we_gate_2"][0], "we_up": x["we_up_2"][0], "we_down": x["we_down_2"][0],
        "ws_gate": x["ws_gate_2"][0], "ws_up": x["ws_up_2"][0], "ws_down": x["ws_down_2"][0],
    }
    nc = bacc.Bacc("TRN2", target_bir_lowering=False, num_devices=1)
    feed, A = {}, {}
    for name, a in arrays.items():
        feed[f"in_{name}"] = np.ascontiguousarray(a)
        A[name] = nc.dram_tensor(f"in_{name}", a.shape, mybir.dt.from_np(a.dtype), kind="ExternalInput").ap()
    out_T = nc.dram_tensor("out_T", (D, T), mybir.dt.float32, kind="ExternalOutput").ap()
    u_rows = nc.dram_tensor("u_rows", (T + P, D), mybir.dt.float32, kind="Internal").ap()
    y_rows = nc.dram_tensor("y_rows", (T + P, D), mybir.dt.float32, kind="Internal").ap()
    two_blocks(nc, A, out_T, u_rows, y_rows)
    result = run_bass_kernel_spmd(nc, [feed], core_ids=[0])
    return np.ascontiguousarray(result.results[0]["out_T"].T).reshape(1, T, D)
```
